# Optimizing a Trainium2 kernel written in Bass

```python
import jax, jax.numpy as jnp
from jax import lax
import numpy as np

D_MODEL = 1024
BATCH = 1
SEQ = 512
DEPTH = 2

MLA_HEADS = 4
MLA_Q_RANK = 256
MLA_KV_RANK = 128
MLA_NOPE = 64
MLA_ROPE = 32
MLA_V = 64
MLA_Q_BLOCK = 128
SC_WIDTH = 256
SC_KERNEL = 3
CF_WIDTH = 256
CF_KERNEL = 31
GQ_HEADS = 4
GQ_KV_HEADS = 2
GQ_HEAD_DIM = 64
WINDOW = 128
BLOCK = 128
ROPE_THETA = 10000.0
N_EXPERTS = 16
EXPERT_FF = 1024
EC_CAPACITY_FACTOR = 2
LN_EPS = 1e-5
RMS_EPS = 1e-6
DEEPNORM_ALPHA = (2 * DEPTH) ** 0.25
DEEPNORM_BETA = (8 * DEPTH) ** -0.25
NEG_INF = -1e30

IN_SPLITS = (MLA_Q_RANK, MLA_KV_RANK, MLA_ROPE,
             SC_WIDTH, SC_WIDTH, SC_WIDTH,
             CF_WIDTH, CF_WIDTH,
             GQ_HEADS * GQ_HEAD_DIM, GQ_KV_HEADS * GQ_HEAD_DIM, GQ_KV_HEADS * GQ_HEAD_DIM)
D_IN = sum(IN_SPLITS)
D_MIX = MLA_HEADS * MLA_V + SC_WIDTH + CF_WIDTH + GQ_HEADS * GQ_HEAD_DIM

kernel_name = "hybrid_parallel_mla_conv_swa_ecmoe_encoder"

def layer_norm(x, g, b):
    xf = x.astype(jnp.float32)
    mu = jnp.mean(xf, axis=-1, keepdims=True)
    var = jnp.mean(jnp.square(xf - mu), axis=-1, keepdims=True)
    y = (xf - mu) * lax.rsqrt(var + LN_EPS) * g.astype(jnp.float32) + b.astype(jnp.float32)
    return y.astype(x.dtype)

def rms_norm(x, g):
    xf = x.astype(jnp.float32)
    y = xf * lax.rsqrt(jnp.mean(jnp.square(xf), axis=-1, keepdims=True) + RMS_EPS) * g.astype(jnp.float32)
    return y.astype(x.dtype)

def rope_cos_sin(positions, dim):
    inv = 1.0 / (ROPE_THETA ** (jnp.arange(0, dim, 2, dtype=jnp.float32) / dim))
    ang = positions.astype(jnp.float32)[..., None] * inv
    return jnp.cos(ang), jnp.sin(ang)

def apply_rope(x, cos, sin):
    xf = x.astype(jnp.float32)
    x1, x2 = jnp.split(xf, 2, axis=-1)
    c = cos[:, :, None, :]
    s = sin[:, :, None, :]
    return jnp.concatenate([x1 * c - x2 * s, x2 * c + x1 * s], axis=-1).astype(x.dtype)

def depthwise_conv(x, w):
    k = w.shape[0]
    c = x.shape[-1]
    return lax.conv_general_dilated(
        x, w[:, None, :].astype(x.dtype), window_strides=(1,),
        padding=[(k // 2, k // 2)], dimension_numbers=('NWC', 'WIO', 'NWC'),
        feature_group_count=c)

def mla_attention(q_lat, kv_lat, k_rope, q_norm_g, w_uq, kv_norm_g, w_ukv, cos, sin):
    b, s, _ = q_lat.shape
    h = MLA_HEADS
    dqk = MLA_NOPE + MLA_ROPE
    q = (rms_norm(q_lat, q_norm_g) @ w_uq).reshape(b, s, h, dqk)
    q = jnp.concatenate([q[..., :MLA_NOPE], apply_rope(q[..., MLA_NOPE:], cos, sin)], axis=-1)
    kv = (rms_norm(kv_lat, kv_norm_g) @ w_ukv).reshape(b, s, h, MLA_NOPE + MLA_V)
    k_nope, v = kv[..., :MLA_NOPE], kv[..., MLA_NOPE:]
    k_pe = apply_rope(k_rope[:, :, None, :], cos, sin)
    k = jnp.concatenate([k_nope, jnp.broadcast_to(k_pe, (b, s, h, MLA_ROPE))], axis=-1)
    scale = dqk ** -0.5
    nb = s // MLA_Q_BLOCK
    q_blocks = q.reshape(b, nb, MLA_Q_BLOCK, h, dqk).transpose(1, 0, 2, 3, 4)

    def attend(qb):
        sc = jnp.einsum('bqhd,bkhd->bhqk', qb, k).astype(jnp.float32) * scale
        p = jax.nn.softmax(sc, axis=-1).astype(v.dtype)
        return jnp.einsum('bhqk,bkhd->bqhd', p, v)

    o = lax.map(attend, q_blocks)
    return o.transpose(1, 0, 2, 3, 4).reshape(b, s, h * MLA_V)

def window_gqa(q, k, v, sink, cos, sin):
    b, s, _ = q.shape
    h, kvh, d = GQ_HEADS, GQ_KV_HEADS, GQ_HEAD_DIM
    g = h // kvh
    nb = s // BLOCK
    q = apply_rope(q.reshape(b, s, h, d), cos, sin).reshape(b, nb, BLOCK, kvh, g, d)
    k = apply_rope(k.reshape(b, s, kvh, d), cos, sin)
    v = v.reshape(b, s, kvh, d)
    pad = ((0, 0), (BLOCK, BLOCK), (0, 0), (0, 0))
    kp = jnp.pad(k, pad).reshape(b, nb + 2, BLOCK, kvh, d)
    vp = jnp.pad(v, pad).reshape(b, nb + 2, BLOCK, kvh, d)
    kb = jnp.concatenate([kp[:, :-2], kp[:, 1:-1], kp[:, 2:]], axis=2)
    vb = jnp.concatenate([vp[:, :-2], vp[:, 1:-1], vp[:, 2:]], axis=2)
    sc = jnp.einsum('bnqkgd,bnjkd->bnkgqj', q, kb).astype(jnp.float32) * (d ** -0.5)
    blk = jnp.arange(nb)[:, None]
    q_pos = blk * BLOCK + jnp.arange(BLOCK)[None, :]
    k_pos = (blk - 1) * BLOCK + jnp.arange(3 * BLOCK)[None, :]
    valid = ((jnp.abs(q_pos[:, :, None] - k_pos[:, None, :]) <= WINDOW)
             & (k_pos[:, None, :] >= 0) & (k_pos[:, None, :] < s))
    sc = jnp.where(valid[None, :, None, None], sc, NEG_INF)
    sink_l = jnp.broadcast_to(sink.astype(jnp.float32).reshape(kvh, g, 1, 1), sc.shape[:-1] + (1,))
    p = jax.nn.softmax(jnp.concatenate([sc, sink_l], axis=-1), axis=-1)[..., :-1].astype(v.dtype)
    o = jnp.einsum('bnkgqj,bnjkd->bnqkgd', p, vb)
    return o.reshape(b, s, h * d)

def conformer_conv(a, gate, w_dw, b_dw, g_n, b_n):
    u = a * jax.nn.sigmoid(gate)
    u = depthwise_conv(u, w_dw) + b_dw.astype(u.dtype)
    return jax.nn.silu(layer_norm(u, g_n, b_n))

def expert_choice_moe(x, w_router, b_router, w_gate, w_up, w_down):
    b, s, d = x.shape
    cap = EC_CAPACITY_FACTOR * s // N_EXPERTS
    logits = (x @ w_router).astype(jnp.float32) + b_router.astype(jnp.float32)
    aff = jax.nn.softmax(logits, axis=-1)
    gates, idx = lax.top_k(aff.transpose(0, 2, 1), cap)
    xs = jax.vmap(lambda xb, ib: xb[ib])(x, idx)
    hid = jax.nn.silu(jnp.einsum('becd,edf->becf', xs, w_gate)) * jnp.einsum('becd,edf->becf', xs, w_up)
    o = jnp.einsum('becf,efd->becd', hid, w_down) * gates[..., None].astype(x.dtype)
    y = jax.vmap(lambda ib, ob: jnp.zeros((s, d), ob.dtype).at[ib.reshape(-1)].add(ob.reshape(-1, d)))(idx, o)
    return y

def _normal(k, shape, scale):
    return jax.random.normal(k, shape, jnp.float32) * scale

def setup_inputs(seed: int = 0) -> dict:
    key = jax.random.key(seed)
    ks = jax.random.split(key, 24)
    L = DEPTH
    x = jax.random.normal(ks[0], (BATCH, SEQ, D_MODEL), jnp.float32)
    offset = jax.random.randint(ks[1], (BATCH, 1), 0, 1024, dtype=jnp.int32)
    positions = (offset + jnp.arange(SEQ, dtype=jnp.int32)[None, :]).astype(jnp.int32)
    return {
        "x": x,
        "positions": positions,
        "w_in": _normal(ks[2], (L, D_MODEL, D_IN), D_MODEL ** -0.5),
        "q_norm_g": 1.0 + _normal(ks[3], (L, MLA_Q_RANK), 0.02),
        "w_uq": _normal(ks[4], (L, MLA_Q_RANK, MLA_HEADS * (MLA_NOPE + MLA_ROPE)), MLA_Q_RANK ** -0.5),
        "kv_norm_g": 1.0 + _normal(ks[5], (L, MLA_KV_RANK), 0.02),
        "w_ukv": _normal(ks[6], (L, MLA_KV_RANK, MLA_HEADS * (MLA_NOPE + MLA_V)), MLA_KV_RANK ** -0.5),
        "sconv_w": _normal(ks[7], (L, SC_KERNEL, SC_WIDTH), SC_KERNEL ** -0.5),
        "cconv_w": _normal(ks[8], (L, CF_KERNEL, CF_WIDTH), CF_KERNEL ** -0.5),
        "cconv_b": _normal(ks[9], (L, CF_WIDTH), 0.02),
        "cnorm_g": 1.0 + _normal(ks[10], (L, CF_WIDTH), 0.02),
        "cnorm_b": _normal(ks[11], (L, CF_WIDTH), 0.02),
        "sink": _normal(ks[12], (L, GQ_HEADS), 0.5),
        "w_out": _normal(ks[13], (L, D_MIX, D_MODEL), DEEPNORM_BETA * D_MIX ** -0.5),
        "ln1_g": 1.0 + _normal(ks[14], (L, D_MODEL), 0.02),
        "ln1_b": _normal(ks[15], (L, D_MODEL), 0.02),
        "w_router": _normal(ks[16], (L, D_MODEL, N_EXPERTS), D_MODEL ** -0.5),
        "b_router": _normal(ks[17], (L, N_EXPERTS), 0.01),
        "w_gate": _normal(ks[18], (L, N_EXPERTS, D_MODEL, EXPERT_FF), D_MODEL ** -0.5),
        "w_up": _normal(ks[19], (L, N_EXPERTS, D_MODEL, EXPERT_FF), D_MODEL ** -0.5),
        "w_down": _normal(ks[20], (L, N_EXPERTS, EXPERT_FF, D_MODEL), DEEPNORM_BETA * EXPERT_FF ** -0.5),
        "ln2_g": 1.0 + _normal(ks[21], (L, D_MODEL), 0.02),
        "ln2_b": _normal(ks[22], (L, D_MODEL), 0.02),
    }

def reference(x, positions, w_in, q_norm_g, w_uq, kv_norm_g, w_ukv, sconv_w, cconv_w, cconv_b,
              cnorm_g, cnorm_b, sink, w_out, ln1_g, ln1_b, w_router, b_router, w_gate, w_up,
              w_down, ln2_g, ln2_b):
    cos_a, sin_a = rope_cos_sin(positions, MLA_ROPE)
    cos_d, sin_d = rope_cos_sin(positions, GQ_HEAD_DIM)
    split_points = np.cumsum(IN_SPLITS)[:-1].tolist()
    for l in range(DEPTH):
        proj = x @ w_in[l]
        (q_lat, kv_lat, k_rope, sc_b, sc_c, sc_h, cf_a, cf_g,
         gq_q, gq_k, gq_v) = jnp.split(proj, split_points, axis=-1)
        y_a = mla_attention(q_lat, kv_lat, k_rope, q_norm_g[l], w_uq[l], kv_norm_g[l], w_ukv[l], cos_a, sin_a)
        y_b = sc_b * depthwise_conv(sc_c * sc_h, sconv_w[l])
        y_c = conformer_conv(cf_a, cf_g, cconv_w[l], cconv_b[l], cnorm_g[l], cnorm_b[l])
        y_d = window_gqa(gq_q, gq_k, gq_v, sink[l], cos_d, sin_d)
        mix = jnp.concatenate([y_a, y_b, y_c, y_d], axis=-1) @ w_out[l]
        x = layer_norm(DEEPNORM_ALPHA * x + mix, ln1_g[l], ln1_b[l])
        moe = expert_choice_moe(x, w_router[l], b_router[l], w_gate[l], w_up[l], w_down[l])
        x = layer_norm(DEEPNORM_ALPHA * x + moe, ln2_g[l], ln2_b[l])
    return x


_drawn_inputs = setup_inputs


def setup_inputs(seed=0):
    import zlib

    import numpy as np

    out = dict(_drawn_inputs(seed))
    spreads = {}
    factors = {'q_norm_g': 8.0,
     'kv_norm_g': 8.0,
     'cconv_b': 8.0,
     'cnorm_g': 8.0,
     'cnorm_b': 8.0,
     'sink': 29.314,
     'b_router': 8.0}
    for name, (base, spread) in spreads.items():
        noise = np.random.default_rng([zlib.crc32(name.encode()), seed]).standard_normal(out[name].shape)
        drawn = base * np.exp(spread * noise) if base else spread * noise
        out[name] = __import__('jax').numpy.asarray(drawn.astype(out[name].dtype))
    for name, factor in factors.items():
        out[name] = (out[name] * factor).astype(out[name].dtype)
    return out
```

```python
from contextlib import ExitStack

import concourse.bass as bass
import numpy as np
from concourse import mybir

F32 = mybir.dt.float32
I32 = mybir.dt.int32
I16 = mybir.dt.int16
U32 = mybir.dt.uint32
ALU = mybir.AluOpType
ACT = mybir.ActivationFunctionType
AX_X = mybir.AxisListType.X

P = 128
DEPTH, D, S = 2, 1024, 512
KD = D // P
NT = S // P
MLA_H, NOPE, ROPE, VD = 4, 64, 32, 64
QK = NOPE + ROPE
Q_RANK, KV_RANK = 256, 128
GQ_H, GQ_D = 4, 64
SC_K, CF_K, CF_W = 3, 31, 256
N_EXP, FF, CAP = 16, 1024, 64
PAIRS = N_EXP // 2
LN_EPS, RMS_EPS = 1e-5, 1e-6
ALPHA = (2 * DEPTH) ** 0.25
MLA_SCALE = float(QK) ** -0.5
GQ_SCALE = float(GQ_D) ** -0.5

CF_G, CF_A, SC_C, SC_H, SC_B, KV, GQK, QLAT, GQQ, GQV, KROPE = 0, 2, 4, 6, 8, 10, 11, 12, 14, 16, 17
N_IN = 18
IN_SLOTS = N_IN // 2

RING = 16
SLOT = 2 * FF
WOUT_AT = IN_SLOTS
LN1_AT = WOUT_AT + D // P // 2
MOE_AT = LN1_AT + 2
PAIR_CHUNKS = 3 * KD
LN2_AT = MOE_AT + PAIRS * PAIR_CHUNKS
CHUNKS = LN2_AT + 1
REVS = CHUNKS // RING
BODY_PAIRS = 2
assert CHUNKS % RING == 0 and BODY_PAIRS * PAIR_CHUNKS % RING == 0

PAR = {}
_at = 0
for _name, _n in (("sconv", 2 * SC_K), ("cconv", 2 * CF_K), ("cconv_b", 2), ("cnorm_g", 2), ("cnorm_b", 2),
                  ("q_g", 2), ("kv_g", 1), ("sink", GQ_H), ("b_router", N_EXP)):
    PAR[_name] = _at
    _at += _n
N_PAR = _at

IDENT, ONES, ROT_A, ROT_D, BAND, FREQ = 0, P, 2 * P, 3 * P, 4 * P, 4 * P + 3 * P
N_CONST = FREQ + 1
TWO_PI_1 = 6.28125
TWO_PI_2 = float(np.float32(np.floor((2 * np.pi - TWO_PI_1) * 2**20) / 2**20))
TWO_PI_3 = float(np.float32(2 * np.pi - TWO_PI_1 - TWO_PI_2))
ROUND = 1.5 * 2.0**23
PI_BELOW = 3.1415925


def bank_uses():
    order = []
    for t in range(NT):
        for half in range(2):
            order.append((("xT", t, half), 4 + (2 * t + half) % 4))
    for i in range(N_IN):
        order.append((("in", i), i % 4))
        if i == QLAT + 1:
            order += [(("ssq", 0), 4), (("mean",), 6), (("rotD", 0), 7)]
        if i == GQQ + 1:
            order += [(("ssq", 1), 5)]
        if i == GQV:
            order += [(("rotD", 1), 4), (("rotD", 2), 6)]
    order.append((("var",), 7))
    order += [(("qup", h), 4 + h) for h in range(MLA_H)]
    order += [(("kup", 0), 4), (("kup", 1), 5), (("vup", 0), 6), (("vup", 1), 7)]
    order += [(("rotQ", h), 4 + h) for h in range(MLA_H)] + [(("rotK",), 2)]
    order += [(("YD", 0), 5), (("YD", 1), 6)]
    for i in range(NT * GQ_H):
        order += [(("SD", i), i % 2), (("TD", i), 2 + i % 2)]
    order += [(("YA", 0), 4), (("YA", 1), 7)]
    for i in range(NT * MLA_H):
        order += [(("SA", i), i % 2), (("TA", i), 2 + i % 2)]
    for t in range(NT):
        order += [(("mix", t, n), (2 * t + n) % 4) for n in range(2)]
        order += [(("x1T", t, half), 4 + half) for half in range(2)]
    order += [(("logits",), 6), (("affT",), 7), (("slotT",), 6)]
    place, count = {}, [0] * 8
    for name, bank in order:
        place[name] = (bank, count[bank])
        count[bank] += 1
    first = list(count)
    pair = [(("xsT", half), 6 + half) for half in range(2)]
    pair += [(("G", n), n) for n in range(2)] + [(("U", n), 2 + n) for n in range(2)]
    pair += [(("hT", half), 6 + half) for half in range(2)]
    pair += [(("O", n), 4 + n) for n in range(2)]
    pair += [(("Y", t, n), 6 + n) for t in range(NT) for n in range(2)]
    for name, bank in pair:
        place[name] = (bank, count[bank])
        count[bank] += 1
    per_pair = [c - f for c, f in zip(count, first)]
    total = [f + PAIRS * q for f, q in zip(first, per_pair)]
    return place, per_pair, total


USES, PER_PAIR, PER_LAYER = bank_uses()


def trunk(nc, x_in, positions, w_in, w_uq, w_ukv, w_router, params, w_out, ln1, ln2, w_gate, w_up, w_down,
          consts, iota, out):
    x1_rows = nc.dram_tensor("x1_rows", (S, D), F32, kind="Internal").ap()

    with ExitStack() as ctx:
        def sb(name, shape, dt=F32):
            return ctx.enter_context(nc.sbuf_tensor(name, shape, dt))

        def sem(name):
            return ctx.enter_context(nc.semaphore(name))

        ring = sb("ring", [P, RING, SLOT])
        cst = sb("cst", [P, N_CONST])
        slot_iota = sb("slot_iota", [P, S], I16)
        cos_a, sin_a, cos_d, sin_d = (sb(n, [P, S]) for n in ("cos_a", "sin_a", "cos_d", "sin_d"))
        par = sb("par", [P, N_PAR])
        wq = sb("wq", [P, 2, MLA_H * QK])
        wkv = sb("wkv", [P, MLA_H * (NOPE + VD)])
        wr = sb("wr", [P, KD, N_EXP])
        X = sb("X", [P, NT, D])
        work = sb("work", [P, 11 * 1024])
        stat = sb("stat", [P, 216])
        cur = sb("cur", [P, 2], I32)
        slot_i = sb("slot_i", [P, PAIRS], I32)

        ident = cst[:, IDENT:IDENT + P]
        ones = cst[:, ONES:ONES + P]
        rot_a = cst[:, ROT_A:ROT_A + P]
        rot_d = cst[:, ROT_D:ROT_D + P]
        band = cst[:, BAND:BAND + 3 * P]
        freq = cst[:, FREQ:FREQ + 1]

        def view(flat, at, *shape):
            n = int(np.prod(shape))
            v = flat[:, at:at + n]
            if len(shape) == 2:
                v = v.rearrange("p (a b) -> p a b", b=shape[1])
            return v

        Xf = X[:].rearrange("p t f -> p (t f)")
        u = view(Xf, 0, 2, S + CF_K - 1)
        scc = view(Xf, 1084, 2, S)
        prod = view(Xf, 2108, 2, S + SC_K - 1)
        gv = view(Xf, 3584, NT, 2 * GQ_D)
        csq = view(Xf, 0, 2, S)
        crs = view(Xf, 0, S)
        pt_a = view(Xf, 0, NT, S)
        pt_d = view(Xf, 0, GQ_H, 3 * P)
        p_d = view(Xf, 2048, GQ_H, 3 * P)
        p_a = view(Xf, 2048, 3, S)
        tmp_d = view(Xf, 2048, 3, S)
        xT = view(work, 0, KD, S)
        Qh = view(work, 0, MLA_H, S)
        Kh = view(work, 2048, MLA_H, S)
        mix = view(work, 4096, 8, S)
        YA, YB, YC, YD = 0, 2, 4, 6
        qlat = view(work, 8192, 2, S)
        V = view(work, 8192, NT, MLA_H * VD)
        kvlat = view(work, 9216, S)
        gq = view(work, 9728, 2, S)
        gk = view(work, 10752, S)
        pt_b = view(work, 9216, NT, S)
        sq_kv, sq_q, r_kv, r_q = mix[:, YA], (mix[:, YA + 1], mix[:, YD]), mix[:, YD + 1], mix[:, YA]
        x1T = view(work, 0, KD, S)
        xs = view(work, 4096, 2, D)
        xsT = view(work, 6144, KD, P)
        hid = view(work, 7168, FF)
        hidT = view(work, 8192, KD, P)
        o_sb = view(work, 9216, D)
        G = view(work, 10240, S)
        aff2 = view(work, 10240, 2, S)
        vals = view(work, 7168, 2, CAP)
        slotf = view(work, 7168 + 128, 2, CAP)
        idx = view(work, 7168 + 256, CAP).bitcast(U32)
        trig = view(work, 0, 6, S)

        bn = stat[:, 0:48].rearrange("p (t k) -> p t k", k=12)
        mv = stat[:, 48:56].rearrange("p (t k) -> p t k", k=2)
        rstd = stat[:, 56:60]
        nmr = stat[:, 60:64]
        mx, nmx, rs, rinv = (stat[:, 64 + 16 * i:80 + 16 * i] for i in range(4))
        snk = stat[:, 128:144]
        halfgb = stat[:, 144:148]
        half_neg = stat[:, 148:149]
        lmax, lsum = stat[:, 152:156], stat[:, 156:160]
        slot_f = stat[:, 160:168]
        slot_gate = stat[:, 168:176]
        c_rms, c_ln = stat[:, 176:177], stat[:, 177:178]
        aff = view(work, 7168 + 384, NT, N_EXP)

        banks = [ctx.enter_context(nc.psum_tensor(f"bank{i}", [P, 512], F32)) for i in range(8)]

        slot_full = [sem(f"slot_full{i}") for i in range(RING)]
        chunk_free = sem("chunk_free")
        bank_full = [sem(f"bank_full{i}") for i in range(8)]
        bank_free = [sem(f"bank_free{i}") for i in range(8)]
        consts_in, x_in_sem, pos_in = sem("consts_in"), sem("x_in_sem"), sem("pos_in")
        params_in = sem("params_in")
        small_ready = sem("small_ready")
        x_ready, x_stored, x_back = sem("x_ready"), sem("x_stored"), sem("x_back")
        angles_ready, sines_ready, trig_ready = sem("angles_ready"), sem("sines_ready"), sem("trig_ready")
        prod_ready, sconv_ready, yb_ready = sem("prod_ready"), sem("sconv_ready"), sem("yb_ready")
        cconv_ready, cdev_ready, csq_ready = sem("cconv_ready"), sem("cdev_ready"), sem("csq_ready")
        rnorm_ready, lat_ready, z_ready, th_ready, yc_ready = (
            sem(n) for n in ("rnorm_ready", "lat_ready", "z_ready", "th_ready", "yc_ready"))
        rot_d_out, rope_d_ready = sem("rot_d_out"), sem("rope_d_ready")
        cos_a_done, rope_a_ready = sem("cos_a_done"), sem("rope_a_ready")
        dmax_ready, dexp_done, dp_ready, pvd_done = (
            sem(n) for n in ("dmax_ready", "dexp_done", "dp_ready", "pvd_done"))
        amax_ready, ap_ready, pva_done = sem("amax_ready"), sem("ap_ready"), sem("pva_done")
        var_ready, rstd_ready, nmr_ready, normed, gained = (
            sem(n) for n in ("var_ready", "rstd_ready", "nmr_ready", "normed", "gained"))
        x1_ready, x1_stored, y_init = sem("x1_ready"), sem("x1_stored"), sem("y_init")
        lsub_ready, lexp_done, aff_ready, slots_ready, route_ready = (
            sem(n) for n in ("lsub_ready", "lexp_done", "aff_ready", "slots_ready", "route_ready"))
        cur_ready = sem("cur_ready")
        xs_full = [sem(f"xs_full{i}") for i in range(2)]
        g_ready = sem("g_ready")
        dve_step, act_step, pool_step = sem("dve_step"), sem("act_step"), sem("pool_step")
        passed = {e: sem(f"passed_{e}") for e in ("dve", "act", "pool", "pe")}

        def at(lay, per_layer, n):
            return lay * per_layer + n

        def bank_count(name, lay, more, pair):
            bank, nth = USES[name]
            if isinstance(pair, int) and pair == 0:
                return bank, lay * PER_LAYER[bank] + (nth + more)
            return bank, lay * PER_LAYER[bank] + pair * PER_PAIR[bank] + (nth + more)


        def full(eng, name, lay, pair=0):
            bank, n = bank_count(name, lay, 1, pair)
            eng.wait_ge(bank_full[bank], n)

        def read_out(eng, name, lay, pair=0):
            bank, n = bank_count(name, lay, 2, pair)
            eng.wait_ge(bank_free[bank], n)

        def before(eng, name, lay, pair=0):
            bank, n = bank_count(name, lay, 1, pair)
            eng.wait_ge(bank_free[bank], n)

        def B(name):
            return banks[USES[name][0]]

        def fullsem(name):
            return bank_full[USES[name][0]]

        def freesem(name):
            return bank_free[USES[name][0]]

        class Steps:

            def __init__(self, eng, s):
                self.eng, self.sem, self.n = eng, s, 0

            def did(self, ins):
                ins.then_inc(self.sem, 1)
                self.n += 1

            def wait(self):
                self.eng.wait_ge(self.sem, self.n)

            def restart(self):
                self.eng.drain()
                self.eng.sem_clear(self.sem)
                self.n = 0

        block = ctx.enter_context(nc.Block())

        @block.sync
        def _(sp):
            sp.dma_start(cst[:], consts).then_inc(consts_in, 16)
            sp.dma_start(slot_iota[:], iota).then_inc(consts_in, 16)

            with sp.Fori(0, DEPTH) as lay:
                for n in range(LN1_AT + 1):
                    sp.wait_ge(chunk_free, at(lay, CHUNKS, n + 1))
                    if n < WOUT_AT:
                        src, dst = w_in[lay, n], ring[:, n]
                    elif n < LN1_AT:
                        k = 2 * (n - WOUT_AT)
                        src = w_out[lay, k * P:(k + 2) * P].rearrange("(c p) f -> p c f", p=P)
                        dst = ring[:, n].rearrange("p (c f) -> p c f", c=2)
                    else:
                        src, dst = ln1[lay].partition_broadcast(P), ring[:, n]
                    sp.dma_start(dst, src).then_inc(slot_full[n], 16)
                with sp.Fori(0, PAIRS // BODY_PAIRS) as body:
                    for j in range(BODY_PAIRS * PAIR_CHUNKS):
                        pair, part, k = j // PAIR_CHUNKS, j % PAIR_CHUNKS // KD, j % KD
                        w = (w_gate, w_up, w_down)[part]
                        slot = (MOE_AT + j) % RING
                        sp.wait_ge(chunk_free, lay * CHUNKS + body * (BODY_PAIRS * PAIR_CHUNKS) + (MOE_AT + j + 1))
                        src = w[lay, bass.ds(body * (2 * BODY_PAIRS) + 2 * pair, 2), k * P:(k + 1) * P]
                        sp.dma_start(ring[:, slot].rearrange("p (e f) -> p e f", e=2),
                                     src.rearrange("e p f -> p e f")).then_inc(slot_full[slot], 16)
                sp.wait_ge(chunk_free, at(lay, CHUNKS, LN2_AT + 1))
                sp.dma_start(ring[:, LN2_AT % RING], ln2[lay].partition_broadcast(P))\
                    .then_inc(slot_full[LN2_AT % RING], 16)

        def slot_in(eng, lay, n, body=0):
            slot = n % RING
            less = 1 if slot == LN1_AT + 1 else 0
            count = lay * (16 * (REVS - less)) + 16 * (n // RING + 1 - less)
            if not isinstance(body, int):
                count = count + body * (16 * BODY_PAIRS * PAIR_CHUNKS // RING)
            eng.wait_ge(slot_full[slot], count)

        @block.tensor
        def _(pe):
            mm = nc.tensor.matmul

            def transposed(name, lay, src, n_blocks, pair=0, retire=0):
                before(pe, name, lay, pair)
                for c in range(n_blocks):
                    ins = nc.tensor.transpose(B(name)[:, c * P:(c + 1) * P], src[:, c * P:(c + 1) * P], ident)
                    if c == 0 and retire:
                        ins.then_inc(chunk_free, retire)
                ins.then_inc(fullsem(name), 1)

            pe.wait_ge(consts_in, 32)
            pe.sem_inc(chunk_free, RING - 1)
            for free in bank_free:
                pe.sem_inc(free, 1)
            with pe.Fori(0, DEPTH) as lay:
                for t in range(NT):
                    pe.wait_ge(x_ready, at(lay, NT, t + 1))
                    for half in range(2):
                        transposed(("xT", t, half), lay, X[:, t, half * 512:half * 512 + 512], 4,
                                   retire=1 if (t, half) == (NT - 1, 0) else 0)

                for i in range(N_IN):
                    n, fc = i // 2, i % 2
                    name = ("in", i)
                    if fc == 0:
                        slot_in(pe, lay, n)
                    if i == 0:
                        for t in range(NT):
                            for half in range(2):
                                read_out(pe, ("xT", t, half), lay)
                    before(pe, name, lay)
                    w = ring[:, n].rearrange("p (c f) -> p c f", c=KD)
                    if i == GQV:
                        for t in range(NT):
                            for k in range(KD):
                                ins = mm(B(name)[:, t * P:(t + 1) * P], xT[:, k, t * P:(t + 1) * P],
                                         w[:, k, 0:P], start=(k == 0), stop=(k == KD - 1))
                                if t == 0 and k == 0:
                                    ins.then_inc(chunk_free, 1)
                    else:
                        lo, m, to = (fc * P, P, 0) if i != KROPE else (fc * P, ROPE, NOPE)
                        for k in range(KD):
                            ins = mm(B(name)[to:to + m, :], w[:, k, lo:lo + m], xT[:, k, :],
                                     start=(k == 0), stop=(k == KD - 1))
                            if fc == 0 and k == 0 and i > 0:
                                ins.then_inc(chunk_free, 1)
                    ins.then_inc(fullsem(name), 1)

                    if i == QLAT + 1:
                        read_out(pe, ("in", KV), lay)
                        before(pe, ("ssq", 0), lay)
                        mm(B(("ssq", 0))[:, :], ones, sq_kv, start=True, stop=True).then_inc(fullsem(("ssq", 0)), 1)
                        pe.wait_ge(cconv_ready, at(lay, 2, 2))
                        before(pe, ("mean",), lay)
                        mm(B(("mean",))[:, :], ones, mix[:, YC], start=True, stop=False)
                        mm(B(("mean",))[:, :], ones, mix[:, YC + 1], start=False, stop=True)\
                            .then_inc(fullsem(("mean",)), 1)
                        read_out(pe, ("in", GQK), lay)
                        before(pe, ("rotD", 0), lay)
                        mm(B(("rotD", 0))[:, :], rot_d, gk, start=True, stop=True).then_inc(fullsem(("rotD", 0)), 1)
                    if i == GQQ + 1:
                        read_out(pe, ("in", QLAT), lay)
                        read_out(pe, ("in", QLAT + 1), lay)
                        before(pe, ("ssq", 1), lay)
                        mm(B(("ssq", 1))[:, :], ones, sq_q[0], start=True, stop=False)
                        mm(B(("ssq", 1))[:, :], ones, sq_q[1], start=False, stop=True)\
                            .then_inc(fullsem(("ssq", 1)), 1)
                    if i == GQV:
                        for j in range(2):
                            name = ("rotD", 1 + j)
                            read_out(pe, ("in", GQQ + j), lay)
                            before(pe, name, lay)
                            mm(B(name)[:, :], rot_d, gq[:, j], start=True, stop=True).then_inc(fullsem(name), 1)

                pe.wait_ge(csq_ready, at(lay, 2, 2))
                before(pe, ("var",), lay)
                mm(B(("var",))[:, :], ones, csq[:, 0], start=True, stop=False).then_inc(chunk_free, 1)
                mm(B(("var",))[:, :], ones, csq[:, 1], start=False, stop=True).then_inc(fullsem(("var",)), 1)

                pe.wait_ge(params_in, at(lay, 64, 64))
                pe.wait_ge(lat_ready, at(lay, 3, 3))
                for h in range(MLA_H):
                    name = ("qup", h)
                    before(pe, name, lay)
                    for k in range(2):
                        ins = mm(B(name)[0:QK, :], wq[:, k, h * QK:(h + 1) * QK], qlat[:, k],
                                 start=(k == 0), stop=(k == 1))
                    ins.then_inc(fullsem(name), 1)
                for j in range(2):
                    name = ("kup", j)
                    before(pe, name, lay)
                    for e in range(2):
                        h = 2 * j + e
                        ins = mm(B(name)[e * NOPE:(e + 1) * NOPE, :], wkv[:, h * NOPE:(h + 1) * NOPE], kvlat,
                                 start=True, stop=True)
                    ins.then_inc(fullsem(name), 1)
                for j in range(2):
                    name = ("vup", j)
                    before(pe, name, lay)
                    for e in range(2):
                        t = 2 * j + e
                        ins = mm(B(name)[:, e * 256:(e + 1) * 256], kvlat[:, t * P:(t + 1) * P],
                                 wkv[:, MLA_H * NOPE:], start=True, stop=True)
                    ins.then_inc(fullsem(name), 1)
                r = slice(NOPE, QK)
                for h in range(MLA_H):
                    name = ("rotQ", h)
                    read_out(pe, ("qup", h), lay)
                    before(pe, name, lay)
                    pe.sem_inc(passed["pe"], 1)
                    mm(B(name)[r, :], rot_a[r, r], Qh[r, h, :], start=True, stop=True).then_inc(fullsem(name), 1)
                read_out(pe, ("in", KROPE), lay)
                before(pe, ("rotK",), lay)
                pe.sem_inc(passed["pe"], 1)
                mm(B(("rotK",))[r, :], rot_a[r, r], Kh[r, 0, :], start=True, stop=True).then_inc(fullsem(("rotK",)), 1)

                def window(n):
                    return max(n - 1, 0), min(n + 2, NT)

                def d_scores(i):
                    n, h = divmod(i, GQ_H)
                    lo, hi = window(n)
                    rows = slice(64 * (h // 2), 64 * (h // 2) + 64)
                    before(pe, ("SD", i), lay)
                    mm(B(("SD", i))[:, 0:(hi - lo) * P], gq[rows, h % 2, n * P:(n + 1) * P],
                       gk[rows, lo * P:hi * P], start=True, stop=True).then_inc(fullsem(("SD", i)), 1)

                def d_values(n, j):
                    lo, hi = window(n)
                    if n == 0:
                        before(pe, ("YD", j), lay)
                    for e in range(2):
                        read_out(pe, ("TD", n * GQ_H + 2 * j + e), lay)
                    for kb in range(hi - lo):
                        for e in range(2):
                            h = 2 * j + e
                            ins = mm(B(("YD", j))[64 * e:64 * e + 64, n * P:(n + 1) * P],
                                     gv[:, lo + kb, 64 * j:64 * j + 64], pt_d[:, h, kb * P:(kb + 1) * P],
                                     start=(kb == 0), stop=(kb == hi - lo - 1))
                    ins.then_inc(pvd_done if n < NT - 1 else fullsem(("YD", j)), 1)

                pe.wait_ge(rope_d_ready, at(lay, 3, 3))
                read_out(pe, ("in", GQV), lay)
                d_scores(0)
                d_scores(1)
                for i in range(NT * GQ_H):
                    n, h = divmod(i, GQ_H)
                    lo, hi = window(n)
                    pe.wait_ge(dp_ready, at(lay, NT * GQ_H, i + 1))
                    before(pe, ("TD", i), lay)
                    for kb in range(hi - lo):
                        ins = nc.tensor.transpose(B(("TD", i))[:, kb * P:(kb + 1) * P],
                                                  p_d[:, h, kb * P:(kb + 1) * P], ident)
                    ins.then_inc(fullsem(("TD", i)), 1)
                    if i + 2 < NT * GQ_H:
                        d_scores(i + 2)
                    if h % 2 == 0 and i > 0:
                        d_values((i - 1) // GQ_H, (i - 1) % GQ_H // 2)

                def a_scores(i):
                    h, t = divmod(i, NT)
                    before(pe, ("SA", i), lay)
                    mm(B(("SA", i))[:, :], Qh[0:QK, h, t * P:(t + 1) * P], Kh[0:QK, h, :], start=True, stop=True)\
                        .then_inc(fullsem(("SA", i)), 1)

                def a_values(h):
                    pt = (pt_a, pt_b)[h % 2]
                    j, e = divmod(h, 2)
                    if h == 0:
                        read_out(pe, ("vup", 0), lay)
                        read_out(pe, ("vup", 1), lay)
                    read_out(pe, ("TA", 4 * h + 2), lay)
                    read_out(pe, ("TA", 4 * h + 3), lay)
                    if e == 0:
                        before(pe, ("YA", j), lay)
                    for k in range(NT):
                        ins = mm(B(("YA", j))[64 * e:64 * e + 64, :], V[:, k, h * VD:(h + 1) * VD], pt[:, k],
                                 start=(k == 0), stop=(k == NT - 1))
                    if e == 0:
                        ins.then_inc(pva_done, 1)
                    else:
                        ins.then_inc(fullsem(("YA", j)), 1)

                pe.wait_ge(rope_a_ready, at(lay, 5, 5))
                for h in range(MLA_H // 2):
                    read_out(pe, ("kup", h), lay)
                a_scores(0)
                d_values(NT - 1, 1)
                a_scores(1)
                for i in range(NT * MLA_H):
                    h, t = divmod(i, NT)
                    pe.wait_ge(ap_ready, at(lay, NT * MLA_H, i + 1))
                    before(pe, ("TA", i), lay)
                    for k in range(NT):
                        ins = nc.tensor.transpose(B(("TA", i))[:, k * P:(k + 1) * P],
                                                  p_a[:, i % 3, k * P:(k + 1) * P], ident)
                    ins.then_inc(fullsem(("TA", i)), 1)
                    if i + 2 < NT * MLA_H:
                        a_scores(i + 2)
                    if t == 0 and h > 0:
                        a_values(h - 1)
                a_values(MLA_H - 1)

                def router(t):
                    for half in range(2):
                        read_out(pe, ("x1T", t, half), lay)
                    for k in range(KD):
                        ins = mm(B(("logits",))[:, t * N_EXP:(t + 1) * N_EXP], x1T[:, k, t * P:(t + 1) * P],
                                 wr[:, k, :], start=(k == 0), stop=(k == KD - 1))
                    return ins

                def x1_turned(t, retire=0):
                    pe.wait_ge(x1_ready, at(lay, NT, t + 1))
                    for half in range(2):
                        transposed(("x1T", t, half), lay, X[:, t, half * 512:half * 512 + 512], 4,
                                   retire=retire if half == 0 else 0)

                pe.wait_ge(yb_ready, at(lay, 2, 2))
                pe.wait_ge(yc_ready, at(lay, 2, 2))
                read_out(pe, ("YD", 0), lay)
                read_out(pe, ("YD", 1), lay)
                read_out(pe, ("YA", 0), lay)
                read_out(pe, ("YA", 1), lay)
                before(pe, ("logits",), lay)
                for t in range(NT):
                    for n in range(2):
                        name = ("mix", t, n)
                        before(pe, name, lay)
                        for k in (4, 5, 2, 3, 6, 7, 0, 1):
                            if t == 0 and n == 0 and k % 2 == 0:
                                slot_in(pe, lay, WOUT_AT + k // 2)
                            w = ring[:, WOUT_AT + k // 2].rearrange("p (c f) -> p c f", c=2)
                            ins = mm(B(name)[:, :], mix[:, k, t * P:(t + 1) * P], w[:, k % 2, n * 512:(n + 1) * 512],
                                     start=(k == 4), stop=(k == 1))
                        ins.then_inc(fullsem(name), 1)
                    if t >= 2:
                        x1_turned(t - 2, retire=4 if t == NT - 1 else 0)
                        router(t - 2)
                x1_turned(2)
                router(2)
                x1_turned(3, retire=2)
                router(3).then_inc(fullsem(("logits",)), 1)

                pe.wait_ge(aff_ready, at(lay, 1, 1))
                before(pe, ("affT",), lay)
                for t in range(NT):
                    ins = nc.tensor.transpose(B(("affT",))[0:N_EXP, t * P:(t + 1) * P], aff[:, t, :], ident)
                ins.then_inc(fullsem(("affT",)), 1)
                pe.wait_ge(slots_ready, at(lay, 1, 1))
                before(pe, ("slotT",), lay)
                pe.sem_inc(passed["pe"], 1)
                for c, src in enumerate((slotf, vals)):
                    ins = nc.tensor.transpose(B(("slotT",))[:, c * N_EXP:(c + 1) * N_EXP],
                                              src[0:N_EXP].rearrange("p a b -> p (a b)"), ident[0:N_EXP, 0:N_EXP])
                ins.then_inc(fullsem(("slotT",)), 1)

                with pe.Fori(0, PAIRS // BODY_PAIRS) as body:
                    for b in range(BODY_PAIRS):
                        pair = body * BODY_PAIRS + b
                        at0 = MOE_AT + b * PAIR_CHUNKS
                        pe.wait_ge(xs_full[b], lay * (16 * PAIRS // 2) + body * 16 + 16)
                        for half in range(2):
                            transposed(("xsT", half), lay, xs[:, b, half * 512:half * 512 + 512], 4, pair)
                        for half in range(2):
                            read_out(pe, ("xsT", half), lay, pair)
                        for part, kind in enumerate("GU"):
                            for n in range(2):
                                before(pe, (kind, n), lay, pair)
                            for k in range(KD):
                                j = at0 + part * KD + k
                                slot_in(pe, lay, j, body)
                                w = ring[:, j % RING].rearrange("p (e f) -> p e f", e=2)
                                for n in range(2):
                                    for e in range(2):
                                        ins = mm(B((kind, n))[64 * e:64 * e + 64, :], xsT[:, k, 64 * e:64 * e + 64],
                                                 w[:, e, n * 512:(n + 1) * 512], start=(k == 0), stop=(k == KD - 1))
                                        if n == 0 and e == 0 and part + k > 0:
                                            ins.then_inc(chunk_free, 1)
                                    if k == KD - 1:
                                        ins.then_inc(fullsem((kind, n)), 1)
                        for half in range(2):
                            read_out(pe, ("U", half), lay, pair)
                            transposed(("hT", half), lay, hid[:, half * 512:half * 512 + 512], 4, pair,
                                       retire=1 if half == 0 else 0)
                        for half in range(2):
                            read_out(pe, ("hT", half), lay, pair)
                        for n in range(2):
                            before(pe, ("O", n), lay, pair)
                        for k in range(KD):
                            j = at0 + 2 * KD + k
                            slot_in(pe, lay, j, body)
                            w = ring[:, j % RING].rearrange("p (e f) -> p e f", e=2)
                            for n in range(2):
                                for e in range(2):
                                    ins = mm(B(("O", n))[64 * e:64 * e + 64, :], hidT[:, k, 64 * e:64 * e + 64],
                                             w[:, e, n * 512:(n + 1) * 512], start=(k == 0), stop=(k == KD - 1))
                                    if n == 0 and e == 0 and k > 0:
                                        ins.then_inc(chunk_free, 1)
                                if k == KD - 1:
                                    ins.then_inc(fullsem(("O", n)), 1)
                        pe.wait_ge(g_ready, lay * PAIRS + body * BODY_PAIRS + (b + 1))
                        for n in range(2):
                            read_out(pe, ("O", n), lay, pair)
                        for t in range(NT):
                            for n in range(2):
                                name = ("Y", t, n)
                                bank, nth = USES[name]
                                before(pe, name, lay, pair)
                                ins = mm(banks[bank][:, :], G[:, t * P:(t + 1) * P], o_sb[:, n * 512:(n + 1) * 512],
                                         start=True, stop=True)
                                if t == 0 and n == 0:
                                    ins.then_inc(bank_full[bank], 1)
                                elif t == 0 and n == 1:
                                    ins.then_inc(bank_full[bank], 1)
                                else:
                                    ins.then_inc(bank_full[bank], 1)
                        pe.wait_ge(bank_full[USES[("Y", 0, 0)][0]],
                                   bank_count(("Y", 0, 0), lay, 1, pair)[1])
                        pe.sem_inc(chunk_free, 1)

        @block.vector
        def _(v):
            step = Steps(v, dve_step)
            did, wait = step.did, step.wait

            def hold(s, n):
                v.wait_ge(s, n)
                v.sem_inc(passed["dve"], 1)

            nc.vector.memset(half_neg, -0.5)
            nc.vector.memset(c_rms, RMS_EPS)
            nc.vector.memset(c_ln, LN_EPS).then_inc(small_ready, 1)

            v.wait_ge(pos_in, 16)
            v.wait_ge(consts_in, 32)
            pos, ang, turns = trig[:, 0], trig[:, 1], trig[:, 2]
            sin_arg, cos_arg = trig[:, 3], trig[:, 4]
            did(nc.vector.tensor_copy(pos, trig[:, 5].bitcast(I32)))
            wait()
            did(nc.vector.tensor_scalar(ang, pos, freq, None, ALU.mult))
            wait()
            for arg, quarter in ((sin_arg, 0.0), (cos_arg, 0.25)):
                did(nc.vector.tensor_scalar(turns, ang, float(1 / (2 * np.pi)), quarter, ALU.mult, ALU.add))
                wait()
                did(nc.vector.tensor_scalar(turns, turns, ROUND, None, ALU.add))
                wait()
                did(nc.vector.tensor_scalar(turns, turns, ROUND, None, ALU.subtract))
                wait()
                src = ang
                for c in (TWO_PI_1, TWO_PI_2, TWO_PI_3):
                    did(nc.vector.scalar_tensor_tensor(out=arg, in0=turns, scalar=-c, in1=src,
                                                       op0=ALU.mult, op1=ALU.add))
                    wait()
                    src = arg
                did(nc.vector.tensor_scalar(arg, arg, 2 * np.pi * quarter, PI_BELOW, ALU.add, ALU.min))
                wait()
                nc.vector.tensor_scalar(arg, arg, -PI_BELOW, None, ALU.max).then_inc(angles_ready, 1)
                wait()
            v.wait_ge(sines_ready, 2)
            every_second = [2 * (i % 16) for i in range(32)]
            nc.vector.stream_shuffle(sin_a[:], sin_d[:], every_second).then_inc(trig_ready, 1)
            nc.vector.stream_shuffle(cos_a[:], cos_d[:], every_second).then_inc(trig_ready, 1)
            v.wait_ge(trig_ready, 2)
            v.wait_ge(x_in_sem, 16 * NT)
            v.sem_inc(x_ready, NT)

            def layer_norm(lay, t, gains, second, last):
                k = 4 * second + t
                for c in range(2):
                    did(nc.vector.bn_stats(bn[:, t, 6 * c:6 * c + 6], X[:, t, c * 512:(c + 1) * 512]))
                wait()
                nc.vector.bn_aggr(mv[:, t, :], bn[:, t, :]).then_inc(var_ready, 1)

            def layer_norm_mid(lay, t, second):
                k = 4 * second + t
                v.wait_ge(rstd_ready, at(lay, 2 * NT, k + 1))
                nc.vector.tensor_scalar(nmr[:, t:t + 1], mv[:, t, 0:1], rstd[:, t:t + 1], -1.0,
                                        ALU.mult, ALU.mult).then_inc(nmr_ready, 1)

            def layer_norm_end(lay, t, gains, second, done):
                k = 4 * second + t
                v.wait_ge(gained, at(lay, 2 * NT, k + 1))
                nc.vector.tensor_tensor(X[:, t], X[:, t], gains[:, D:2 * D], ALU.add).then_inc(done, 1)

            with v.Fori(0, DEPTH) as lay:
                step.restart()
                hold(x_stored, at(lay, 16 * NT, 16 * NT))
                full(v, ("in", 0), lay)
                v.sem_inc(passed["dve"], 1)
                pad = CF_K // 2
                did(nc.vector.memset(u[:, :, 0:pad], 0.0))
                did(nc.vector.memset(u[:, :, pad + S:], 0.0))
                did(nc.vector.memset(prod[:, :, 0:1], 0.0))
                did(nc.vector.memset(prod[:, :, S + 1:], 0.0))
                for j in range(2):
                    read_out(v, ("in", CF_G + j), lay)
                    v.sem_inc(passed["dve"], 1)
                    full(v, ("in", CF_A + j), lay)
                    nc.vector.scalar_tensor_tensor(out=u[:, j, pad:pad + S], in0=mix[:, YC + j], scalar=1.0,
                                                   in1=B(("in", CF_A + j))[:, :], op0=ALU.add, op1=ALU.mult)\
                        .then_inc(freesem(("in", CF_A + j)), 1)
                hold(params_in, at(lay, 64, 64))
                for j in range(2):
                    read_out(v, ("in", CF_A + j), lay)
                wait()
                for j in range(2):
                    c = PAR["cconv"] + j * CF_K
                    did(nc.vector.tensor_scalar(mix[:, YC + j], u[:, j, 0:S], par[:, c:c + 1], None, ALU.mult))
                start = step.n
                with v.Fori(1, CF_K) as tap:
                    for j in range(2):
                        v.wait_ge(dve_step, tap * 2 + (start - 3 + j))
                        nc.vector.scalar_tensor_tensor(
                            out=mix[:, YC + j], in0=u[:, j, bass.ds(tap, S)],
                            scalar=par[:, bass.ds(tap + (PAR["cconv"] + j * CF_K), 1)],
                            in1=mix[:, YC + j], op0=ALU.mult, op1=ALU.add).then_inc(dve_step, 1)
                step.n += 2 * (CF_K - 1)
                wait()
                for j in range(2):
                    c = PAR["cconv_b"] + j
                    nc.vector.tensor_scalar(mix[:, YC + j], mix[:, YC + j], 0.5, par[:, c:c + 1], ALU.mult, ALU.add)\
                        .then_inc(cconv_ready, 1)
                did(nc.vector.tensor_scalar(halfgb, par[:, PAR["cnorm_g"]:PAR["cnorm_g"] + 4], 0.5, None, ALU.mult))
                hold(prod_ready, at(lay, 2, 2))
                for k in range(SC_K):
                    for j in range(2):
                        c = PAR["sconv"] + j * SC_K + k
                        if k == 0:
                            did(nc.vector.tensor_scalar(scc[:, j], prod[:, j, 0:S], par[:, c:c + 1], None, ALU.mult))
                        else:
                            v.wait_ge(dve_step, step.n - 1 if (j == 0 or k < SC_K - 1) else step.n)
                            ins = nc.vector.scalar_tensor_tensor(
                                out=scc[:, j], in0=prod[:, j, k:k + S], scalar=par[:, c:c + 1],
                                in1=scc[:, j], op0=ALU.mult, op1=ALU.add)
                            if k < SC_K - 1:
                                did(ins)
                            else:
                                ins.then_inc(sconv_ready, 1)
                for j in range(2):
                    full(v, ("mean",), lay)
                    v.sem_inc(passed["dve"], 1)
                    v.wait_ge(cconv_ready, at(lay, 2, 2))
                    nc.vector.scalar_tensor_tensor(
                        out=mix[:, YC + j], in0=B(("mean",))[:, :], scalar=-1.0 / CF_W, in1=mix[:, YC + j],
                        op0=ALU.mult, op1=ALU.add).then_inc(freesem(("mean",)) if j else cdev_ready, 1)
                v.wait_ge(rnorm_ready, at(lay, 3, 1))
                nc.vector.scalar_tensor_tensor(out=kvlat, in0=kvlat, scalar=par[:, PAR["kv_g"]:PAR["kv_g"] + 1],
                                               in1=r_kv, op0=ALU.mult, op1=ALU.mult).then_inc(lat_ready, 1)
                hold(yb_ready, at(lay, 2, 2))
                full(v, ("rotD", 0), lay)
                nc.vector.tensor_tensor(tmp_d[:, 0], B(("rotD", 0))[:, :], sin_d[:], ALU.mult)\
                    .then_inc(freesem(("rotD", 0)), 1)
                v.wait_ge(rnorm_ready, at(lay, 3, 2))
                for j in range(2):
                    c = PAR["q_g"] + j
                    nc.vector.scalar_tensor_tensor(out=qlat[:, j], in0=qlat[:, j], scalar=par[:, c:c + 1], in1=r_q,
                                                   op0=ALU.mult, op1=ALU.mult).then_inc(lat_ready, 1)
                for j in range(2):
                    name = ("rotD", 1 + j)
                    full(v, name, lay)
                    nc.vector.tensor_tensor(tmp_d[:, 1 + j], B(name)[:, :], sin_d[:], ALU.mult)\
                        .then_inc(freesem(name), 1)
                v.wait_ge(rnorm_ready, at(lay, 3, 3))
                for j in range(2):
                    did(nc.vector.tensor_tensor(mix[:, YC + j], mix[:, YC + j], crs, ALU.mult))
                wait()
                for j in range(2):
                    nc.vector.tensor_scalar(mix[:, YC + j], mix[:, YC + j], halfgb[:, j:j + 1], halfgb[:, 2 + j:3 + j],
                                            ALU.mult, ALU.add).then_inc(z_ready, 1)
                v.wait_ge(th_ready, at(lay, 2, 2))
                for j in range(2):
                    nc.vector.scalar_tensor_tensor(out=mix[:, YC + j], in0=csq[:, j], scalar=1.0, in1=mix[:, YC + j],
                                                   op0=ALU.add, op1=ALU.mult).then_inc(yc_ready, 1)

                def d_width(n):
                    return (0 if n > 0 else P), ((min(n + 2, NT) - max(n - 1, 0)) * P)

                def d_max(i):
                    n, h = divmod(i, GQ_H)
                    off, w = d_width(n)
                    if i >= GQ_H:
                        full(v, ("TD", i - GQ_H), lay)
                        v.sem_inc(passed["dve"], 1)
                    full(v, ("SD", i), lay)
                    v.sem_inc(passed["dve"], 1)
                    ins = nc.vector.tensor_tensor_reduce(p_d[:, h, 0:w], B(("SD", i))[:, 0:w], band[:, off:off + w],
                                                         1.0, -3.0e38, ALU.add, ALU.max, mx[:, i:i + 1])
                    ins.then_inc(freesem(("SD", i)), 1)
                    read_out(v, ("SD", i), lay)
                    c = PAR["sink"] + h
                    nc.vector.tensor_scalar(nmx[:, i:i + 1], mx[:, i:i + 1], par[:, c:c + 1], -1.0,
                                            ALU.max, ALU.mult).then_inc(dmax_ready, 1)

                def d_norm(i):
                    n, h = divmod(i, GQ_H)
                    off, w = d_width(n)
                    v.wait_ge(dexp_done, at(lay, NT * GQ_H, i + 1))
                    did(nc.vector.tensor_tensor(rs[:, i:i + 1], rs[:, i:i + 1], snk[:, i:i + 1], ALU.add))
                    wait()
                    did(nc.vector.reciprocal(rinv[:, i:i + 1], rs[:, i:i + 1]))
                    wait()
                    nc.vector.tensor_scalar(p_d[:, h, 0:w], p_d[:, h, 0:w], rinv[:, i:i + 1], None, ALU.mult)\
                        .then_inc(dp_ready, 1)

                hold(rope_d_ready, at(lay, 3, 3))
                d_max(0)
                for i in range(NT * GQ_H):
                    if i + 1 < NT * GQ_H:
                        d_max(i + 1)
                    d_norm(i)
                    if i < MLA_H + 1:
                        r = slice(NOPE, QK)
                        tmp = mix[r, YA + i % 2]
                        if i == 0:
                            hold(cos_a_done, at(lay, 2, 1))
                            full(v, ("rotK",), lay)
                            nc.vector.tensor_tensor(tmp, B(("rotK",))[r, :], sin_a[r, :], ALU.mult)\
                                .then_inc(freesem(("rotK",)), 1)
                            read_out(v, ("rotK",), lay)
                            for h in (1, 2, 3, 0):
                                ins = nc.vector.tensor_tensor(Kh[r, h, :], Kh[r, 0, :], tmp, ALU.add)
                            ins.then_inc(rope_a_ready, 1)
                        else:
                            if i == 1:
                                hold(cos_a_done, at(lay, 2, 2))
                            name = ("rotQ", i - 1)
                            full(v, name, lay)
                            nc.vector.tensor_tensor(tmp, B(name)[r, :], sin_a[r, :], ALU.mult).then_inc(freesem(name), 1)
                            read_out(v, name, lay)
                            nc.vector.tensor_tensor(Qh[r, i - 1, :], Qh[r, i - 1, :], tmp, ALU.add)\
                                .then_inc(rope_a_ready, 1)

                def a_max(i):
                    full(v, ("SA", i), lay)
                    v.sem_inc(passed["dve"], 1)
                    nc.vector.tensor_reduce(nmx[:, i:i + 1], B(("SA", i))[:, :], AX_X, ALU.max, negate=True)\
                        .then_inc(amax_ready, 1)

                def a_norm(i):
                    read_out(v, ("SA", i), lay)
                    did(nc.vector.reciprocal(rinv[:, i:i + 1], rs[:, i:i + 1]))
                    wait()
                    nc.vector.tensor_scalar(p_a[:, i % 3], p_a[:, i % 3], rinv[:, i:i + 1], None, ALU.mult)\
                        .then_inc(ap_ready, 1)

                a_max(0)
                for i in range(NT * MLA_H):
                    if i + 1 < NT * MLA_H:
                        a_max(i + 1)
                    a_norm(i)
                    if i == 1:
                        for j in range(2):
                            full(v, ("YD", j), lay)
                            nc.vector.tensor_copy(mix[:, YD + j], B(("YD", j))[:, :]).then_inc(freesem(("YD", j)), 1)
                for j in range(2):
                    full(v, ("YA", j), lay)
                    nc.vector.tensor_copy(mix[:, YA + j], B(("YA", j))[:, :]).then_inc(freesem(("YA", j)), 1)

                ln1_gb = ring[:, LN1_AT]
                hold(x_back, at(lay, 16, 16))
                slot_in(v, lay, LN1_AT)
                v.sem_inc(passed["dve"], 1)
                for t in range(NT + 1):
                    if t < NT:
                        for n in range(2):
                            name = ("mix", t, n)
                            full(v, name, lay)
                            cols = slice(n * 512, (n + 1) * 512)
                            nc.vector.scalar_tensor_tensor(out=X[:, t, cols], in0=X[:, t, cols], scalar=ALPHA,
                                                           in1=B(name)[:, :], op0=ALU.mult, op1=ALU.add)\
                                .then_inc(freesem(name), 1)
                        for n in range(2):
                            read_out(v, ("mix", t, n), lay)
                            v.sem_inc(passed["dve"], 1)
                        layer_norm(lay, t, ln1_gb, 0, x1_ready)
                        layer_norm_mid(lay, t, 0)
                    if t > 0:
                        layer_norm_end(lay, t - 1, ln1_gb, 0, x1_ready)

                lg = aff
                full(v, ("logits",), lay)
                v.sem_inc(passed["dve"], 1)
                lgp = B(("logits",))[:, 0:NT * N_EXP].rearrange("p (t e) -> p t e", e=N_EXP)
                br = par[:, PAR["b_router"]:PAR["b_router"] + N_EXP].unsqueeze(1).broadcast_to([P, NT, N_EXP])
                nc.vector.tensor_tensor(lg, lgp, br, ALU.add).then_inc(freesem(("logits",)), 1)
                read_out(v, ("logits",), lay)
                v.sem_inc(passed["dve"], 1)
                did(nc.vector.tensor_reduce(lmax, lg, AX_X, ALU.max))
                wait()
                nc.vector.tensor_tensor(lg, lg, lmax.unsqueeze(2).broadcast_to([P, NT, N_EXP]), ALU.subtract)\
                    .then_inc(lsub_ready, 1)
                hold(lexp_done, at(lay, 1, 1))
                did(nc.vector.tensor_reduce(lsum, lg, AX_X, ALU.add))
                wait()
                did(nc.vector.reciprocal(lsum, lsum))
                wait()
                nc.vector.tensor_tensor(lg, lg, lsum.unsqueeze(2).broadcast_to([P, NT, N_EXP]), ALU.mult)\
                    .then_inc(aff_ready, 1)
                full(v, ("affT",), lay)
                nc.vector.tensor_copy(aff2[0:N_EXP, 0], B(("affT",))[0:N_EXP, :]).then_inc(freesem(("affT",)), 1)
                read_out(v, ("affT",), lay)
                v.sem_inc(passed["dve"], 1)
                for r8 in range(CAP // 8):
                    src, nxt = aff2[0:N_EXP, r8 % 2], aff2[0:N_EXP, (r8 + 1) % 2]
                    top = vals[0:N_EXP, 0, 8 * r8:8 * r8 + 8]
                    did(nc.vector.max(top, src))
                    wait()
                    if r8 < CAP // 8 - 1:
                        did(nc.vector.match_replace(nxt, top, src, -1.0))
                    did(nc.vector.max_index(idx[0:N_EXP, 8 * r8:8 * r8 + 8], top, src))
                    v.wait_ge(dve_step, step.n - 1)
                wait()
                did(nc.vector.tensor_copy(slotf[0:N_EXP, 0, :], idx[0:N_EXP, :]))
                did(nc.vector.tensor_copy(slotf[0:N_EXP, 1, :], idx[0:N_EXP, :]))
                did(nc.vector.tensor_copy(vals[0:N_EXP, 1, :], vals[0:N_EXP, 0, :]))
                wait()
                v.sem_inc(slots_ready, 1)
                full(v, ("slotT",), lay)
                v.sem_inc(passed["dve"], 1)
                for c, dst in enumerate((slot_f, slot_gate)):
                    src = B(("slotT",))[:, c * N_EXP:(c + 1) * N_EXP].rearrange("p (q e) -> p q e", e=2)
                    for e in range(2):
                        rows = slice(64 * e, 64 * e + 64)
                        ins = nc.vector.tensor_copy(dst[rows, :], src[rows, :, e])
                        if (c, e) != (1, 1):
                            did(ins)
                        else:
                            ins.then_inc(freesem(("slotT",)), 1)
                wait()
                nc.vector.tensor_copy(slot_i[:], slot_f).then_inc(route_ready, 1)

                hold(y_init, at(lay, NT, NT))
                with v.Fori(0, PAIRS // BODY_PAIRS) as body:
                    for b in range(BODY_PAIRS):
                        pair = body * BODY_PAIRS + b
                        for n in range(2):
                            cols = slice(n * 512, (n + 1) * 512)
                            read_out(v, ("G", n), lay, pair)
                            v.sem_inc(passed["dve"], 1)
                            full(v, ("U", n), lay, pair)
                            nc.vector.tensor_tensor(hid[:, cols], hid[:, cols], B(("U", n))[:, :], ALU.mult)\
                                .then_inc(freesem(("U", n)), 1)
                        nc.vector.tensor_scalar(G, slot_iota[:], slot_f[:, bass.ds(pair, 1)],
                                                slot_gate[:, bass.ds(pair, 1)], ALU.is_equal, ALU.mult)\
                            .then_inc(g_ready, 1)
                        full(v, ("O", 1), lay, pair)
                        nc.vector.tensor_copy(o_sb[:, 512:1024], B(("O", 1))[:, :]).then_inc(freesem(("O", 1)), 1)
                        for t in range(NT):
                            for n in range(2):
                                name = ("Y", t, n)
                                cols = slice(n * 512, (n + 1) * 512)
                                full(v, name, lay, pair)
                                nc.vector.tensor_tensor(X[:, t, cols], X[:, t, cols], B(name)[:, :], ALU.add)\
                                    .then_inc(freesem(name), 1)

                ln2_gb = ring[:, LN2_AT % RING]
                slot_in(v, lay, LN2_AT)
                v.sem_inc(passed["dve"], 1)
                for n in range(2):
                    read_out(v, ("Y", NT - 1, n), lay, PAIRS - 1)
                    v.sem_inc(passed["dve"], 1)
                for t in range(NT + 1):
                    if t < NT:
                        layer_norm(lay, t, ln2_gb, 1, x_ready)
                        layer_norm_mid(lay, t, 1)
                    if t > 0:
                        layer_norm_end(lay, t - 1, ln2_gb, 1, x_ready)

        @block.scalar
        def _(ac):
            step = Steps(ac, act_step)
            did, wait = step.did, step.wait
            act = nc.scalar.activation

            for t in range(NT):
                ac.dma_start(X[:, t], x_in[t * P:(t + 1) * P]).then_inc(x_in_sem, 16)
            ac.dma_start(trig[:, 5].bitcast(I32), positions.partition_broadcast(P)).then_inc(pos_in, 16)
            nc.scalar.preload_act_table(ACT.Sin)
            ac.wait_ge(angles_ready, 1)
            act(sin_d[:], trig[:, 3], ACT.Sin).then_inc(sines_ready, 1)
            ac.wait_ge(angles_ready, 2)
            act(cos_d[:], trig[:, 4], ACT.Sin).then_inc(sines_ready, 1)
            ac.wait_ge(sines_ready, 2)
            ac.wait_ge(small_ready, 1)
            ac.wait_ge(x_in_sem, 16 * NT)
            for t in range(NT):
                ac.dma_start(out[t * P:(t + 1) * P], X[:, t]).then_inc(x_stored, 16)

            with ac.Fori(0, DEPTH) as lay:
                step.restart()
                nc.scalar.preload_act_table_set("exp_and_others")
                for t in range(NT):
                    for half in range(2):
                        name = ("xT", t, half)
                        full(ac, name, lay)
                        act(xT[:, 4 * half:4 * half + 4, t * P:(t + 1) * P],
                            B(name)[:, :].rearrange("p (c f) -> p c f", c=4), ACT.Copy).then_inc(freesem(name), 1)
                ac.wait_ge(x_stored, at(lay, 16 * NT, 16 * NT))
                ac.dma_start(par[:], params[lay]).then_inc(params_in, 16)
                ac.dma_start(wq[:], w_uq[lay].rearrange("(c p) f -> p c f", p=P)).then_inc(params_in, 16)
                ac.dma_start(wkv[:], w_ukv[lay]).then_inc(params_in, 16)
                ac.dma_start(wr[:], w_router[lay].rearrange("(c p) f -> p c f", p=P)).then_inc(params_in, 16)

                def copy_out(name, dst, src=None, scale=1.0, frees=True):
                    full(ac, name, lay)
                    ins = act(dst, B(name)[:, :] if src is None else src, ACT.Copy, scale=scale)
                    if frees:
                        ins.then_inc(freesem(name), 1)
                    return ins

                for j in range(2):
                    name = ("in", CF_G + j)
                    full(ac, name, lay)
                    act(mix[:, YC + j], B(name)[:, :], ACT.Tanh, scale=0.5).then_inc(freesem(name), 1)
                nc.scalar.preload_act_table_set("natural_log_exp_and_others")
                for j in range(2):
                    copy_out(("in", SC_C + j), scc[:, j])
                for j in range(2):
                    copy_out(("in", SC_H + j), prod[:, j, 1:1 + S])
                for j in range(2):
                    copy_out(("in", SC_B + j), mix[:, YB + j])
                copy_out(("in", KV), kvlat, frees=False)
                act(sq_kv, B(("in", KV))[:, :], ACT.Square).then_inc(freesem(("in", KV)), 1)
                copy_out(("in", GQK), gk)
                for j in range(2):
                    name = ("in", QLAT + j)
                    copy_out(name, qlat[:, j], frees=False)
                    act(sq_q[j], B(name)[:, :], ACT.Square).then_inc(freesem(name), 1)

                def inverse_root(name, dst, n, eps):
                    full(ac, name, lay)
                    act(dst, B(name)[:, :], ACT.Ln, scale=1.0 / n, bias=eps).then_inc(freesem(name), 1)
                    read_out(ac, name, lay)
                    act(dst, dst, ACT.Exp, scale=-0.5).then_inc(rnorm_ready, 1)

                inverse_root(("ssq", 0), r_kv, KV_RANK, c_rms)
                for j in range(2):
                    copy_out(("in", GQQ + j), gq[:, j], scale=GQ_SCALE)
                for j in range(2):
                    read_out(ac, ("mean",), lay)
                    act(csq[:, j], mix[:, YC + j], ACT.Square).then_inc(csq_ready, 1)
                inverse_root(("ssq", 1), r_q, Q_RANK, c_rms)
                copy_out(("in", GQV), gv[:].rearrange("p t f -> p (t f)"))
                copy_out(("in", KROPE), Kh[NOPE:QK, 0, :], B(("in", KROPE))[NOPE:QK, :])
                inverse_root(("var",), crs, CF_W, c_ln)
                nc.scalar.preload_act_table_set("exp_and_others")
                for h in range(MLA_H):
                    copy_out(("qup", h), Qh[0:QK, h, :], B(("qup", h))[0:QK, :], scale=MLA_SCALE)
                for j in range(2):
                    ac.wait_ge(z_ready, at(lay, 2, 2))
                    act(csq[:, j], mix[:, YC + j], ACT.Tanh).then_inc(th_ready, 1)
                for j in range(2):
                    for e in range(2):
                        copy_out(("kup", j), Kh[0:NOPE, 2 * j + e, :], B(("kup", j))[64 * e:64 * e + 64, :],
                                 frees=(e == 1))
                for j in range(2):
                    copy_out(("vup", j), V[:, 2 * j:2 * j + 2, :].rearrange("p t f -> p (t f)"))

                def d_exp(i):
                    n, h = divmod(i, GQ_H)
                    w = (min(n + 2, NT) - max(n - 1, 0)) * P
                    ac.wait_ge(dmax_ready, at(lay, NT * GQ_H, i + 1))
                    did(act(p_d[:, h, 0:w], p_d[:, h, 0:w], ACT.Exp, bias=nmx[:, i:i + 1], accum_out=rs[:, i:i + 1]))
                    c = PAR["sink"] + h
                    wait()
                    act(snk[:, i:i + 1], par[:, c:c + 1], ACT.Exp, bias=nmx[:, i:i + 1]).then_inc(dexp_done, 1)

                def d_turned(i):
                    n, h = divmod(i, GQ_H)
                    w = (min(n + 2, NT) - max(n - 1, 0)) * P
                    if i == 0:
                        ac.wait_ge(yc_ready, at(lay, 2, 2))
                        ac.wait_ge(yb_ready, at(lay, 2, 2))
                    if n > 0:
                        ac.wait_ge(pvd_done, at(lay, 2 * (NT - 1), 2 * (n - 1) + h // 2 + 1))
                    full(ac, ("TD", i), lay)
                    act(pt_d[:, h, 0:w], B(("TD", i))[:, 0:w], ACT.Copy).then_inc(freesem(("TD", i)), 1)

                d_exp(0)
                for i in range(NT * GQ_H):
                    if i + 1 < NT * GQ_H:
                        d_exp(i + 1)
                    d_turned(i)

                def a_exp(i):
                    if i < 3:
                        full(ac, ("TD", NT * GQ_H - 1), lay)
                    else:
                        full(ac, ("TA", i - 3), lay)
                    ac.wait_ge(amax_ready, at(lay, NT * MLA_H, i + 1))
                    act(p_a[:, i % 3], B(("SA", i))[:, :], ACT.Exp, bias=nmx[:, i:i + 1],
                        accum_out=rs[:, i:i + 1]).then_inc(freesem(("SA", i)), 1)

                def a_turned(i):
                    h, t = divmod(i, NT)
                    pt = (pt_a, pt_b)[h % 2]
                    if i == 0:
                        full(ac, ("YD", 0), lay)
                        full(ac, ("YD", 1), lay)
                    if h == 2:
                        ac.wait_ge(pva_done, at(lay, 2, 1))
                    if h == 3:
                        full(ac, ("YA", 0), lay)
                    full(ac, ("TA", i), lay)
                    act(pt[:, :, t * P:(t + 1) * P], B(("TA", i))[:, :].rearrange("p (c f) -> p c f", c=NT), ACT.Copy)\
                        .then_inc(freesem(("TA", i)), 1)

                a_exp(0)
                for i in range(NT * MLA_H):
                    if i + 1 < NT * MLA_H:
                        a_exp(i + 1)
                    a_turned(i)
                full(ac, ("YA", 1), lay)
                ac.dma_start(X[:], out.rearrange("(t p) f -> p t f", p=P)).then_inc(x_back, 16)

                def normalize(t, second):
                    k = 4 * second + t
                    ac.wait_ge(nmr_ready, at(lay, 2 * NT, k + 1))
                    act(X[:, t], X[:, t], ACT.Identity, scale=rstd[:, t:t + 1], bias=nmr[:, t:t + 1])\
                        .then_inc(normed, 1)

                def x1_turned(t):
                    ac.wait_ge(x1_ready, at(lay, NT, t + 1))
                    ac.dma_start(x1_rows[t * P:(t + 1) * P], X[:, t]).then_inc(x1_stored, 16)
                    for half in range(2):
                        name = ("x1T", t, half)
                        full(ac, name, lay)
                        act(x1T[:, 4 * half:4 * half + 4, t * P:(t + 1) * P],
                            B(name)[:, :].rearrange("p (c f) -> p c f", c=4), ACT.Copy).then_inc(freesem(name), 1)

                normalize(0, 0)
                normalize(1, 0)
                normalize(2, 0)
                x1_turned(0)
                normalize(3, 0)
                for t in range(1, NT):
                    x1_turned(t)
                ac.wait_ge(lsub_ready, at(lay, 1, 1))
                act(aff, aff, ACT.Exp).then_inc(lexp_done, 1)
                nc.scalar.preload_act_table(ACT.Silu)
                ac.wait_ge(x1_stored, at(lay, 16 * NT, 16 * NT))
                for t in range(NT):
                    act(X[:, t], X[:, t], ACT.Copy, scale=ALPHA).then_inc(y_init, 1)

                with ac.Fori(0, PAIRS // BODY_PAIRS) as body:
                    for b in range(BODY_PAIRS):
                        pair = body * BODY_PAIRS + b

                        def quarter_copies(kind, dst):
                            for half in range(2):
                                full(ac, (kind, half), lay, pair)
                                act(dst[:, 4 * half:4 * half + 4, :].rearrange("p c f -> p (c f)"),
                                    B((kind, half))[:, :], ACT.Copy).then_inc(freesem((kind, half)), 1)

                        quarter_copies("xsT", xsT)
                        for n in range(2):
                            full(ac, ("G", n), lay, pair)
                            act(hid[:, n * 512:(n + 1) * 512], B(("G", n))[:, :], ACT.Silu)\
                                .then_inc(freesem(("G", n)), 1)
                        quarter_copies("hT", hidT)
                        full(ac, ("O", 0), lay, pair)
                        act(o_sb[:, 0:512], B(("O", 0))[:, :], ACT.Copy).then_inc(freesem(("O", 0)), 1)

                for t in range(NT + 1):
                    if t < NT:
                        normalize(t, 1)
                    if t > 0:
                        ac.wait_ge(x_ready, at(lay, NT, NT + t))
                        ac.dma_start(out[(t - 1) * P:t * P], X[:, t - 1]).then_inc(x_stored, 16)
            ac.wait_ge(x_stored, 16 * NT * (DEPTH + 1))
            ac.wait_ge(x1_stored, 16 * NT * DEPTH)

        @block.gpsimd
        def _(g):
            step = Steps(g, pool_step)
            did, wait = step.did, step.wait
            tt = nc.gpsimd.tensor_tensor

            def hold(s, n):
                g.wait_ge(s, n)
                g.sem_inc(passed["pool"], 1)

            g.wait_ge(small_ready, 1)
            g.wait_ge(trig_ready, 2)

            def inverse_deviation(lay, t, second):
                hold(var_ready, at(lay, 2 * NT, 4 * second + t + 1))
                did(nc.gpsimd.tensor_scalar(rstd[:, t:t + 1], mv[:, t, 1:2], LN_EPS, None, ALU.add))
                wait()
                tt(rstd[:, t:t + 1], rstd[:, t:t + 1], half_neg, ALU.pow).then_inc(rstd_ready, 1)

            def apply_gain(lay, t, gains, second):
                hold(normed, at(lay, 2 * NT, 4 * second + t + 1))
                tt(X[:, t], X[:, t], gains[:, 0:D], ALU.mult).then_inc(gained, 1)

            with g.Fori(0, DEPTH) as lay:
                step.restart()
                for j in range(2):
                    hold(freesem(("in", SC_C + j)), bank_count(("in", SC_C + j), lay, 2, 0)[1])
                    hold(freesem(("in", SC_H + j)), bank_count(("in", SC_H + j), lay, 2, 0)[1])
                    tt(prod[:, j, 1:1 + S], prod[:, j, 1:1 + S], scc[:, j], ALU.mult).then_inc(prod_ready, 1)
                hold(sconv_ready, at(lay, 2, 2))
                for j in range(2):
                    hold(freesem(("in", SC_B + j)), bank_count(("in", SC_B + j), lay, 2, 0)[1])
                    tt(mix[:, YB + j], mix[:, YB + j], scc[:, j], ALU.mult).then_inc(yb_ready, 1)
                for j, buf in enumerate((gk, gq[:, 0], gq[:, 1])):
                    hold(freesem(("rotD", j)), bank_count(("rotD", j), lay, 2, 0)[1])
                    did(tt(buf, buf, cos_d[:], ALU.mult))
                    wait()
                    tt(buf, buf, tmp_d[:, j], ALU.add).then_inc(rope_d_ready, 1)
                r = slice(NOPE, QK)
                hold(rope_d_ready, at(lay, 3, 3))
                hold(fullsem(("rotK",)), bank_count(("rotK",), lay, 1, 0)[1])
                tt(Kh[r, 0, :], Kh[r, 0, :], cos_a[r, :], ALU.mult).then_inc(cos_a_done, 1)
                for h in range(MLA_H):
                    hold(fullsem(("rotQ", h)), bank_count(("rotQ", h), lay, 1, 0)[1])
                tt(Qh[r, :, :], Qh[r, :, :], cos_a[r, :].unsqueeze(1).broadcast_to([ROPE, MLA_H, S]), ALU.mult)\
                    .then_inc(cos_a_done, 1)

                hold(cos_a_done, at(lay, 2, 2))
                slot_in(g, lay, LN1_AT)
                g.sem_inc(passed["pool"], 1)
                for t in range(NT + 1):
                    if t < NT:
                        inverse_deviation(lay, t, 0)
                    if t > 0:
                        apply_gain(lay, t - 1, ring[:, LN1_AT], 0)

                hold(route_ready, at(lay, 1, 1))
                hold(x1_stored, at(lay, 16 * NT, 16 * NT))

                def gather(b, pair, count):
                    nc.gpsimd.tensor_copy(cur[:, b:b + 1], slot_i[:, bass.ds(pair, 1)]).then_inc(cur_ready, 1)
                    hold(cur_ready, count)
                    nc.gpsimd.indirect_dma_start(xs[:, b, :], None, x1_rows,
                                                 bass.IndirectOffsetOnAxis(ap=cur[:, b:b + 1], axis=0))\
                        .then_inc(xs_full[b], 16)

                for b in range(BODY_PAIRS):
                    gather(b, b, at(lay, PAIRS, b + 1))
                with g.Fori(1, PAIRS // BODY_PAIRS) as body:
                    for b in range(BODY_PAIRS):
                        bank, nth = USES[("xsT", 1)]
                        hold(bank_full[bank], lay * PER_LAYER[bank] + body * (BODY_PAIRS * PER_PAIR[bank])
                             + ((b - BODY_PAIRS) * PER_PAIR[bank] + nth + 1))
                        gather(b, body * BODY_PAIRS + b, lay * PAIRS + body * BODY_PAIRS + (b + 1))

                slot_in(g, lay, LN2_AT)
                g.sem_inc(passed["pool"], 1)
                for t in range(NT + 1):
                    if t < NT:
                        inverse_deviation(lay, t, 1)
                    if t > 0:
                        apply_gain(lay, t - 1, ring[:, LN2_AT % RING], 1)


def constants():
    c = np.zeros((P, N_CONST), np.float32)
    c[:, IDENT:IDENT + P] = np.eye(P, dtype=np.float32)
    c[:, ONES:ONES + P] = 1.0
    for at, block in ((ROT_A, ROPE), (ROT_D, GQ_D)):
        half = block // 2
        for m in range(P):
            first = m % block < half
            c[m + half if first else m - half, at + m] = -1.0 if first else 1.0
    i, j = np.arange(P)[:, None], np.arange(3 * P)[None, :]
    c[:, BAND:BAND + 3 * P] = np.where(np.abs(i - (j - P)) <= 128, 0.0, -1.0e30)
    inv = 1.0 / (np.float32(10000.0) ** (np.arange(0, GQ_D, 2, dtype=np.float32) / np.float32(GQ_D)))
    c[:, FREQ] = inv.astype(np.float32)[np.arange(P) % (GQ_D // 2)]
    iota = np.ascontiguousarray(np.broadcast_to(np.arange(S, dtype=np.int16), (P, S)))
    return c, iota


def lay_out(a):
    sizes = (256, 128, 32, 256, 256, 256, 256, 256, 256, 128, 128)
    ends = np.cumsum(sizes)
    q_lat, kv, k_rope, sc_b, sc_c, sc_h, cf_a, cf_g, gq_q, gq_k, gq_v = (
        np.arange(e - n, e) for e, n in zip(ends, sizes))
    gq_q = gq_q.reshape(GQ_H, GQ_D)[[0, 2, 1, 3]].ravel()
    order = np.concatenate([cf_g, cf_a, sc_c, sc_h, sc_b, kv, gq_k, q_lat, gq_q, gq_v, k_rope])
    w_in = np.zeros((DEPTH, D, IN_SLOTS * 256), np.float32)
    w_in[:, :, :len(order)] = a["w_in"][:, :, order]
    w_in = w_in.reshape(DEPTH, KD, P, IN_SLOTS, 256).transpose(0, 3, 2, 1, 4).reshape(DEPTH, IN_SLOTS, P, SLOT)
    ukv = a["w_ukv"].reshape(DEPTH, KV_RANK, MLA_H, 2, 64).transpose(0, 1, 3, 2, 4).reshape(DEPTH, KV_RANK, -1)

    def on_partitions(v):
        n = v.shape[-1] // P
        return v.reshape(DEPTH, -1, n, P).transpose(0, 3, 2, 1).reshape(DEPTH, P, -1)

    def every(v):
        return np.broadcast_to(v[:, None, :], (DEPTH, P, v.shape[-1]))

    par = np.concatenate([on_partitions(a[k]) for k in (
        "sconv_w", "cconv_w", "cconv_b", "cnorm_g", "cnorm_b", "q_norm_g", "kv_norm_g")]
        + [every(a["sink"]), every(a["b_router"])], axis=2)
    c, iota = constants()
    return {
        "x_in": a["x"].reshape(S, D), "positions": a["positions"].reshape(S), "w_in": w_in, "w_uq": a["w_uq"],
        "w_ukv": ukv, "w_router": a["w_router"], "params": par, "w_out": a["w_out"],
        "ln1": np.concatenate([a["ln1_g"], a["ln1_b"]], axis=1), "ln2": np.concatenate([a["ln2_g"], a["ln2_b"]], axis=1),
        "w_gate": a["w_gate"], "w_up": a["w_up"], "w_down": a["w_down"], "consts": c, "iota": iota,
    }


def kernel(**inputs):
    import concourse.bacc as bacc
    from concourse.bass_utils import run_bass_kernel_spmd

    nc = bacc.Bacc("TRN2", target_bir_lowering=False, num_devices=1)
    arrays = {k: np.ascontiguousarray(v) for k, v in lay_out({k: np.asarray(v) for k, v in inputs.items()}).items()}
    aps = {k: nc.dram_tensor(k, v.shape, mybir.dt.from_np(v.dtype), kind="ExternalInput").ap()
           for k, v in arrays.items()}
    out = nc.dram_tensor("out", (S, D), F32, kind="ExternalOutput").ap()
    trunk(nc, **aps, out=out)
    r = run_bass_kernel_spmd(nc, [arrays], core_ids=[0])
    return r.results[0]["out"].reshape(1, S, D)
```

```python
from contextlib import ExitStack

import concourse.bass as bass
import numpy as np
from concourse import mybir

F32 = mybir.dt.float32
I32 = mybir.dt.int32
I16 = mybir.dt.int16
U32 = mybir.dt.uint32
ALU = mybir.AluOpType
ACT = mybir.ActivationFunctionType
AX_X = mybir.AxisListType.X

P = 128
DEPTH, D, S = 2, 1024, 512
KD = D // P
NT = S // P
MLA_H, NOPE, ROPE, VD = 4, 64, 32, 64
QK = NOPE + ROPE
Q_RANK, KV_RANK = 256, 128
GQ_H, GQ_D = 4, 64
SC_K, CF_K, CF_W = 3, 31, 256
N_EXP, FF, CAP = 16, 1024, 64
PAIRS = N_EXP // 2
LN_EPS, RMS_EPS = 1e-5, 1e-6
ALPHA = (2 * DEPTH) ** 0.25
MLA_SCALE = float(QK) ** -0.5
GQ_SCALE = float(GQ_D) ** -0.5

CF_G, CF_A, SC_C, SC_H, SC_B, KV, GQK, QLAT, GQQ, GQV, KROPE = 0, 2, 4, 6, 8, 10, 11, 12, 14, 16, 17
N_IN = 18
IN_SLOTS = N_IN // 2

RING = 16
SLOT = 2 * FF
WOUT_AT = IN_SLOTS
LN1_AT = WOUT_AT + D // P // 2
MOE_AT = LN1_AT + 2
PAIR_CHUNKS = 3 * KD
LN2_AT = MOE_AT + PAIRS * PAIR_CHUNKS
CHUNKS = LN2_AT + 1
REVS = CHUNKS // RING
BODY_PAIRS = 2
assert CHUNKS % RING == 0 and BODY_PAIRS * PAIR_CHUNKS % RING == 0

PAR = {}
_at = 0
for _name, _n in (("sconv", 2 * SC_K), ("cconv", 2 * CF_K), ("cconv_b", 2), ("cnorm_g", 2), ("cnorm_b", 2),
                  ("q_g", 2), ("kv_g", 1), ("sink", GQ_H), ("b_router", N_EXP)):
    PAR[_name] = _at
    _at += _n
N_PAR = _at

IDENT, ONES, ROT_A, ROT_D, BAND, FREQ = 0, P, 2 * P, 3 * P, 4 * P, 4 * P + 3 * P
N_CONST = FREQ + 1
TWO_PI_1 = 6.28125
TWO_PI_2 = float(np.float32(np.floor((2 * np.pi - TWO_PI_1) * 2**20) / 2**20))
TWO_PI_3 = float(np.float32(2 * np.pi - TWO_PI_1 - TWO_PI_2))
ROUND = 1.5 * 2.0**23
PI_BELOW = 3.1415925


def bank_uses():
    order = []
    for t in range(NT):
        for half in range(2):
            order.append((("xT", t, half), 4 + (2 * t + half) % 4))
    for i in range(N_IN):
        order.append((("in", i), i % 4))
        if i == QLAT + 1:
            order += [(("ssq", 0), 4), (("mean",), 6), (("rotD", 0), 7)]
        if i == GQQ + 1:
            order += [(("ssq", 1), 5)]
        if i == GQV:
            order += [(("rotD", 1), 4), (("rotD", 2), 6)]
    order.append((("var",), 7))
    order += [(("qup", h), 4 + h) for h in range(MLA_H)]
    order += [(("kup", 0), 4), (("kup", 1), 5), (("vup", 0), 6), (("vup", 1), 7)]
    order += [(("rotQ", h), (7, 4, 5, 6)[h]) for h in range(MLA_H)] + [(("rotK",), 2)]
    order += [(("YD", 0), 5), (("YD", 1), 6)]
    for i in range(NT * GQ_H):
        order += [(("SD", i), (0, 1, 4, 7)[i % 4]), (("TD", i), 2 + i % 2)]
    order += [(("YA", 0), 4), (("YA", 1), 7)]
    for i in range(NT * MLA_H):
        order += [(("SA", i), (0, 1, 5, 6)[i % 4]), (("TA", i), 2 + i % 2)]
    for t in range(NT):
        order += [(("mix", t, n), (2 * t + n) % 4) for n in range(2)]
        order += [(("x1T", t, half), 4 + half) for half in range(2)]
    order += [(("logits",), 6), (("affT",), 7), (("slotT",), 6)]
    place, count = {}, [0] * 8
    for name, bank in order:
        place[name] = (bank, count[bank])
        count[bank] += 1
    first = list(count)
    pair = [(("xsT", half), 6 + half) for half in range(2)]
    pair += [(("G", n), n) for n in range(2)] + [(("U", n), 2 + n) for n in range(2)]
    pair += [(("hT", half), 6 + half) for half in range(2)]
    pair += [(("O", n), 4 + n) for n in range(2)]
    pair += [(("Y", t, n), 6 + n) for t in range(NT) for n in range(2)]
    for name, bank in pair:
        place[name] = (bank, count[bank])
        count[bank] += 1
    per_pair = [c - f for c, f in zip(count, first)]
    total = [f + PAIRS * q for f, q in zip(first, per_pair)]
    return place, per_pair, total


USES, PER_PAIR, PER_LAYER = bank_uses()


def trunk(nc, x_in, positions, w_in, w_uq, w_ukv, w_router, params, w_out, ln1, ln2, w_gate, w_up, w_down,
          consts, iota, out):
    x1_rows = nc.dram_tensor("x1_rows", (S, D), F32, kind="Internal").ap()

    with ExitStack() as ctx:
        def sb(name, shape, dt=F32):
            return ctx.enter_context(nc.sbuf_tensor(name, shape, dt))

        def sem(name):
            return ctx.enter_context(nc.semaphore(name))

        ring = sb("ring", [P, RING, SLOT])
        cst = sb("cst", [P, N_CONST])
        slot_iota = sb("slot_iota", [P, S], I16)
        cos_a, sin_a, cos_d, sin_d = (sb(n, [P, S]) for n in ("cos_a", "sin_a", "cos_d", "sin_d"))
        par = sb("par", [P, N_PAR])
        wq = sb("wq", [P, 2, MLA_H * QK])
        wkv = sb("wkv", [P, MLA_H * (NOPE + VD)])
        wr = sb("wr", [P, KD, N_EXP])
        X = sb("X", [P, NT, D])
        work = sb("work", [P, 11 * 1024])
        stat = sb("stat", [P, 216])
        cur = sb("cur", [P, 2], I32)
        slot_i = sb("slot_i", [P, PAIRS], I32)

        ident = cst[:, IDENT:IDENT + P]
        ones = cst[:, ONES:ONES + P]
        rot_a = cst[:, ROT_A:ROT_A + P]
        rot_d = cst[:, ROT_D:ROT_D + P]
        band = cst[:, BAND:BAND + 3 * P]
        freq = cst[:, FREQ:FREQ + 1]

        def view(flat, at, *shape):
            n = int(np.prod(shape))
            v = flat[:, at:at + n]
            if len(shape) == 2:
                v = v.rearrange("p (a b) -> p a b", b=shape[1])
            return v

        Xf = X[:].rearrange("p t f -> p (t f)")
        u = view(Xf, 0, 2, S + CF_K - 1)
        scc = view(Xf, 1084, 2, S)
        prod = view(Xf, 2108, 2, S + SC_K - 1)
        gv = view(Xf, 3584, NT, 2 * GQ_D)
        csq = view(Xf, 0, 2, S)
        crs = view(Xf, 0, S)
        pt_a = view(Xf, 0, 4, S)
        pt_d = view(Xf, 0, GQ_H, 3 * P)
        p_d = view(Xf, 2048, GQ_H, 3 * P)
        p_a = view(Xf, 2048, 4, S)
        tmp_d = view(Xf, 2048, 3, S)
        xT = view(work, 0, KD, S)
        Qh = view(work, 0, MLA_H, S)
        Kh = view(work, 2048, MLA_H, S)
        mix = view(work, 4096, 8, S)
        YA, YB, YC, YD = 0, 2, 4, 6
        qlat = view(work, 8192, 2, S)
        V = view(work, 8192, NT, MLA_H * VD)
        kvlat = view(work, 9216, S)
        gq = view(work, 9728, 2, S)
        gk = view(work, 10752, S)
        sq_kv, sq_q, r_kv, r_q = mix[:, YA], (mix[:, YA + 1], mix[:, YD]), mix[:, YD + 1], mix[:, YA]
        x1T = view(work, 0, KD, S)
        xs = view(work, 4096, 2, D)
        xsT = view(work, 6144, KD, P)
        hid = view(work, 7168, FF)
        hidT = view(work, 8192, KD, P)
        o_sb = view(work, 9216, D)
        G = view(work, 10240, S)
        aff2 = view(work, 10240, 2, S)
        vals = view(work, 7168, 2, CAP)
        slotf = view(work, 7168 + 128, 2, CAP)
        idx = view(work, 7168 + 256, CAP).bitcast(U32)
        trig = view(work, 4096, 6, S)

        bn = stat[:, 0:48].rearrange("p (t k) -> p t k", k=12)
        mv = stat[:, 48:56].rearrange("p (t k) -> p t k", k=2)
        rstd = stat[:, 56:60]
        mx, nmx, rs, rinv = (stat[:, 64 + 16 * i:80 + 16 * i] for i in range(4))
        snk = stat[:, 128:144]
        halfgb = stat[:, 144:148]
        half_neg = stat[:, 148:149]
        lmax, lsum = stat[:, 152:156], stat[:, 156:160]
        slot_f = stat[:, 160:168]
        slot_gate = stat[:, 168:176]
        c_rms, c_ln = stat[:, 176:177], stat[:, 177:178]
        aff = view(work, 7168 + 384, NT, N_EXP)

        banks = [ctx.enter_context(nc.psum_tensor(f"bank{i}", [P, 512], F32)) for i in range(8)]

        slot_full = [sem(f"slot_full{i}") for i in range(RING)]
        chunk_free = sem("chunk_free")
        bank_full = [sem(f"bank_full{i}") for i in range(8)]
        bank_free = [sem(f"bank_free{i}") for i in range(8)]
        consts_in, x_in_sem, pos_in = sem("consts_in"), sem("x_in_sem"), sem("pos_in")
        params_in = sem("params_in")
        small_ready = sem("small_ready")
        x_ready, x_stored, x_back = sem("x_ready"), sem("x_stored"), sem("x_back")
        angles_ready, sines_ready, trig_ready = sem("angles_ready"), sem("sines_ready"), sem("trig_ready")
        prod_ready, sconv_ready, yb_ready = sem("prod_ready"), sem("sconv_ready"), sem("yb_ready")
        cconv_ready, cdev_ready, csq_ready = sem("cconv_ready"), sem("cdev_ready"), sem("csq_ready")
        rnorm_ready, lat_ready, z_ready, th_ready, yc_ready = (
            sem(n) for n in ("rnorm_ready", "lat_ready", "z_ready", "th_ready", "yc_ready"))
        rot_d_out, rope_d_ready = sem("rot_d_out"), sem("rope_d_ready")
        cos_a_done, rope_a_ready = sem("cos_a_done"), sem("rope_a_ready")
        dmax_ready, dexp_done, dp_ready, pvd_done = (
            sem(n) for n in ("dmax_ready", "dexp_done", "dp_ready", "pvd_done"))
        amax_ready, ap_ready, pva_done = sem("amax_ready"), sem("ap_ready"), sem("pva_done")
        var_ready, rstd_ready = sem("var_ready"), sem("rstd_ready")
        x1_ready, x1_stored, y_init = sem("x1_ready"), sem("x1_stored"), sem("y_init")
        lsub_ready, lexp_done, aff_ready, slots_ready, route_ready = (
            sem(n) for n in ("lsub_ready", "lexp_done", "aff_ready", "slots_ready", "route_ready"))
        cur_ready = sem("cur_ready")
        xs_full = [sem(f"xs_full{i}") for i in range(2)]
        g_ready = sem("g_ready")
        dve_step, act_step, pool_step = sem("dve_step"), sem("act_step"), sem("pool_step")
        passed = {e: sem(f"passed_{e}") for e in ("dve", "act", "pool", "pe")}

        def at(lay, per_layer, n):
            return lay * per_layer + n

        def bank_count(name, lay, more, pair):
            bank, nth = USES[name]
            if isinstance(pair, int) and pair == 0:
                return bank, lay * PER_LAYER[bank] + (nth + more)
            return bank, lay * PER_LAYER[bank] + pair * PER_PAIR[bank] + (nth + more)


        def full(eng, name, lay, pair=0):
            bank, n = bank_count(name, lay, 1, pair)
            eng.wait_ge(bank_full[bank], n)

        def read_out(eng, name, lay, pair=0):
            bank, n = bank_count(name, lay, 2, pair)
            eng.wait_ge(bank_free[bank], n)

        def before(eng, name, lay, pair=0):
            bank, n = bank_count(name, lay, 1, pair)
            eng.wait_ge(bank_free[bank], n)

        def B(name):
            return banks[USES[name][0]]

        def fullsem(name):
            return bank_full[USES[name][0]]

        def freesem(name):
            return bank_free[USES[name][0]]

        class Steps:

            def __init__(self, eng, s):
                self.eng, self.sem, self.n = eng, s, 0

            def did(self, ins):
                ins.then_inc(self.sem, 1)
                self.n += 1

            def wait(self):
                self.eng.wait_ge(self.sem, self.n)

            def restart(self):
                self.eng.drain()
                self.eng.sem_clear(self.sem)
                self.n = 0

        block = ctx.enter_context(nc.Block())

        @block.sync
        def _(sp):
            sp.dma_start(cst[:], consts).then_inc(consts_in, 16)
            sp.dma_start(slot_iota[:], iota).then_inc(consts_in, 16)

            with sp.Fori(0, DEPTH) as lay:
                for n in range(LN1_AT + 1):
                    sp.wait_ge(chunk_free, at(lay, CHUNKS, n + 1))
                    if n < WOUT_AT:
                        src, dst = w_in[lay, n], ring[:, n]
                    elif n < LN1_AT:
                        k = 2 * (n - WOUT_AT)
                        src = w_out[lay, k * P:(k + 2) * P].rearrange("(c p) f -> p c f", p=P)
                        dst = ring[:, n].rearrange("p (c f) -> p c f", c=2)
                    else:
                        src, dst = ln1[lay].partition_broadcast(P), ring[:, n]
                    sp.dma_start(dst, src).then_inc(slot_full[n], 16)
                with sp.Fori(0, PAIRS // BODY_PAIRS) as body:
                    for j in range(BODY_PAIRS * PAIR_CHUNKS):
                        pair, part, k = j // PAIR_CHUNKS, j % PAIR_CHUNKS // KD, j % KD
                        w = (w_gate, w_up, w_down)[part]
                        slot = (MOE_AT + j) % RING
                        sp.wait_ge(chunk_free, lay * CHUNKS + body * (BODY_PAIRS * PAIR_CHUNKS) + (MOE_AT + j + 1))
                        src = w[lay, bass.ds(body * (2 * BODY_PAIRS) + 2 * pair, 2), k * P:(k + 1) * P]
                        sp.dma_start(ring[:, slot].rearrange("p (e f) -> p e f", e=2),
                                     src.rearrange("e p f -> p e f")).then_inc(slot_full[slot], 16)
                sp.wait_ge(chunk_free, at(lay, CHUNKS, LN2_AT + 1))
                sp.dma_start(ring[:, LN2_AT % RING], ln2[lay].partition_broadcast(P))\
                    .then_inc(slot_full[LN2_AT % RING], 16)

        def slot_in(eng, lay, n, body=0):
            slot = n % RING
            less = 1 if slot == LN1_AT + 1 else 0
            count = lay * (16 * (REVS - less)) + 16 * (n // RING + 1 - less)
            if not isinstance(body, int):
                count = count + body * (16 * BODY_PAIRS * PAIR_CHUNKS // RING)
            eng.wait_ge(slot_full[slot], count)

        @block.tensor
        def _(pe):
            mm = nc.tensor.matmul

            def transposed(name, lay, src, n_blocks, pair=0, retire=0):
                before(pe, name, lay, pair)
                for c in range(n_blocks):
                    ins = nc.tensor.transpose(B(name)[:, c * P:(c + 1) * P], src[:, c * P:(c + 1) * P], ident)
                    if c == 0 and retire:
                        ins.then_inc(chunk_free, retire)
                ins.then_inc(fullsem(name), 1)

            pe.wait_ge(consts_in, 32)
            pe.wait_ge(x_in_sem, 16 * NT)
            pe.sem_inc(x_ready, 2 * NT)
            pe.sem_inc(chunk_free, RING - 1)
            for free in bank_free:
                pe.sem_inc(free, 1)
            with pe.Fori(0, DEPTH) as lay:
                for t in range(NT):
                    for half in range(2):
                        pe.wait_ge(x_ready, at(lay, 2 * NT, 2 * t + half + 1))
                        transposed(("xT", t, half), lay, X[:, t, half * 512:half * 512 + 512], 4,
                                   retire=1 if (t, half) == (NT - 1, 1) else 0)

                for i in range(N_IN):
                    n, fc = i // 2, i % 2
                    name = ("in", i)
                    if fc == 0:
                        slot_in(pe, lay, n)
                    if i == 0:
                        for t in range(NT):
                            for half in range(2):
                                read_out(pe, ("xT", t, half), lay)
                    before(pe, name, lay)
                    w = ring[:, n].rearrange("p (c f) -> p c f", c=KD)
                    if i == GQV:
                        for t in range(NT):
                            for k in range(KD):
                                ins = mm(B(name)[:, t * P:(t + 1) * P], xT[:, k, t * P:(t + 1) * P],
                                         w[:, k, 0:P], start=(k == 0), stop=(k == KD - 1))
                                if t == 0 and k == 0:
                                    ins.then_inc(chunk_free, 1)
                    else:
                        lo, m, to = (fc * P, P, 0) if i != KROPE else (fc * P, ROPE, NOPE)
                        for k in range(KD):
                            ins = mm(B(name)[to:to + m, :], w[:, k, lo:lo + m], xT[:, k, :],
                                     start=(k == 0), stop=(k == KD - 1))
                            if fc == 0 and k == 0 and i > 0:
                                ins.then_inc(chunk_free, 1)
                    ins.then_inc(fullsem(name), 1)

                    if i == QLAT + 1:
                        read_out(pe, ("in", KV), lay)
                        before(pe, ("ssq", 0), lay)
                        mm(B(("ssq", 0))[:, :], ones, sq_kv, start=True, stop=True).then_inc(fullsem(("ssq", 0)), 1)
                        pe.wait_ge(cconv_ready, at(lay, 2, 2))
                        before(pe, ("mean",), lay)
                        mm(B(("mean",))[:, :], ones, mix[:, YC], start=True, stop=False)
                        mm(B(("mean",))[:, :], ones, mix[:, YC + 1], start=False, stop=True)\
                            .then_inc(fullsem(("mean",)), 1)
                        read_out(pe, ("in", GQK), lay)
                        before(pe, ("rotD", 0), lay)
                        mm(B(("rotD", 0))[:, :], rot_d, gk, start=True, stop=True).then_inc(fullsem(("rotD", 0)), 1)
                    if i == GQQ + 1:
                        read_out(pe, ("in", QLAT), lay)
                        read_out(pe, ("in", QLAT + 1), lay)
                        before(pe, ("ssq", 1), lay)
                        mm(B(("ssq", 1))[:, :], ones, sq_q[0], start=True, stop=False)
                        mm(B(("ssq", 1))[:, :], ones, sq_q[1], start=False, stop=True)\
                            .then_inc(fullsem(("ssq", 1)), 1)
                    if i == GQV:
                        for j in range(2):
                            name = ("rotD", 1 + j)
                            read_out(pe, ("in", GQQ + j), lay)
                            before(pe, name, lay)
                            mm(B(name)[:, :], rot_d, gq[:, j], start=True, stop=True).then_inc(fullsem(name), 1)

                pe.wait_ge(csq_ready, at(lay, 2, 2))
                before(pe, ("var",), lay)
                mm(B(("var",))[:, :], ones, csq[:, 0], start=True, stop=False).then_inc(chunk_free, 1)
                mm(B(("var",))[:, :], ones, csq[:, 1], start=False, stop=True).then_inc(fullsem(("var",)), 1)

                def window(n):
                    return max(n - 1, 0), min(n + 2, NT)

                def d_scores(i):
                    n, h = divmod(i, GQ_H)
                    lo, hi = window(n)
                    rows = slice(64 * (h // 2), 64 * (h // 2) + 64)
                    before(pe, ("SD", i), lay)
                    mm(B(("SD", i))[:, 0:(hi - lo) * P], gq[rows, h % 2, n * P:(n + 1) * P],
                       gk[rows, lo * P:hi * P], start=True, stop=True).then_inc(fullsem(("SD", i)), 1)

                pe.wait_ge(params_in, at(lay, 64, 64))
                pe.wait_ge(lat_ready, at(lay, 3, 3))
                for h in range(MLA_H):
                    name = ("qup", h)
                    before(pe, name, lay)
                    for k in range(2):
                        ins = mm(B(name)[0:QK, :], wq[:, k, h * QK:(h + 1) * QK], qlat[:, k],
                                 start=(k == 0), stop=(k == 1))
                    ins.then_inc(fullsem(name), 1)
                for j in range(2):
                    name = ("kup", j)
                    before(pe, name, lay)
                    for e in range(2):
                        h = 2 * j + e
                        ins = mm(B(name)[e * NOPE:(e + 1) * NOPE, :], wkv[:, h * NOPE:(h + 1) * NOPE], kvlat,
                                 start=True, stop=True)
                    ins.then_inc(fullsem(name), 1)
                for j in range(2):
                    name = ("vup", j)
                    before(pe, name, lay)
                    for e in range(2):
                        t = 2 * j + e
                        ins = mm(B(name)[:, e * 256:(e + 1) * 256], kvlat[:, t * P:(t + 1) * P],
                                 wkv[:, MLA_H * NOPE:], start=True, stop=True)
                    ins.then_inc(fullsem(name), 1)
                pe.wait_ge(rope_d_ready, at(lay, 3, 3))
                d_scores(0)
                d_scores(1)
                r = slice(NOPE, QK)
                for h in range(MLA_H):
                    name = ("rotQ", h)
                    read_out(pe, ("qup", h), lay)
                    before(pe, name, lay)
                    pe.sem_inc(passed["pe"], 1)
                    mm(B(name)[r, :], rot_a[r, r], Qh[r, h, :], start=True, stop=True).then_inc(fullsem(name), 1)
                read_out(pe, ("in", KROPE), lay)
                before(pe, ("rotK",), lay)
                pe.sem_inc(passed["pe"], 1)
                mm(B(("rotK",))[r, :], rot_a[r, r], Kh[r, 0, :], start=True, stop=True).then_inc(fullsem(("rotK",)), 1)

                def d_values(n, j):
                    lo, hi = window(n)
                    if n == 0:
                        before(pe, ("YD", j), lay)
                    for e in range(2):
                        read_out(pe, ("TD", n * GQ_H + 2 * j + e), lay)
                    for kb in range(hi - lo):
                        for e in range(2):
                            h = 2 * j + e
                            ins = mm(B(("YD", j))[64 * e:64 * e + 64, n * P:(n + 1) * P],
                                     gv[:, lo + kb, 64 * j:64 * j + 64], pt_d[:, h, kb * P:(kb + 1) * P],
                                     start=(kb == 0), stop=(kb == hi - lo - 1))
                    ins.then_inc(pvd_done if n < NT - 1 else fullsem(("YD", j)), 1)

                read_out(pe, ("in", GQV), lay)
                def a_scores(i):
                    h, t = 2 * (i // 8) + i % 2, i // 2 % NT
                    before(pe, ("SA", i), lay)
                    mm(B(("SA", i))[:, :], Qh[0:QK, h, t * P:(t + 1) * P], Kh[0:QK, h, :], start=True, stop=True)\
                        .then_inc(fullsem(("SA", i)), 1)

                for i in range(NT * GQ_H):
                    n, h = divmod(i, GQ_H)
                    lo, hi = window(n)
                    pe.wait_ge(dp_ready, at(lay, NT * GQ_H, i + 1))
                    before(pe, ("TD", i), lay)
                    for kb in range(hi - lo):
                        ins = nc.tensor.transpose(B(("TD", i))[:, kb * P:(kb + 1) * P],
                                                  p_d[:, h, kb * P:(kb + 1) * P], ident)
                    ins.then_inc(fullsem(("TD", i)), 1)
                    if i + 4 < NT * GQ_H:
                        for later in ((2, 3, 4) if i == 0 else (i + 4,)):
                            d_scores(later)
                    elif i + 4 == NT * GQ_H:
                        pe.wait_ge(rope_a_ready, at(lay, 5, 5))
                        for j in range(MLA_H // 2):
                            read_out(pe, ("kup", j), lay)
                        a_scores(0)
                    elif i + 4 == NT * GQ_H + 1:
                        a_scores(1)
                    if h % 2 == 0 and i > 0:
                        d_values((i - 1) // GQ_H, (i - 1) % GQ_H // 2)

                def a_values(j, t):
                    if t == 0:
                        if j == 0:
                            read_out(pe, ("vup", 0), lay)
                            read_out(pe, ("vup", 1), lay)
                        before(pe, ("YA", j), lay)
                    for e in range(2):
                        read_out(pe, ("TA", 8 * j + 2 * t + e), lay)
                    for k in range(NT):
                        for e in range(2):
                            h = 2 * j + e
                            ins = mm(B(("YA", j))[64 * e:64 * e + 64, t * P:(t + 1) * P],
                                     V[:, k, h * VD:(h + 1) * VD], pt_a[:, (2 * t + e) % 4, k * P:(k + 1) * P],
                                     start=(k == 0), stop=(k == NT - 1))
                    ins.then_inc(pva_done if t < NT - 1 else fullsem(("YA", j)), 1)

                d_values(NT - 1, 1)
                for i in range(NT * MLA_H):
                    pe.wait_ge(ap_ready, at(lay, NT * MLA_H, i + 1))
                    before(pe, ("TA", i), lay)
                    for k in range(NT):
                        ins = nc.tensor.transpose(B(("TA", i))[:, k * P:(k + 1) * P],
                                                  p_a[:, i % 4, k * P:(k + 1) * P], ident)
                    ins.then_inc(fullsem(("TA", i)), 1)
                    for later in ((2, 3, 4) if i == 0 else (i + 4,)):
                        if later < NT * MLA_H:
                            a_scores(later)
                    if i % 2 == 0 and i > 0:
                        a_values((i - 2) // 8, (i - 2) // 2 % NT)
                a_values(1, NT - 1)

                def router(t, retire=0):
                    for half in range(2):
                        pe.wait_ge(x1_ready, at(lay, 2 * NT, 2 * t + half + 1))
                        transposed(("x1T", t, half), lay, X[:, t, half * 512:half * 512 + 512], 4,
                                   retire=retire if half == 1 else 0)
                    for k in range(KD):
                        if k % 4 == 0:
                            read_out(pe, ("x1T", t, k // 4), lay)
                        ins = mm(B(("logits",))[:, t * N_EXP:(t + 1) * N_EXP], x1T[:, k, t * P:(t + 1) * P],
                                 wr[:, k, :], start=(k == 0), stop=(k == KD - 1))
                    return ins

                pe.wait_ge(yb_ready, at(lay, 2, 2))
                pe.wait_ge(yc_ready, at(lay, 2, 2))
                read_out(pe, ("YD", 0), lay)
                read_out(pe, ("YD", 1), lay)
                read_out(pe, ("YA", 0), lay)
                read_out(pe, ("YA", 1), lay)
                before(pe, ("logits",), lay)
                for t in range(NT):
                    for n in range(2):
                        name = ("mix", t, n)
                        before(pe, name, lay)
                        for k in (4, 5, 2, 3, 6, 7, 0, 1):
                            if t == 0 and n == 0 and k % 2 == 0:
                                slot_in(pe, lay, WOUT_AT + k // 2)
                            w = ring[:, WOUT_AT + k // 2].rearrange("p (c f) -> p c f", c=2)
                            ins = mm(B(name)[:, :], mix[:, k, t * P:(t + 1) * P], w[:, k % 2, n * 512:(n + 1) * 512],
                                     start=(k == 4), stop=(k == 1))
                        ins.then_inc(fullsem(name), 1)
                    if t >= 1:
                        router(t - 1, retire=4 if t == NT - 1 else 0)
                router(NT - 1, retire=2).then_inc(fullsem(("logits",)), 1)

                pe.wait_ge(aff_ready, at(lay, 1, 1))
                before(pe, ("affT",), lay)
                for t in range(NT):
                    ins = nc.tensor.transpose(B(("affT",))[0:N_EXP, t * P:(t + 1) * P], aff[:, t, :], ident)
                ins.then_inc(fullsem(("affT",)), 1)
                pe.wait_ge(slots_ready, at(lay, 1, 1))
                before(pe, ("slotT",), lay)
                pe.sem_inc(passed["pe"], 1)
                for c, src in enumerate((slotf, vals)):
                    ins = nc.tensor.transpose(B(("slotT",))[:, c * N_EXP:(c + 1) * N_EXP],
                                              src[0:N_EXP].rearrange("p a b -> p (a b)"), ident[0:N_EXP, 0:N_EXP])
                ins.then_inc(fullsem(("slotT",)), 1)

                with pe.Fori(0, PAIRS // BODY_PAIRS) as body:
                    for b in range(BODY_PAIRS):
                        pair = body * BODY_PAIRS + b
                        at0 = MOE_AT + b * PAIR_CHUNKS
                        pe.wait_ge(xs_full[b], lay * (16 * PAIRS // 2) + body * 16 + 16)
                        for half in range(2):
                            transposed(("xsT", half), lay, xs[:, b, half * 512:half * 512 + 512], 4, pair)
                        for half in range(2):
                            read_out(pe, ("xsT", half), lay, pair)
                        for part, kind in enumerate("GU"):
                            for n in range(2):
                                before(pe, (kind, n), lay, pair)
                            for k in range(KD):
                                j = at0 + part * KD + k
                                slot_in(pe, lay, j, body)
                                w = ring[:, j % RING].rearrange("p (e f) -> p e f", e=2)
                                for n in range(2):
                                    for e in range(2):
                                        ins = mm(B((kind, n))[64 * e:64 * e + 64, :], xsT[:, k, 64 * e:64 * e + 64],
                                                 w[:, e, n * 512:(n + 1) * 512], start=(k == 0), stop=(k == KD - 1))
                                        if n == 0 and e == 0 and part + k > 0:
                                            ins.then_inc(chunk_free, 1)
                                    if k == KD - 1:
                                        ins.then_inc(fullsem((kind, n)), 1)
                        for half in range(2):
                            read_out(pe, ("U", half), lay, pair)
                            transposed(("hT", half), lay, hid[:, half * 512:half * 512 + 512], 4, pair,
                                       retire=1 if half == 0 else 0)
                        for half in range(2):
                            read_out(pe, ("hT", half), lay, pair)
                        for n in range(2):
                            before(pe, ("O", n), lay, pair)
                        for k in range(KD):
                            j = at0 + 2 * KD + k
                            slot_in(pe, lay, j, body)
                            w = ring[:, j % RING].rearrange("p (e f) -> p e f", e=2)
                            for n in range(2):
                                for e in range(2):
                                    ins = mm(B(("O", n))[64 * e:64 * e + 64, :], hidT[:, k, 64 * e:64 * e + 64],
                                             w[:, e, n * 512:(n + 1) * 512], start=(k == 0), stop=(k == KD - 1))
                                    if n == 0 and e == 0 and k > 0:
                                        ins.then_inc(chunk_free, 1)
                                if k == KD - 1:
                                    ins.then_inc(fullsem(("O", n)), 1)
                        pe.wait_ge(g_ready, lay * PAIRS + body * BODY_PAIRS + (b + 1))
                        for n in range(2):
                            read_out(pe, ("O", n), lay, pair)
                        for t in range(NT):
                            for n in range(2):
                                name = ("Y", t, n)
                                bank, nth = USES[name]
                                before(pe, name, lay, pair)
                                ins = mm(banks[bank][:, :], G[:, t * P:(t + 1) * P], o_sb[:, n * 512:(n + 1) * 512],
                                         start=True, stop=True)
                                if t == 0 and n == 0:
                                    ins.then_inc(bank_full[bank], 1)
                                elif t == 0 and n == 1:
                                    ins.then_inc(bank_full[bank], 1)
                                else:
                                    ins.then_inc(bank_full[bank], 1)
                        pe.wait_ge(bank_full[USES[("Y", 0, 0)][0]],
                                   bank_count(("Y", 0, 0), lay, 1, pair)[1])
                        pe.sem_inc(chunk_free, 1)

        @block.vector
        def _(v):
            step = Steps(v, dve_step)
            did, wait = step.did, step.wait

            def hold(s, n):
                v.wait_ge(s, n)
                v.sem_inc(passed["dve"], 1)

            nc.vector.memset(half_neg, -0.5)
            nc.vector.memset(c_rms, RMS_EPS)
            nc.vector.memset(c_ln, LN_EPS).then_inc(small_ready, 1)

            v.wait_ge(pos_in, 16)
            v.wait_ge(consts_in, 32)
            pos, ang, turns = trig[:, 0], trig[:, 1], trig[:, 2]
            sin_arg, cos_arg = trig[:, 3], trig[:, 4]
            did(nc.vector.tensor_copy(pos, trig[:, 5].bitcast(I32)))
            wait()
            did(nc.vector.tensor_scalar(ang, pos, freq, None, ALU.mult))
            wait()
            for arg, quarter in ((sin_arg, 0.0), (cos_arg, 0.25)):
                did(nc.vector.tensor_scalar(turns, ang, float(1 / (2 * np.pi)), quarter, ALU.mult, ALU.add))
                wait()
                did(nc.vector.tensor_scalar(turns, turns, ROUND, None, ALU.add))
                wait()
                did(nc.vector.tensor_scalar(turns, turns, ROUND, None, ALU.subtract))
                wait()
                src = ang
                for c in (TWO_PI_1, TWO_PI_2, TWO_PI_3):
                    did(nc.vector.scalar_tensor_tensor(out=arg, in0=turns, scalar=-c, in1=src,
                                                       op0=ALU.mult, op1=ALU.add))
                    wait()
                    src = arg
                did(nc.vector.tensor_scalar(arg, arg, 2 * np.pi * quarter, PI_BELOW, ALU.add, ALU.min))
                wait()
                nc.vector.tensor_scalar(arg, arg, -PI_BELOW, None, ALU.max).then_inc(angles_ready, 1)
                wait()
            v.wait_ge(sines_ready, 2)
            every_second = [2 * (i % 16) for i in range(32)]
            nc.vector.stream_shuffle(sin_a[:], sin_d[:], every_second).then_inc(trig_ready, 1)
            nc.vector.stream_shuffle(cos_a[:], cos_d[:], every_second).then_inc(trig_ready, 1)
            v.wait_ge(trig_ready, 2)

            def half_stats(t, n):
                did(nc.vector.bn_stats(bn[:, t, 6 * n:6 * n + 6], X[:, t, n * 512:(n + 1) * 512]))

            def layer_norm(lay, t, gains, second, done):
                k = 4 * second + t
                wait()
                nc.vector.bn_aggr(mv[:, t, :], bn[:, t, :]).then_inc(var_ready, 1)
                v.wait_ge(var_ready, at(lay, 2 * NT, k + 1))
                for n in range(2):
                    cols = slice(n * 512, (n + 1) * 512)
                    did(nc.vector.scalar_tensor_tensor(out=X[:, t, cols], in0=X[:, t, cols], scalar=mv[:, t, 0:1],
                                                       in1=gains[:, cols], op0=ALU.subtract, op1=ALU.mult))
                hold(rstd_ready, at(lay, 2 * NT, k + 1))
                for n in range(2):
                    cols = slice(n * 512, (n + 1) * 512)
                    v.wait_ge(dve_step, step.n - 1 + n)
                    nc.vector.scalar_tensor_tensor(out=X[:, t, cols], in0=X[:, t, cols], scalar=rstd[:, t:t + 1],
                                                   in1=gains[:, D + n * 512:D + (n + 1) * 512],
                                                   op0=ALU.mult, op1=ALU.add).then_inc(done, 1)

            with v.Fori(0, DEPTH) as lay:
                step.restart()
                hold(x_stored, at(lay, 16 * NT, 16 * NT))
                full(v, ("in", 0), lay)
                v.sem_inc(passed["dve"], 1)
                pad = CF_K // 2
                did(nc.vector.memset(u[:, :, 0:pad], 0.0))
                did(nc.vector.memset(u[:, :, pad + S:], 0.0))
                did(nc.vector.memset(prod[:, :, 0:1], 0.0))
                did(nc.vector.memset(prod[:, :, S + 1:], 0.0))
                for j in range(2):
                    read_out(v, ("in", CF_G + j), lay)
                    v.sem_inc(passed["dve"], 1)
                    full(v, ("in", CF_A + j), lay)
                    nc.vector.scalar_tensor_tensor(out=u[:, j, pad:pad + S], in0=mix[:, YC + j], scalar=1.0,
                                                   in1=B(("in", CF_A + j))[:, :], op0=ALU.add, op1=ALU.mult)\
                        .then_inc(freesem(("in", CF_A + j)), 1)
                hold(params_in, at(lay, 64, 64))
                for j in range(2):
                    read_out(v, ("in", CF_A + j), lay)
                wait()
                for j in range(2):
                    c = PAR["cconv"] + j * CF_K
                    did(nc.vector.tensor_scalar(mix[:, YC + j], u[:, j, 0:S], par[:, c:c + 1], None, ALU.mult))
                start = step.n
                with v.Fori(1, CF_K) as tap:
                    for j in range(2):
                        v.wait_ge(dve_step, tap * 2 + (start - 3 + j))
                        nc.vector.scalar_tensor_tensor(
                            out=mix[:, YC + j], in0=u[:, j, bass.ds(tap, S)],
                            scalar=par[:, bass.ds(tap + (PAR["cconv"] + j * CF_K), 1)],
                            in1=mix[:, YC + j], op0=ALU.mult, op1=ALU.add).then_inc(dve_step, 1)
                step.n += 2 * (CF_K - 1)
                wait()
                for j in range(2):
                    c = PAR["cconv_b"] + j
                    nc.vector.tensor_scalar(mix[:, YC + j], mix[:, YC + j], 0.5, par[:, c:c + 1], ALU.mult, ALU.add)\
                        .then_inc(cconv_ready, 1)
                did(nc.vector.tensor_scalar(halfgb, par[:, PAR["cnorm_g"]:PAR["cnorm_g"] + 4], 0.5, None, ALU.mult))
                hold(prod_ready, at(lay, 2, 2))
                for k in range(SC_K):
                    for j in range(2):
                        c = PAR["sconv"] + j * SC_K + k
                        if k == 0:
                            did(nc.vector.tensor_scalar(scc[:, j], prod[:, j, 0:S], par[:, c:c + 1], None, ALU.mult))
                        else:
                            v.wait_ge(dve_step, step.n - 1 if (j == 0 or k < SC_K - 1) else step.n)
                            ins = nc.vector.scalar_tensor_tensor(
                                out=scc[:, j], in0=prod[:, j, k:k + S], scalar=par[:, c:c + 1],
                                in1=scc[:, j], op0=ALU.mult, op1=ALU.add)
                            if k < SC_K - 1:
                                did(ins)
                            else:
                                ins.then_inc(sconv_ready, 1)
                for j in range(2):
                    full(v, ("mean",), lay)
                    v.sem_inc(passed["dve"], 1)
                    v.wait_ge(cconv_ready, at(lay, 2, 2))
                    nc.vector.scalar_tensor_tensor(
                        out=mix[:, YC + j], in0=B(("mean",))[:, :], scalar=-1.0 / CF_W, in1=mix[:, YC + j],
                        op0=ALU.mult, op1=ALU.add).then_inc(freesem(("mean",)) if j else cdev_ready, 1)
                v.wait_ge(rnorm_ready, at(lay, 3, 1))
                nc.vector.scalar_tensor_tensor(out=kvlat, in0=kvlat, scalar=par[:, PAR["kv_g"]:PAR["kv_g"] + 1],
                                               in1=r_kv, op0=ALU.mult, op1=ALU.mult).then_inc(lat_ready, 1)
                hold(yb_ready, at(lay, 2, 2))
                full(v, ("rotD", 0), lay)
                nc.vector.tensor_tensor(tmp_d[:, 0], B(("rotD", 0))[:, :], sin_d[:], ALU.mult)\
                    .then_inc(freesem(("rotD", 0)), 1)
                v.wait_ge(rnorm_ready, at(lay, 3, 2))
                for j in range(2):
                    c = PAR["q_g"] + j
                    nc.vector.scalar_tensor_tensor(out=qlat[:, j], in0=qlat[:, j], scalar=par[:, c:c + 1], in1=r_q,
                                                   op0=ALU.mult, op1=ALU.mult).then_inc(lat_ready, 1)
                for j in range(2):
                    name = ("rotD", 1 + j)
                    full(v, name, lay)
                    nc.vector.tensor_tensor(tmp_d[:, 1 + j], B(name)[:, :], sin_d[:], ALU.mult)\
                        .then_inc(freesem(name), 1)
                v.wait_ge(rnorm_ready, at(lay, 3, 3))
                for j in range(2):
                    did(nc.vector.tensor_tensor(mix[:, YC + j], mix[:, YC + j], crs, ALU.mult))
                wait()
                for j in range(2):
                    nc.vector.tensor_scalar(mix[:, YC + j], mix[:, YC + j], halfgb[:, j:j + 1], halfgb[:, 2 + j:3 + j],
                                            ALU.mult, ALU.add).then_inc(z_ready, 1)
                v.wait_ge(th_ready, at(lay, 2, 2))
                for j in range(2):
                    nc.vector.scalar_tensor_tensor(out=mix[:, YC + j], in0=csq[:, j], scalar=1.0, in1=mix[:, YC + j],
                                                   op0=ALU.add, op1=ALU.mult).then_inc(yc_ready, 1)

                def d_width(n):
                    return (0 if n > 0 else P), ((min(n + 2, NT) - max(n - 1, 0)) * P)

                def d_max(i):
                    n, h = divmod(i, GQ_H)
                    off, w = d_width(n)
                    if i >= GQ_H:
                        full(v, ("TD", i - GQ_H), lay)
                        v.sem_inc(passed["dve"], 1)
                    full(v, ("SD", i), lay)
                    v.sem_inc(passed["dve"], 1)
                    ins = nc.vector.tensor_tensor_reduce(p_d[:, h, 0:w], B(("SD", i))[:, 0:w], band[:, off:off + w],
                                                         1.0, -3.0e38, ALU.add, ALU.max, mx[:, i:i + 1])
                    ins.then_inc(freesem(("SD", i)), 1)
                    read_out(v, ("SD", i), lay)
                    c = PAR["sink"] + h
                    nc.vector.tensor_scalar(nmx[:, i:i + 1], mx[:, i:i + 1], par[:, c:c + 1], -1.0,
                                            ALU.max, ALU.mult).then_inc(dmax_ready, 1)

                def d_norm(i):
                    n, h = divmod(i, GQ_H)
                    off, w = d_width(n)
                    v.wait_ge(dexp_done, at(lay, NT * GQ_H, i + 1))
                    did(nc.vector.tensor_tensor(rs[:, i:i + 1], rs[:, i:i + 1], snk[:, i:i + 1], ALU.add))
                    wait()
                    did(nc.vector.reciprocal(rinv[:, i:i + 1], rs[:, i:i + 1]))
                    wait()
                    nc.vector.tensor_scalar(p_d[:, h, 0:w], p_d[:, h, 0:w], rinv[:, i:i + 1], None, ALU.mult)\
                        .then_inc(dp_ready, 1)

                hold(rope_d_ready, at(lay, 3, 3))
                def a_max(i):
                    full(v, ("SA", i), lay)
                    v.sem_inc(passed["dve"], 1)
                    nc.vector.tensor_reduce(nmx[:, i:i + 1], B(("SA", i))[:, :], AX_X, ALU.max, negate=True)\
                        .then_inc(amax_ready, 1)

                def a_norm(i):
                    read_out(v, ("SA", i), lay)
                    did(nc.vector.reciprocal(rinv[:, i:i + 1], rs[:, i:i + 1]))
                    wait()
                    nc.vector.tensor_scalar(p_a[:, i % 4], p_a[:, i % 4], rinv[:, i:i + 1], None, ALU.mult)\
                        .then_inc(ap_ready, 1)

                r = slice(NOPE, QK)

                def k_rope():
                    tmp = mix[r, YA]
                    hold(cos_a_done, at(lay, 3, 1))
                    full(v, ("rotK",), lay)
                    nc.vector.tensor_tensor(tmp, B(("rotK",))[r, :], sin_a[r, :], ALU.mult)\
                        .then_inc(freesem(("rotK",)), 1)
                    read_out(v, ("rotK",), lay)
                    for h in (1, 2, 3, 0):
                        ins = nc.vector.tensor_tensor(Kh[r, h, :], Kh[r, 0, :], tmp, ALU.add)
                    ins.then_inc(rope_a_ready, 1)

                def q_rope(h):
                    tmp = mix[r, YA + (h + 1) % 2]
                    if h % 2 == 0:
                        hold(cos_a_done, at(lay, 3, 2 + h // 2))
                    name = ("rotQ", h)
                    full(v, name, lay)
                    nc.vector.tensor_tensor(tmp, B(name)[r, :], sin_a[r, :], ALU.mult).then_inc(freesem(name), 1)
                    read_out(v, name, lay)
                    nc.vector.tensor_tensor(Qh[r, h, :], Qh[r, h, :], tmp, ALU.add).then_inc(rope_a_ready, 1)

                d_max(0)
                d_max(1)
                k_rope()
                d_norm(0)
                q_rope(0)
                q_rope(1)
                d_max(2)
                for i in range(1, NT * GQ_H):
                    if i + 2 < NT * GQ_H:
                        d_max(i + 2)
                    else:
                        a_max(i + 2 - NT * GQ_H)
                    d_norm(i)
                    if i < 3:
                        q_rope(1 + i)
                a_norm(0)
                for j in range(2):
                    full(v, ("YD", j), lay)
                    nc.vector.tensor_copy(mix[:, YD + j], B(("YD", j))[:, :]).then_inc(freesem(("YD", j)), 1)
                a_max(2)
                for i in range(1, NT * MLA_H):
                    if i + 2 < NT * MLA_H:
                        a_max(i + 2)
                    a_norm(i)
                for j in range(2):
                    full(v, ("YA", j), lay)
                    nc.vector.tensor_copy(mix[:, YA + j], B(("YA", j))[:, :]).then_inc(freesem(("YA", j)), 1)

                ln1_gb = ring[:, LN1_AT]
                hold(x_back, at(lay, 16, 16))
                slot_in(v, lay, LN1_AT)
                v.sem_inc(passed["dve"], 1)
                for t in range(NT):
                    for n in range(2):
                        name = ("mix", t, n)
                        full(v, name, lay)
                        cols = slice(n * 512, (n + 1) * 512)
                        nc.vector.scalar_tensor_tensor(out=X[:, t, cols], in0=X[:, t, cols], scalar=ALPHA,
                                                       in1=B(name)[:, :], op0=ALU.mult, op1=ALU.add)\
                            .then_inc(freesem(name), 1)
                        read_out(v, name, lay)
                        v.sem_inc(passed["dve"], 1)
                        half_stats(t, n)
                    layer_norm(lay, t, ln1_gb, 0, x1_ready)

                lg = aff
                full(v, ("logits",), lay)
                v.sem_inc(passed["dve"], 1)
                lgp = B(("logits",))[:, 0:NT * N_EXP].rearrange("p (t e) -> p t e", e=N_EXP)
                br = par[:, PAR["b_router"]:PAR["b_router"] + N_EXP].unsqueeze(1).broadcast_to([P, NT, N_EXP])
                nc.vector.tensor_tensor(lg, lgp, br, ALU.add).then_inc(freesem(("logits",)), 1)
                read_out(v, ("logits",), lay)
                v.sem_inc(passed["dve"], 1)
                did(nc.vector.tensor_reduce(lmax, lg, AX_X, ALU.max))
                wait()
                nc.vector.tensor_tensor(lg, lg, lmax.unsqueeze(2).broadcast_to([P, NT, N_EXP]), ALU.subtract)\
                    .then_inc(lsub_ready, 1)
                hold(lexp_done, at(lay, 1, 1))
                did(nc.vector.tensor_reduce(lsum, lg, AX_X, ALU.add))
                wait()
                did(nc.vector.reciprocal(lsum, lsum))
                wait()
                nc.vector.tensor_tensor(lg, lg, lsum.unsqueeze(2).broadcast_to([P, NT, N_EXP]), ALU.mult)\
                    .then_inc(aff_ready, 1)
                full(v, ("affT",), lay)
                nc.vector.tensor_copy(aff2[0:N_EXP, 0], B(("affT",))[0:N_EXP, :]).then_inc(freesem(("affT",)), 1)
                read_out(v, ("affT",), lay)
                v.sem_inc(passed["dve"], 1)
                for r8 in range(CAP // 8):
                    src, nxt = aff2[0:N_EXP, r8 % 2], aff2[0:N_EXP, (r8 + 1) % 2]
                    top = vals[0:N_EXP, 0, 8 * r8:8 * r8 + 8]
                    did(nc.vector.max(top, src))
                    wait()
                    if r8 < CAP // 8 - 1:
                        did(nc.vector.match_replace(nxt, top, src, -1.0))
                    did(nc.vector.max_index(idx[0:N_EXP, 8 * r8:8 * r8 + 8], top, src))
                    v.wait_ge(dve_step, step.n - 1)
                wait()
                did(nc.vector.tensor_copy(slotf[0:N_EXP, 0, :], idx[0:N_EXP, :]))
                did(nc.vector.tensor_copy(slotf[0:N_EXP, 1, :], idx[0:N_EXP, :]))
                did(nc.vector.tensor_copy(vals[0:N_EXP, 1, :], vals[0:N_EXP, 0, :]))
                wait()
                v.sem_inc(slots_ready, 1)
                full(v, ("slotT",), lay)
                v.sem_inc(passed["dve"], 1)
                for c, dst in enumerate((slot_f, slot_gate)):
                    src = B(("slotT",))[:, c * N_EXP:(c + 1) * N_EXP].rearrange("p (q e) -> p q e", e=2)
                    for e in range(2):
                        rows = slice(64 * e, 64 * e + 64)
                        ins = nc.vector.tensor_copy(dst[rows, :], src[rows, :, e])
                        if (c, e) != (1, 1):
                            did(ins)
                        else:
                            ins.then_inc(freesem(("slotT",)), 1)
                wait()
                nc.vector.tensor_copy(slot_i[:], slot_f).then_inc(route_ready, 1)

                hold(y_init, at(lay, NT, NT))
                with v.Fori(0, PAIRS // BODY_PAIRS) as body:
                    for b in range(BODY_PAIRS):
                        pair = body * BODY_PAIRS + b
                        for n in range(2):
                            cols = slice(n * 512, (n + 1) * 512)
                            read_out(v, ("G", n), lay, pair)
                            v.sem_inc(passed["dve"], 1)
                            full(v, ("U", n), lay, pair)
                            nc.vector.tensor_tensor(hid[:, cols], hid[:, cols], B(("U", n))[:, :], ALU.mult)\
                                .then_inc(freesem(("U", n)), 1)
                        nc.vector.tensor_scalar(G, slot_iota[:], slot_f[:, bass.ds(pair, 1)],
                                                slot_gate[:, bass.ds(pair, 1)], ALU.is_equal, ALU.mult)\
                            .then_inc(g_ready, 1)
                        full(v, ("O", 1), lay, pair)
                        nc.vector.tensor_copy(o_sb[:, 512:1024], B(("O", 1))[:, :]).then_inc(freesem(("O", 1)), 1)
                        for t in range(NT):
                            for n in range(2):
                                name = ("Y", t, n)
                                cols = slice(n * 512, (n + 1) * 512)
                                full(v, name, lay, pair)
                                nc.vector.tensor_tensor(X[:, t, cols], X[:, t, cols], B(name)[:, :], ALU.add)\
                                    .then_inc(freesem(name), 1)

                ln2_gb = ring[:, LN2_AT % RING]
                slot_in(v, lay, LN2_AT)
                v.sem_inc(passed["dve"], 1)
                for n in range(2):
                    read_out(v, ("Y", NT - 1, n), lay, PAIRS - 1)
                    v.sem_inc(passed["dve"], 1)
                for t in range(NT):
                    for n in range(2):
                        half_stats(t, n)
                    layer_norm(lay, t, ln2_gb, 1, x_ready)

        @block.scalar
        def _(ac):
            step = Steps(ac, act_step)
            did, wait = step.did, step.wait
            act = nc.scalar.activation

            ac.dma_start(trig[:, 5].bitcast(I32), positions.partition_broadcast(P)).then_inc(pos_in, 16)
            for t in range(NT):
                ac.dma_start(X[:, t], x_in[t * P:(t + 1) * P]).then_inc(x_in_sem, 16)
            nc.scalar.preload_act_table(ACT.Sin)
            ac.wait_ge(angles_ready, 1)
            act(sin_d[:], trig[:, 3], ACT.Sin).then_inc(sines_ready, 1)
            ac.wait_ge(angles_ready, 2)
            act(cos_d[:], trig[:, 4], ACT.Sin).then_inc(sines_ready, 1)
            ac.wait_ge(sines_ready, 2)
            ac.wait_ge(small_ready, 1)
            ac.wait_ge(x_in_sem, 16 * NT)
            for t in range(NT):
                ac.dma_start(out[t * P:(t + 1) * P], X[:, t]).then_inc(x_stored, 16)

            with ac.Fori(0, DEPTH) as lay:
                step.restart()
                nc.scalar.preload_act_table_set("exp_and_others")
                for t in range(NT):
                    for half in range(2):
                        name = ("xT", t, half)
                        full(ac, name, lay)
                        act(xT[:, 4 * half:4 * half + 4, t * P:(t + 1) * P],
                            B(name)[:, :].rearrange("p (c f) -> p c f", c=4), ACT.Copy).then_inc(freesem(name), 1)
                ac.wait_ge(x_stored, at(lay, 16 * NT, 16 * NT))
                ac.dma_start(par[:], params[lay]).then_inc(params_in, 16)
                ac.dma_start(wq[:], w_uq[lay].rearrange("(c p) f -> p c f", p=P)).then_inc(params_in, 16)
                ac.dma_start(wkv[:], w_ukv[lay]).then_inc(params_in, 16)
                ac.dma_start(wr[:], w_router[lay].rearrange("(c p) f -> p c f", p=P)).then_inc(params_in, 16)

                def copy_out(name, dst, src=None, scale=1.0, frees=True):
                    full(ac, name, lay)
                    ins = act(dst, B(name)[:, :] if src is None else src, ACT.Copy, scale=scale)
                    if frees:
                        ins.then_inc(freesem(name), 1)
                    return ins

                for j in range(2):
                    name = ("in", CF_G + j)
                    full(ac, name, lay)
                    act(mix[:, YC + j], B(name)[:, :], ACT.Tanh, scale=0.5).then_inc(freesem(name), 1)
                nc.scalar.preload_act_table_set("natural_log_exp_and_others")
                for j in range(2):
                    copy_out(("in", SC_C + j), scc[:, j])
                for j in range(2):
                    copy_out(("in", SC_H + j), prod[:, j, 1:1 + S])
                for j in range(2):
                    copy_out(("in", SC_B + j), mix[:, YB + j])
                copy_out(("in", KV), kvlat, frees=False)
                act(sq_kv, B(("in", KV))[:, :], ACT.Square).then_inc(freesem(("in", KV)), 1)
                copy_out(("in", GQK), gk)
                for j in range(2):
                    name = ("in", QLAT + j)
                    copy_out(name, qlat[:, j], frees=False)
                    act(sq_q[j], B(name)[:, :], ACT.Square).then_inc(freesem(name), 1)

                def inverse_root(name, dst, n, eps):
                    full(ac, name, lay)
                    act(dst, B(name)[:, :], ACT.Ln, scale=1.0 / n, bias=eps).then_inc(freesem(name), 1)
                    read_out(ac, name, lay)
                    act(dst, dst, ACT.Exp, scale=-0.5).then_inc(rnorm_ready, 1)

                inverse_root(("ssq", 0), r_kv, KV_RANK, c_rms)
                for j in range(2):
                    copy_out(("in", GQQ + j), gq[:, j], scale=GQ_SCALE)
                for j in range(2):
                    read_out(ac, ("mean",), lay)
                    act(csq[:, j], mix[:, YC + j], ACT.Square).then_inc(csq_ready, 1)
                inverse_root(("ssq", 1), r_q, Q_RANK, c_rms)
                copy_out(("in", GQV), gv[:].rearrange("p t f -> p (t f)"))
                copy_out(("in", KROPE), Kh[NOPE:QK, 0, :], B(("in", KROPE))[NOPE:QK, :])
                inverse_root(("var",), crs, CF_W, c_ln)
                nc.scalar.preload_act_table_set("exp_and_others")
                for h in range(MLA_H):
                    copy_out(("qup", h), Qh[0:QK, h, :], B(("qup", h))[0:QK, :], scale=MLA_SCALE)
                for j in range(2):
                    ac.wait_ge(z_ready, at(lay, 2, 2))
                    act(csq[:, j], mix[:, YC + j], ACT.Tanh).then_inc(th_ready, 1)
                for j in range(2):
                    for e in range(2):
                        copy_out(("kup", j), Kh[0:NOPE, 2 * j + e, :], B(("kup", j))[64 * e:64 * e + 64, :],
                                 frees=(e == 1))
                for j in range(2):
                    copy_out(("vup", j), V[:, 2 * j:2 * j + 2, :].rearrange("p t f -> p (t f)"))

                def d_exp(i):
                    n, h = divmod(i, GQ_H)
                    w = (min(n + 2, NT) - max(n - 1, 0)) * P
                    ac.wait_ge(dmax_ready, at(lay, NT * GQ_H, i + 1))
                    did(act(p_d[:, h, 0:w], p_d[:, h, 0:w], ACT.Exp, bias=nmx[:, i:i + 1], accum_out=rs[:, i:i + 1]))
                    c = PAR["sink"] + h
                    wait()
                    act(snk[:, i:i + 1], par[:, c:c + 1], ACT.Exp, bias=nmx[:, i:i + 1]).then_inc(dexp_done, 1)

                def d_turned(i):
                    n, h = divmod(i, GQ_H)
                    w = (min(n + 2, NT) - max(n - 1, 0)) * P
                    if i == 0:
                        ac.wait_ge(yc_ready, at(lay, 2, 2))
                        ac.wait_ge(yb_ready, at(lay, 2, 2))
                    if n > 0:
                        ac.wait_ge(pvd_done, at(lay, 2 * (NT - 1), 2 * (n - 1) + h // 2 + 1))
                    full(ac, ("TD", i), lay)
                    act(pt_d[:, h, 0:w], B(("TD", i))[:, 0:w], ACT.Copy).then_inc(freesem(("TD", i)), 1)

                def a_exp(i):
                    if i < 3:
                        full(ac, ("TD", NT * GQ_H - 3 + i), lay)
                    elif i > 3:
                        full(ac, ("TA", i - 4), lay)
                    ac.wait_ge(amax_ready, at(lay, NT * MLA_H, i + 1))
                    act(p_a[:, i % 4], B(("SA", i))[:, :], ACT.Exp, bias=nmx[:, i:i + 1],
                        accum_out=rs[:, i:i + 1]).then_inc(freesem(("SA", i)), 1)

                def a_turned(i):
                    if i == 0:
                        full(ac, ("YD", 0), lay)
                        full(ac, ("YD", 1), lay)
                    if i >= 4:
                        j, t = (i - 4) // 8, (i - 4) // 2 % NT
                        if t < NT - 1:
                            ac.wait_ge(pva_done, at(lay, 2 * (NT - 1), (NT - 1) * j + t + 1))
                        else:
                            full(ac, ("YA", j), lay)
                    full(ac, ("TA", i), lay)
                    act(pt_a[:, i % 4], B(("TA", i))[:, :], ACT.Copy).then_inc(freesem(("TA", i)), 1)

                d_exp(0)
                d_exp(1)
                for i in range(NT * GQ_H):
                    if i + 2 < NT * GQ_H:
                        d_exp(i + 2)
                    else:
                        a_exp(i + 2 - NT * GQ_H)
                    d_turned(i)
                a_turned(0)
                a_exp(2)
                for i in range(1, NT * MLA_H):
                    if i + 2 < NT * MLA_H:
                        a_exp(i + 2)
                    a_turned(i)
                full(ac, ("YA", 1), lay)
                ac.dma_start(X[:], out.rearrange("(t p) f -> p t f", p=P)).then_inc(x_back, 16)

                def x1_turned(t):
                    ac.wait_ge(x1_ready, at(lay, 2 * NT, 2 * t + 2))
                    ac.dma_start(x1_rows[t * P:(t + 1) * P], X[:, t]).then_inc(x1_stored, 16)
                    for half in range(2):
                        name = ("x1T", t, half)
                        full(ac, name, lay)
                        act(x1T[:, 4 * half:4 * half + 4, t * P:(t + 1) * P],
                            B(name)[:, :].rearrange("p (c f) -> p c f", c=4), ACT.Copy).then_inc(freesem(name), 1)

                for t in range(NT):
                    x1_turned(t)
                ac.wait_ge(lsub_ready, at(lay, 1, 1))
                act(aff, aff, ACT.Exp).then_inc(lexp_done, 1)
                nc.scalar.preload_act_table(ACT.Silu)
                ac.wait_ge(x1_stored, at(lay, 16 * NT, 16 * NT))
                for t in range(NT):
                    act(X[:, t], X[:, t], ACT.Copy, scale=ALPHA).then_inc(y_init, 1)

                with ac.Fori(0, PAIRS // BODY_PAIRS) as body:
                    for b in range(BODY_PAIRS):
                        pair = body * BODY_PAIRS + b

                        def quarter_copies(kind, dst):
                            for half in range(2):
                                full(ac, (kind, half), lay, pair)
                                act(dst[:, 4 * half:4 * half + 4, :].rearrange("p c f -> p (c f)"),
                                    B((kind, half))[:, :], ACT.Copy).then_inc(freesem((kind, half)), 1)

                        quarter_copies("xsT", xsT)
                        for n in range(2):
                            full(ac, ("G", n), lay, pair)
                            act(hid[:, n * 512:(n + 1) * 512], B(("G", n))[:, :], ACT.Silu)\
                                .then_inc(freesem(("G", n)), 1)
                        quarter_copies("hT", hidT)
                        full(ac, ("O", 0), lay, pair)
                        act(o_sb[:, 0:512], B(("O", 0))[:, :], ACT.Copy).then_inc(freesem(("O", 0)), 1)

                for t in range(NT):
                    ac.wait_ge(x_ready, at(lay, 2 * NT, 2 * (NT + t + 1)))
                    ac.dma_start(out[t * P:(t + 1) * P], X[:, t]).then_inc(x_stored, 16)
            ac.wait_ge(x_stored, 16 * NT * (DEPTH + 1))
            ac.wait_ge(x1_stored, 16 * NT * DEPTH)

        @block.gpsimd
        def _(g):
            step = Steps(g, pool_step)
            did, wait = step.did, step.wait
            tt = nc.gpsimd.tensor_tensor

            def hold(s, n):
                g.wait_ge(s, n)
                g.sem_inc(passed["pool"], 1)

            g.wait_ge(small_ready, 1)
            g.wait_ge(trig_ready, 2)

            def inverse_deviation(lay, t, second):
                hold(var_ready, at(lay, 2 * NT, 4 * second + t + 1))
                did(nc.gpsimd.tensor_scalar(rstd[:, t:t + 1], mv[:, t, 1:2], LN_EPS, None, ALU.add))
                wait()
                tt(rstd[:, t:t + 1], rstd[:, t:t + 1], half_neg, ALU.pow).then_inc(rstd_ready, 1)

            with g.Fori(0, DEPTH) as lay:
                step.restart()
                for j in range(2):
                    hold(freesem(("in", SC_C + j)), bank_count(("in", SC_C + j), lay, 2, 0)[1])
                    hold(freesem(("in", SC_H + j)), bank_count(("in", SC_H + j), lay, 2, 0)[1])
                    tt(prod[:, j, 1:1 + S], prod[:, j, 1:1 + S], scc[:, j], ALU.mult).then_inc(prod_ready, 1)
                hold(sconv_ready, at(lay, 2, 2))
                for j in range(2):
                    hold(freesem(("in", SC_B + j)), bank_count(("in", SC_B + j), lay, 2, 0)[1])
                    tt(mix[:, YB + j], mix[:, YB + j], scc[:, j], ALU.mult).then_inc(yb_ready, 1)
                for j, buf in enumerate((gk, gq[:, 0], gq[:, 1])):
                    hold(freesem(("rotD", j)), bank_count(("rotD", j), lay, 2, 0)[1])
                    did(tt(buf, buf, cos_d[:], ALU.mult))
                    wait()
                    tt(buf, buf, tmp_d[:, j], ALU.add).then_inc(rope_d_ready, 1)
                r = slice(NOPE, QK)
                hold(rope_d_ready, at(lay, 3, 3))
                hold(fullsem(("rotK",)), bank_count(("rotK",), lay, 1, 0)[1])
                tt(Kh[r, 0, :], Kh[r, 0, :], cos_a[r, :], ALU.mult).then_inc(cos_a_done, 1)
                for h in range(0, MLA_H, 2):
                    for e in range(2):
                        hold(fullsem(("rotQ", h + e)), bank_count(("rotQ", h + e), lay, 1, 0)[1])
                    tt(Qh[r, h:h + 2, :], Qh[r, h:h + 2, :], cos_a[r, :].unsqueeze(1).broadcast_to([ROPE, 2, S]),
                       ALU.mult).then_inc(cos_a_done, 1)

                hold(cos_a_done, at(lay, 3, 3))
                for t in range(NT):
                    inverse_deviation(lay, t, 0)

                hold(route_ready, at(lay, 1, 1))
                hold(x1_stored, at(lay, 16 * NT, 16 * NT))

                def gather(b, pair, count):
                    nc.gpsimd.tensor_copy(cur[:, b:b + 1], slot_i[:, bass.ds(pair, 1)]).then_inc(cur_ready, 1)
                    hold(cur_ready, count)
                    nc.gpsimd.indirect_dma_start(xs[:, b, :], None, x1_rows,
                                                 bass.IndirectOffsetOnAxis(ap=cur[:, b:b + 1], axis=0))\
                        .then_inc(xs_full[b], 16)

                for b in range(BODY_PAIRS):
                    gather(b, b, at(lay, PAIRS, b + 1))
                with g.Fori(1, PAIRS // BODY_PAIRS) as body:
                    for b in range(BODY_PAIRS):
                        bank, nth = USES[("xsT", 1)]
                        hold(bank_full[bank], lay * PER_LAYER[bank] + body * (BODY_PAIRS * PER_PAIR[bank])
                             + ((b - BODY_PAIRS) * PER_PAIR[bank] + nth + 1))
                        gather(b, body * BODY_PAIRS + b, lay * PAIRS + body * BODY_PAIRS + (b + 1))

                for t in range(NT):
                    inverse_deviation(lay, t, 1)


def constants():
    c = np.zeros((P, N_CONST), np.float32)
    c[:, IDENT:IDENT + P] = np.eye(P, dtype=np.float32)
    c[:, ONES:ONES + P] = 1.0
    for at, block in ((ROT_A, ROPE), (ROT_D, GQ_D)):
        half = block // 2
        for m in range(P):
            first = m % block < half
            c[m + half if first else m - half, at + m] = -1.0 if first else 1.0
    i, j = np.arange(P)[:, None], np.arange(3 * P)[None, :]
    c[:, BAND:BAND + 3 * P] = np.where(np.abs(i - (j - P)) <= 128, 0.0, -1.0e30)
    inv = 1.0 / (np.float32(10000.0) ** (np.arange(0, GQ_D, 2, dtype=np.float32) / np.float32(GQ_D)))
    c[:, FREQ] = inv.astype(np.float32)[np.arange(P) % (GQ_D // 2)]
    iota = np.ascontiguousarray(np.broadcast_to(np.arange(S, dtype=np.int16), (P, S)))
    return c, iota


def lay_out(a):
    sizes = (256, 128, 32, 256, 256, 256, 256, 256, 256, 128, 128)
    ends = np.cumsum(sizes)
    q_lat, kv, k_rope, sc_b, sc_c, sc_h, cf_a, cf_g, gq_q, gq_k, gq_v = (
        np.arange(e - n, e) for e, n in zip(ends, sizes))
    gq_q = gq_q.reshape(GQ_H, GQ_D)[[0, 2, 1, 3]].ravel()
    order = np.concatenate([cf_g, cf_a, sc_c, sc_h, sc_b, kv, gq_k, q_lat, gq_q, gq_v, k_rope])
    w_in = np.zeros((DEPTH, D, IN_SLOTS * 256), np.float32)
    w_in[:, :, :len(order)] = a["w_in"][:, :, order]
    w_in = w_in.reshape(DEPTH, KD, P, IN_SLOTS, 256).transpose(0, 3, 2, 1, 4).reshape(DEPTH, IN_SLOTS, P, SLOT)
    ukv = a["w_ukv"].reshape(DEPTH, KV_RANK, MLA_H, 2, 64).transpose(0, 1, 3, 2, 4).reshape(DEPTH, KV_RANK, -1)

    def on_partitions(v):
        n = v.shape[-1] // P
        return v.reshape(DEPTH, -1, n, P).transpose(0, 3, 2, 1).reshape(DEPTH, P, -1)

    def every(v):
        return np.broadcast_to(v[:, None, :], (DEPTH, P, v.shape[-1]))

    par = np.concatenate([on_partitions(a[k]) for k in (
        "sconv_w", "cconv_w", "cconv_b", "cnorm_g", "cnorm_b", "q_norm_g", "kv_norm_g")]
        + [every(a["sink"]), every(a["b_router"])], axis=2)
    c, iota = constants()
    return {
        "x_in": a["x"].reshape(S, D), "positions": a["positions"].reshape(S), "w_in": w_in, "w_uq": a["w_uq"],
        "w_ukv": ukv, "w_router": a["w_router"], "params": par, "w_out": a["w_out"],
        "ln1": np.concatenate([a["ln1_g"], a["ln1_b"]], axis=1), "ln2": np.concatenate([a["ln2_g"], a["ln2_b"]], axis=1),
        "w_gate": a["w_gate"], "w_up": a["w_up"], "w_down": a["w_down"], "consts": c, "iota": iota,
    }


def kernel(**inputs):
    import concourse.bacc as bacc
    from concourse.bass_utils import run_bass_kernel_spmd

    nc = bacc.Bacc("TRN2", target_bir_lowering=False, num_devices=1)
    arrays = {k: np.ascontiguousarray(v) for k, v in lay_out({k: np.asarray(v) for k, v in inputs.items()}).items()}
    aps = {k: nc.dram_tensor(k, v.shape, mybir.dt.from_np(v.dtype), kind="ExternalInput").ap()
           for k, v in arrays.items()}
    out = nc.dram_tensor("out", (S, D), F32, kind="ExternalOutput").ap()
    trunk(nc, **aps, out=out)
    r = run_bass_kernel_spmd(nc, [arrays], core_ids=[0])
    return r.results[0]["out"].reshape(1, S, D)
```

```python
from contextlib import ExitStack

import concourse.bass as bass
import numpy as np
from concourse import mybir

F32 = mybir.dt.float32
F32R = mybir.dt.float32r
I32 = mybir.dt.int32
I16 = mybir.dt.int16
U32 = mybir.dt.uint32
ALU = mybir.AluOpType
ACT = mybir.ActivationFunctionType
AX_X = mybir.AxisListType.X

P = 128
DEPTH, D, S = 2, 1024, 512
KD = D // P
NT = S // P
MLA_H, NOPE, ROPE, VD = 4, 64, 32, 64
QK = NOPE + ROPE
Q_RANK, KV_RANK = 256, 128
GQ_H, GQ_D = 4, 64
SC_K, CF_K, CF_W = 3, 31, 256
N_EXP, FF, CAP = 16, 1024, 64
PAIRS = N_EXP // 2
LN_EPS, RMS_EPS = 1e-5, 1e-6
ALPHA = (2 * DEPTH) ** 0.25
MLA_SCALE = float(QK) ** -0.5
GQ_SCALE = float(GQ_D) ** -0.5

CF_G, CF_A, SC_C, SC_H, SC_B, KV, GQK, QLAT, GQQ, GQV, KROPE = 0, 2, 4, 6, 8, 10, 11, 12, 14, 16, 17
N_IN = 18
IN_SLOTS = N_IN // 2

RING = 16
SLOT = 2 * FF
HI_AT = IN_SLOTS
X_HI_AT = HI_AT + 2
WOUT_AT = X_HI_AT + 2
LN1_AT = WOUT_AT + D // P // 2
MIX_HI_AT = LN1_AT + 1
MOE_AT = MIX_HI_AT + 2
PAIR_CHUNKS = 3 * KD
USED = MOE_AT + PAIRS * PAIR_CHUNKS
CHUNKS = -(-USED // RING) * RING
BODY_PAIRS = 2
assert BODY_PAIRS * PAIR_CHUNKS % RING == 0


def loads(slot, last):
    return sum(n % RING == slot and not HI_AT <= n < WOUT_AT and not MIX_HI_AT <= n < MOE_AT
               for n in range(min(last, USED - 1) + 1))


PAR = {}
_at = 0
for _name, _n in (("sconv", 2 * SC_K), ("cconv", 2 * CF_K), ("cconv_b", 2), ("cnorm_g", 2), ("cnorm_b", 2),
                  ("q_g", 2), ("kv_g", 1), ("sink", GQ_H), ("b_router", N_EXP)):
    PAR[_name] = _at
    _at += _n
N_PAR = _at

IDENT, ONES, ROT_A, ROT_D, BAND, FREQ = 0, P, 2 * P, 3 * P, 4 * P, 4 * P + 3 * P
N_CONST = FREQ + 1
TWO_PI_1 = 6.28125
TWO_PI_2 = float(np.float32(np.floor((2 * np.pi - TWO_PI_1) * 2**20) / 2**20))
TWO_PI_3 = float(np.float32(2 * np.pi - TWO_PI_1 - TWO_PI_2))
ROUND = 1.5 * 2.0**23
PI_BELOW = 3.1415925


TILE_ORDER = (0, 2, 1, 3)


def bank_uses():
    order = []
    for place, t in enumerate(TILE_ORDER):
        for half in range(2):
            order.append((("xT", t, half), (4 + 2 * place + half) % 8))
    for i in range(N_IN):
        order.append((("in", i), i % 4))
        if i == QLAT + 1:
            order += [(("ssq", 0), 4), (("mean",), 6), (("rotD", 0), 7)]
        if i == GQQ + 1:
            order += [(("ssq", 1), 5)]
        if i == GQV:
            order += [(("rotD", 1), 4), (("rotD", 2), 6)]
    order += [(("var",), 7), (("gvT",), 5)]
    order += [(("qup", h), 4 + h) for h in range(MLA_H)]
    order += [(("kup", 0), 4), (("kup", 1), 5), (("vup", 0), 6), (("vup", 1), 7)]
    order += [(("rotQ",), 7), (("rotK",), 6)]
    order += [(("YD", 0), 5), (("YD", 1), 6)]
    for i in range(NT * GQ_H):
        order += [(("SD", i), (0, 1, 4)[i % 3]), (("TD", i), 2 + i % 2)]
    order += [(("YA", 0), 7), (("YA", 1), 6)]
    for i in range(NT * MLA_H):
        order += [(("SA", i), (0, 1, 4, 5)[i % 4]), (("TA", i), 2 + i % 2)]
    for t in range(NT):
        order += [(("mix", t, n), (2 * t + n) % 4) for n in range(2)]
        order += [(("x1T", t, half), 4 + half) for half in range(2)]
    order += [(("logits",), 6), (("affT",), 7), (("slotT",), 6)]
    place, count = {}, [0] * 8
    for name, bank in order:
        place[name] = (bank, count[bank])
        count[bank] += 1
    first = list(count)
    pair = [(("xsT", half), 6 + half) for half in range(2)]
    pair += [(("G", n), n) for n in range(2)] + [(("U", n), 2 + n) for n in range(2)]
    pair += [(("hT", half), 6 + half) for half in range(2)]
    pair += [(("O", n), 4 + n) for n in range(2)]
    pair += [(("Y", t, n), 6 + n) for t in range(NT) for n in range(2)]
    for name, bank in pair:
        place[name] = (bank, count[bank])
        count[bank] += 1
    per_pair = [c - f for c, f in zip(count, first)]
    total = [f + PAIRS * q for f, q in zip(first, per_pair)]
    return place, per_pair, total


USES, PER_PAIR, PER_LAYER = bank_uses()


def trunk(nc, x_in, positions, w_in, w_uq, w_ukv, w_router, params, w_out, ln1, ln2, w_gate, w_up, w_down,
          consts, iota, out):
    x1_rows = nc.dram_tensor("x1_rows", (S, D), F32, kind="Internal").ap()

    with ExitStack() as ctx:
        def sb(name, shape, dt=F32):
            return ctx.enter_context(nc.sbuf_tensor(name, shape, dt))

        def sem(name):
            return ctx.enter_context(nc.semaphore(name))

        with nc.sbuf_tensor("w_lo", [P, IN_SLOTS, SLOT], F32R) as w_lo, \
                nc.sbuf_tensor("w_hi", [P, 2, SLOT], F32R) as w_hi, \
                nc.sbuf_tensor("x_hi", [P, KD, S], F32R) as x_hi, \
                nc.sbuf_tensor("wout_lo", [P, RING - WOUT_AT, SLOT], F32R) as wout_lo:
            pass
        ring = sb("ring", [P, RING, SLOT])
        cst = sb("cst", [P, N_CONST])
        slot_iota = sb("slot_iota", [P, S], I16)
        cos_a, sin_a, cos_d, sin_d = (sb(n, [P, S]) for n in ("cos_a", "sin_a", "cos_d", "sin_d"))
        par = sb("par", [P, N_PAR])
        wq = sb("wq", [P, 2, MLA_H * QK])
        wkv = sb("wkv", [P, MLA_H * (NOPE + VD)])
        wr = sb("wr", [P, KD, N_EXP])
        X = sb("X", [P, NT, D])
        with nc.sbuf_tensor("x_lo", [P, KD, S], F32R) as x_lo, \
                nc.sbuf_tensor("mix_lo", [P, 8, S], F32R) as mix_lo:
            pass
        work = sb("work", [P, 11 * 1024])
        stat = sb("stat", [P, 216])
        cur = sb("cur", [P, 2], I32)
        slot_i = sb("slot_i", [P, PAIRS], I32)

        x_hi_flat = x_hi[:].rearrange("p k s -> p (k s)")
        wout_hi = [w_hi[:, 0], w_hi[:, 1], x_hi_flat[:, 0:SLOT], x_hi_flat[:, SLOT:2 * SLOT]]
        wout_low = [wout_lo[:, n] if n < RING - WOUT_AT else w_lo[:, n - (RING - WOUT_AT)] for n in range(4)]
        n = MIX_HI_AT % RING
        mix_hi = w_lo[:, n:n + 2].rearrange("p a f -> p (a f)").rearrange("p (k s) -> p k s", k=8)

        ident = cst[:, IDENT:IDENT + P]
        ones = cst[:, ONES:ONES + P]
        rot_a = cst[:, ROT_A:ROT_A + P]
        rot_d = cst[:, ROT_D:ROT_D + P]
        band = cst[:, BAND:BAND + 3 * P]
        freq = cst[:, FREQ:FREQ + 1]

        def view(flat, at, *shape):
            n = int(np.prod(shape))
            v = flat[:, at:at + n]
            if len(shape) == 2:
                v = v.rearrange("p (a b) -> p a b", b=shape[1])
            return v

        Xf = X[:].rearrange("p t f -> p (t f)")
        u = view(Xf, 0, 2, S + CF_K - 1)
        scc = view(Xf, 1084, 2, S)
        prod = view(Xf, 2108, 2, S + SC_K - 1)
        gv = view(Xf, 3584, NT, 2 * GQ_D)
        csq = view(Xf, 0, 2, S)
        crs = view(Xf, 0, S)
        pt_a = view(Xf, 0, 4, S)
        pt_d = view(Xf, 0, GQ_H, 3 * P)
        p_d = view(Xf, 2048, GQ_H, 3 * P)
        p_a = view(Xf, 2048, 4, S)
        tmp_d = view(Xf, 2048, 3, S)
        Qh = view(work, 0, MLA_H, S)
        Kh = view(work, 2048, MLA_H, S)
        mix = view(work, 4096, 8, S)
        YA, YB, YC, YD = 0, 2, 4, 6
        qlat = view(work, 8192, 2, S)
        V = view(work, 8192, NT, MLA_H * VD)
        kvlat = view(work, 9216, S)
        gq = view(work, 9728, 2, S)
        gk = view(work, 10752, S)
        sq_kv, sq_q, r_kv, r_q = mix[:, YA], (mix[:, YA + 1], mix[:, YD]), mix[:, YD + 1], mix[:, YA]
        gv_turned = mix[:, YA + 1]
        x1T = view(work, 0, KD, S)
        xs = view(work, 4096, 2, D)
        xsT = view(work, 6144, KD, P)
        hid = view(work, 7168, FF)
        hidT = view(work, 8192, KD, P)
        o_sb = view(work, 9216, D)
        G = view(work, 10240, S)
        aff2 = view(work, 10240, 2, S)
        ln2_gb = view(work, 0, 2 * D)
        vals = view(work, 7168, 2, CAP)
        slotf = view(work, 7168 + 128, 2, CAP)
        idx = view(work, 7168 + 256, CAP).bitcast(U32)
        trig = view(work, 4096, 6, S)

        bn = stat[:, 0:48].rearrange("p (t k) -> p t k", k=12)
        mv = stat[:, 48:56].rearrange("p (t k) -> p t k", k=2)
        rstd = stat[:, 56:60]
        nmr = stat[:, 60:64]
        mx, nmx, rs, rinv = (stat[:, 64 + 16 * i:80 + 16 * i] for i in range(4))
        snk = stat[:, 128:144]
        halfgb = stat[:, 144:148]
        half_neg = stat[:, 148:149]
        lmax, lsum = stat[:, 152:156], stat[:, 156:160]
        slot_f = stat[:, 160:168]
        slot_gate = stat[:, 168:176]
        c_rms, c_ln = stat[:, 176:177], stat[:, 177:178]
        aff = view(work, 7168 + 384, NT, N_EXP)

        banks = [ctx.enter_context(nc.psum_tensor(f"bank{i}", [P, 512], F32)) for i in range(8)]

        slot_full = [sem(f"slot_full{i}") for i in range(RING)]
        chunk_free = sem("chunk_free")
        bank_full = [sem(f"bank_full{i}") for i in range(8)]
        bank_free = [sem(f"bank_free{i}") for i in range(8)]
        consts_in, x_in_sem, pos_in = sem("consts_in"), sem("x_in_sem"), sem("pos_in")
        params_in, ln2_in = sem("params_in"), sem("ln2_in")
        x_hi_ready, w_hi_ready, w_lo0_ready, w_lo_ready = (
            sem(n) for n in ("x_hi_ready", "w_hi_ready", "w_lo0_ready", "w_lo_ready"))
        wout_hi_ready, wout_lo_ready, mix_hi_ready, split_hi, split_ready = (
            sem(n) for n in ("wout_hi_ready", "wout_lo_ready", "mix_hi_ready", "split_hi", "split_ready"))
        small_ready = sem("small_ready")
        x_ready, x_stored, x_back = sem("x_ready"), sem("x_stored"), sem("x_back")
        angles_ready, sines_ready, trig_ready = sem("angles_ready"), sem("sines_ready"), sem("trig_ready")
        prod_ready, sconv_ready, yb_ready = sem("prod_ready"), sem("sconv_ready"), sem("yb_ready")
        cconv_ready, cdev_ready, csq_ready = sem("cconv_ready"), sem("cdev_ready"), sem("csq_ready")
        rnorm_ready, lat_ready, z_ready, th_ready, yc_ready = (
            sem(n) for n in ("rnorm_ready", "lat_ready", "z_ready", "th_ready", "yc_ready"))
        rot_d_out, rope_d_ready = sem("rot_d_out"), sem("rope_d_ready")
        cos_a_done, rope_k_ready, keys_ready, queries_ready = (
            sem(n) for n in ("cos_a_done", "rope_k_ready", "keys_ready", "queries_ready"))
        dmax_ready, dexp_done, dp_ready, pvd_done = (
            sem(n) for n in ("dmax_ready", "dexp_done", "dp_ready", "pvd_done"))
        amax_ready, ap_ready, pva_done = sem("amax_ready"), sem("ap_ready"), sem("pva_done")
        var_ready, rstd_ready = sem("var_ready"), sem("rstd_ready")
        x1_ready, x1_stored, y_init = sem("x1_ready"), sem("x1_stored"), sem("y_init")
        nmr_ready, centred, gained, biased = (sem(n) for n in ("nmr_ready", "centred", "gained", "biased"))
        lsub_ready, lexp_done, aff_ready, slots_ready, route_ready = (
            sem(n) for n in ("lsub_ready", "lexp_done", "aff_ready", "slots_ready", "route_ready"))
        cur_ready = sem("cur_ready")
        xs_full = [sem(f"xs_full{i}") for i in range(2)]
        g_ready = sem("g_ready")
        dve_step, act_step, pool_step = sem("dve_step"), sem("act_step"), sem("pool_step")
        passed = {e: sem(f"passed_{e}") for e in ("dve", "act", "pool", "pe")}

        def at(lay, per_layer, n):
            return lay * per_layer + n

        def bank_count(name, lay, more, pair):
            bank, nth = USES[name]
            if isinstance(pair, int) and pair == 0:
                return bank, lay * PER_LAYER[bank] + (nth + more)
            return bank, lay * PER_LAYER[bank] + pair * PER_PAIR[bank] + (nth + more)


        def full(eng, name, lay, pair=0):
            bank, n = bank_count(name, lay, 1, pair)
            eng.wait_ge(bank_full[bank], n)

        def read_out(eng, name, lay, pair=0):
            bank, n = bank_count(name, lay, 2, pair)
            eng.wait_ge(bank_free[bank], n)

        def before(eng, name, lay, pair=0):
            bank, n = bank_count(name, lay, 1, pair)
            eng.wait_ge(bank_free[bank], n)

        def B(name):
            return banks[USES[name][0]]

        def fullsem(name):
            return bank_full[USES[name][0]]

        def freesem(name):
            return bank_free[USES[name][0]]

        class Steps:

            def __init__(self, eng, s):
                self.eng, self.sem, self.n = eng, s, 0

            def did(self, ins):
                ins.then_inc(self.sem, 1)
                self.n += 1

            def wait(self):
                self.eng.wait_ge(self.sem, self.n)

            def restart(self):
                self.eng.drain()
                self.eng.sem_clear(self.sem)
                self.n = 0

        block = ctx.enter_context(nc.Block())

        MIX_ORDER = (YC, YC + 1, YB, YB + 1, YD, YD + 1, YA, YA + 1)

        @block.sync
        def _(sp):
            sp.dma_start(cst[:], consts).then_inc(consts_in, 16)
            sp.dma_start(slot_iota[:], iota).then_inc(consts_in, 16)

            with sp.Fori(0, DEPTH) as lay:
                for n in [*range(HI_AT), *range(WOUT_AT, LN1_AT + 1)]:
                    sp.wait_ge(chunk_free, at(lay, CHUNKS, n + 1))
                    slot = n % RING
                    if n < HI_AT:
                        src, dst = w_in[lay, n], ring[:, slot]
                    elif n < LN1_AT:
                        k = 2 * (n - WOUT_AT)
                        src = w_out[lay, k * P:(k + 2) * P].rearrange("(c p) f -> p c f", p=P)
                        dst = ring[:, slot].rearrange("p (c f) -> p c f", c=2)
                    else:
                        src, dst = ln1[lay].partition_broadcast(P), ring[:, slot]
                    sp.dma_start(dst, src).then_inc(slot_full[slot], 16)
                with sp.Fori(0, PAIRS // BODY_PAIRS) as body:
                    for j in range(BODY_PAIRS * PAIR_CHUNKS):
                        pair, part, k = j // PAIR_CHUNKS, j % PAIR_CHUNKS // KD, j % KD
                        w = (w_gate, w_up, w_down)[part]
                        slot = (MOE_AT + j) % RING
                        sp.wait_ge(chunk_free, lay * CHUNKS + body * (BODY_PAIRS * PAIR_CHUNKS) + (MOE_AT + j + 1))
                        src = w[lay, bass.ds(body * (2 * BODY_PAIRS) + 2 * pair, 2), k * P:(k + 1) * P]
                        sp.dma_start(ring[:, slot].rearrange("p (e f) -> p e f", e=2),
                                     src.rearrange("e p f -> p e f")).then_inc(slot_full[slot], 16)

        def slot_in(eng, lay, n, body=0):
            slot = n % RING
            count = lay * (16 * loads(slot, CHUNKS)) + 16 * loads(slot, n)
            if not isinstance(body, int):
                count = count + body * (16 * BODY_PAIRS * PAIR_CHUNKS // RING)
            eng.wait_ge(slot_full[slot], count)

        @block.tensor
        def _(pe):
            mm = nc.tensor.matmul

            def transposed(name, lay, src, n_blocks, pair=0, retire=0):
                before(pe, name, lay, pair)
                for c in range(n_blocks):
                    ins = nc.tensor.transpose(B(name)[:, c * P:(c + 1) * P], src[:, c * P:(c + 1) * P], ident)
                    if c == 0 and retire:
                        ins.then_inc(chunk_free, retire)
                ins.then_inc(fullsem(name), 1)

            pe.wait_ge(consts_in, 32)
            pe.wait_ge(x_in_sem, 16 * NT)
            pe.sem_inc(x_ready, 6)
            pe.sem_inc(biased, 1)
            pe.sem_inc(chunk_free, RING - (CHUNKS - USED))
            for free in bank_free:
                pe.sem_inc(free, 1)
            with pe.Fori(0, DEPTH) as lay:
                for place, t in enumerate(TILE_ORDER):
                    if place == 0:
                        pe.wait_ge(biased, at(lay, 1, 1))
                    for half in range(2):
                        if place > 0:
                            pe.wait_ge(x_ready, at(lay, 6, 2 * place - 1 + (1 if t == 1 else half)))
                        transposed(("xT", t, half), lay, X[:, t, half * 512:half * 512 + 512], 4,
                                   retire=CHUNKS - USED if (t, half) == (NT - 1, 1) else 0)

                def w_parts(n):
                    return [a.rearrange("p (c f) -> p c f", c=KD) for a in (w_hi[:, n % 2], w_lo[:, n])]

                def project(i, passes, first=True, last=True):
                    n, fc = i // 2, i % 2
                    hi, lo = w_parts(n)
                    for number, (w, x) in enumerate(passes):
                        w, x = (hi, lo)[w], (x_hi, x_lo)[x]
                        for k in range(KD):
                            ins = mm(B(("in", i))[:, :], w[:, k, fc * P:(fc + 1) * P], x[:, k, :],
                                     start=(first and number == 0 and k == 0),
                                     stop=(last and number == len(passes) - 1 and k == KD - 1))
                            if fc == 0 and number == 0 and k == 0 and i > 0:
                                ins.then_inc(chunk_free, 1)
                    return ins

                HI_HI, HI_LO, LO_HI = (0, 0), (0, 1), (1, 0)
                pe.wait_ge(w_hi_ready, at(lay, IN_SLOTS, 1))
                pe.wait_ge(x_hi_ready, at(lay, 2 * NT, 2 * NT))
                for i in range(2):
                    before(pe, ("in", i), lay)
                    project(i, (HI_HI,), last=False)
                for t in range(NT):
                    for half in range(2):
                        read_out(pe, ("xT", t, half), lay)
                for i in range(2):
                    project(i, (HI_LO,), first=False, last=False)
                pe.wait_ge(w_lo0_ready, at(lay, 1, 1))
                for i in range(2):
                    project(i, (LO_HI,), first=False).then_inc(fullsem(("in", i)), 1)
                for i in range(2, N_IN):
                    n = i // 2
                    name = ("in", i)
                    if i % 2 == 0:
                        pe.wait_ge(w_lo_ready, at(lay, IN_SLOTS - 1, n))
                    before(pe, name, lay)
                    ins = project(i, (HI_HI, HI_LO, LO_HI))
                    ins.then_inc(fullsem(name), 1)

                    if i == QLAT + 1:
                        read_out(pe, ("in", KV), lay)
                        before(pe, ("ssq", 0), lay)
                        mm(B(("ssq", 0))[:, :], ones, sq_kv, start=True, stop=True).then_inc(fullsem(("ssq", 0)), 1)
                        pe.wait_ge(cconv_ready, at(lay, 2, 2))
                        before(pe, ("mean",), lay)
                        mm(B(("mean",))[:, :], ones, mix[:, YC], start=True, stop=False)
                        mm(B(("mean",))[:, :], ones, mix[:, YC + 1], start=False, stop=True)\
                            .then_inc(fullsem(("mean",)), 1)
                        read_out(pe, ("in", GQK), lay)
                        before(pe, ("rotD", 0), lay)
                        mm(B(("rotD", 0))[:, :], rot_d, gk, start=True, stop=True).then_inc(fullsem(("rotD", 0)), 1)
                    if i == GQQ + 1:
                        read_out(pe, ("in", QLAT), lay)
                        read_out(pe, ("in", QLAT + 1), lay)
                        before(pe, ("ssq", 1), lay)
                        mm(B(("ssq", 1))[:, :], ones, sq_q[0], start=True, stop=False)
                        mm(B(("ssq", 1))[:, :], ones, sq_q[1], start=False, stop=True)\
                            .then_inc(fullsem(("ssq", 1)), 1)
                    if i == GQV:
                        for j in range(2):
                            name = ("rotD", 1 + j)
                            read_out(pe, ("in", GQQ + j), lay)
                            before(pe, name, lay)
                            mm(B(name)[:, :], rot_d, gq[:, j], start=True, stop=True).then_inc(fullsem(name), 1)

                pe.wait_ge(csq_ready, at(lay, 2, 2))
                before(pe, ("var",), lay)
                mm(B(("var",))[:, :], ones, csq[:, 0], start=True, stop=False)\
                    .then_inc(chunk_free, 1)
                mm(B(("var",))[:, :], ones, csq[:, 1], start=False, stop=True).then_inc(fullsem(("var",)), 1)

                def window(n):
                    return max(n - 1, 0), min(n + 2, NT)

                def d_scores(i):
                    n, h = divmod(i, GQ_H)
                    lo, hi = window(n)
                    rows = slice(64 * (h // 2), 64 * (h // 2) + 64)
                    before(pe, ("SD", i), lay)
                    mm(B(("SD", i))[:, 0:(hi - lo) * P], gq[rows, h % 2, n * P:(n + 1) * P],
                       gk[rows, lo * P:hi * P], start=True, stop=True).then_inc(fullsem(("SD", i)), 1)

                read_out(pe, ("in", GQV), lay)
                transposed(("gvT",), lay, gv_turned, NT)

                pe.wait_ge(params_in, at(lay, 64, 64))
                pe.wait_ge(lat_ready, at(lay, 3, 3))
                for h in range(MLA_H):
                    name = ("qup", h)
                    before(pe, name, lay)
                    for k in range(2):
                        ins = mm(B(name)[0:QK, :], wq[:, k, h * QK:(h + 1) * QK], qlat[:, k],
                                 start=(k == 0), stop=(k == 1))
                    ins.then_inc(fullsem(name), 1)
                for j in range(2):
                    name = ("kup", j)
                    before(pe, name, lay)
                    for e in range(2):
                        h = 2 * j + e
                        ins = mm(B(name)[e * NOPE:(e + 1) * NOPE, :], wkv[:, h * NOPE:(h + 1) * NOPE], kvlat,
                                 start=True, stop=True)
                    ins.then_inc(fullsem(name), 1)
                for j in range(2):
                    name = ("vup", j)
                    before(pe, name, lay)
                    for e in range(2):
                        t = 2 * j + e
                        ins = mm(B(name)[:, e * 256:(e + 1) * 256], kvlat[:, t * P:(t + 1) * P],
                                 wkv[:, MLA_H * NOPE:], start=True, stop=True)
                    ins.then_inc(fullsem(name), 1)
                pe.wait_ge(rope_d_ready, at(lay, 3, 3))
                d_scores(0)
                d_scores(1)
                r = slice(NOPE, QK)
                before(pe, ("rotQ",), lay)
                for h in range(MLA_H):
                    read_out(pe, ("qup", h), lay)
                    pe.sem_inc(passed["pe"], 1)
                    ins = mm(B(("rotQ",))[ROPE * h:ROPE * (h + 1), :], rot_a[r, r], Qh[r, h, :], start=True, stop=True)
                ins.then_inc(fullsem(("rotQ",)), 1)
                read_out(pe, ("in", KROPE), lay)
                before(pe, ("rotK",), lay)
                pe.sem_inc(passed["pe"], 1)
                mm(B(("rotK",))[r, :], rot_a[r, r], Kh[r, 0, :], start=True, stop=True).then_inc(fullsem(("rotK",)), 1)

                def d_values(n, j):
                    lo, hi = window(n)
                    if n == 0:
                        before(pe, ("YD", j), lay)
                    for e in range(2):
                        read_out(pe, ("TD", n * GQ_H + 2 * j + e), lay)
                    for kb in range(hi - lo):
                        for e in range(2):
                            h = 2 * j + e
                            ins = mm(B(("YD", j))[64 * e:64 * e + 64, n * P:(n + 1) * P],
                                     gv[:, lo + kb, 64 * j:64 * j + 64], pt_d[:, h, kb * P:(kb + 1) * P],
                                     start=(kb == 0), stop=(kb == hi - lo - 1))
                    ins.then_inc(pvd_done if n < NT - 1 else fullsem(("YD", j)), 1)

                d_scores(2)
                read_out(pe, ("gvT",), lay)
                def a_scores(i):
                    h, t = 2 * (i // 8) + i % 2, i // 2 % NT
                    before(pe, ("SA", i), lay)
                    mm(B(("SA", i))[:, :], Qh[0:QK, h, t * P:(t + 1) * P], Kh[0:QK, h, :], start=True, stop=True)\
                        .then_inc(fullsem(("SA", i)), 1)

                for i in range(NT * GQ_H):
                    n, h = divmod(i, GQ_H)
                    lo, hi = window(n)
                    if i + 3 < NT * GQ_H:
                        d_scores(i + 3)
                    pe.wait_ge(dp_ready, at(lay, NT * GQ_H, i + 1))
                    before(pe, ("TD", i), lay)
                    for kb in range(hi - lo):
                        ins = nc.tensor.transpose(B(("TD", i))[:, kb * P:(kb + 1) * P],
                                                  p_d[:, h, kb * P:(kb + 1) * P], ident)
                    ins.then_inc(fullsem(("TD", i)), 1)
                    if i + 4 == NT * GQ_H:
                        pe.wait_ge(keys_ready, at(lay, 1, 1))
                        pe.wait_ge(queries_ready, at(lay, MLA_H, MLA_H))
                        for j in range(MLA_H // 2):
                            read_out(pe, ("kup", j), lay)
                        a_scores(0)
                    if i + 4 == NT * GQ_H + 1:
                        a_scores(1)
                    if i + 4 == NT * GQ_H + 2:
                        a_scores(2)
                    if h % 2 == 0 and i > 0:
                        d_values((i - 1) // GQ_H, (i - 1) % GQ_H // 2)

                def a_values(j, t):
                    if t == 0:
                        if j == 0:
                            read_out(pe, ("vup", 0), lay)
                            read_out(pe, ("vup", 1), lay)
                        before(pe, ("YA", j), lay)
                    for e in range(2):
                        read_out(pe, ("TA", 8 * j + 2 * t + e), lay)
                    for k in range(NT):
                        for e in range(2):
                            h = 2 * j + e
                            ins = mm(B(("YA", j))[64 * e:64 * e + 64, t * P:(t + 1) * P],
                                     V[:, k, h * VD:(h + 1) * VD], pt_a[:, (2 * t + e) % 4, k * P:(k + 1) * P],
                                     start=(k == 0), stop=(k == NT - 1))
                    ins.then_inc(pva_done if t < NT - 1 else fullsem(("YA", j)), 1)

                d_values(NT - 1, 1)
                for i in range(NT * MLA_H):
                    if 0 < i < NT * MLA_H - 4:
                        a_scores(i + 4)
                    pe.wait_ge(ap_ready, at(lay, NT * MLA_H, i + 1))
                    before(pe, ("TA", i), lay)
                    for k in range(NT):
                        ins = nc.tensor.transpose(B(("TA", i))[:, k * P:(k + 1) * P],
                                                  p_a[:, i % 4, k * P:(k + 1) * P], ident)
                    ins.then_inc(fullsem(("TA", i)), 1)
                    if i == 0:
                        for later in (3, 4):
                            a_scores(later)
                    if i % 2 == 0 and i > 0:
                        a_values((i - 2) // 8, (i - 2) // 2 % NT)
                a_values(1, NT - 1)

                def x1_turned(t):
                    for half in range(2):
                        pe.wait_ge(x1_ready, at(lay, 2 * NT, 2 * t + half + 1))
                        transposed(("x1T", t, half), lay, X[:, t, half * 512:half * 512 + 512], 4)

                def logits(t, retire=0):
                    for k in range(KD):
                        if k % 4 == 0:
                            read_out(pe, ("x1T", t, k // 4), lay)
                        ins = mm(B(("logits",))[:, t * N_EXP:(t + 1) * N_EXP], x1T[:, k, t * P:(t + 1) * P],
                                 wr[:, k, :], start=(k == 0), stop=(k == KD - 1))
                        if k == 0 and retire:
                            ins.then_inc(chunk_free, retire)
                    return ins

                pe.wait_ge(split_ready, at(lay, 4, 4))
                read_out(pe, ("YD", 0), lay)
                read_out(pe, ("YD", 1), lay)
                before(pe, ("logits",), lay)
                for t in range(NT):
                    for n in range(2):
                        name = ("mix", t, n)
                        before(pe, name, lay)
                        for number, k in enumerate(MIX_ORDER):
                            if t == 0 and n == 0 and k % 2 == 0:
                                pe.wait_ge(wout_lo_ready, at(lay, 4, number // 2 + 1))
                                if k == YA:
                                    read_out(pe, ("YA", 0), lay)
                                    read_out(pe, ("YA", 1), lay)
                            rows, cols = slice(t * P, (t + 1) * P), slice(n * 512, (n + 1) * 512)
                            hi, lo = (a[k // 2].rearrange("p (c f) -> p c f", c=2)[:, k % 2, cols]
                                      for a in (wout_hi, wout_low))
                            mm(B(name)[:, :], mix_hi[:, k, rows], hi, start=(number == 0), stop=False)
                            mm(B(name)[:, :], mix_hi[:, k, rows], lo, start=False, stop=False)
                            ins = mm(B(name)[:, :], mix_lo[:, k, rows], hi, start=False, stop=(number == 7))
                        ins.then_inc(fullsem(name), 1)
                        if t >= 1 and n == 0:
                            x1_turned(t - 1)
                    if t >= 1:
                        logits(t - 1, retire=LN1_AT - HI_AT if t == NT - 1 else 0)
                x1_turned(NT - 1)
                logits(NT - 1, retire=MOE_AT - LN1_AT).then_inc(fullsem(("logits",)), 1)

                pe.wait_ge(aff_ready, at(lay, 1, 1))
                before(pe, ("affT",), lay)
                for t in range(NT):
                    ins = nc.tensor.transpose(B(("affT",))[0:N_EXP, t * P:(t + 1) * P], aff[:, t, :], ident)
                ins.then_inc(fullsem(("affT",)), 1)
                pe.wait_ge(slots_ready, at(lay, 1, 1))
                before(pe, ("slotT",), lay)
                pe.sem_inc(passed["pe"], 1)
                for c, src in enumerate((slotf, vals)):
                    ins = nc.tensor.transpose(B(("slotT",))[:, c * N_EXP:(c + 1) * N_EXP],
                                              src[0:N_EXP].rearrange("p a b -> p (a b)"), ident[0:N_EXP, 0:N_EXP])
                ins.then_inc(fullsem(("slotT",)), 1)

                with pe.Fori(0, PAIRS // BODY_PAIRS) as body:
                    for b in range(BODY_PAIRS):
                        pair = body * BODY_PAIRS + b
                        at0 = MOE_AT + b * PAIR_CHUNKS
                        pe.wait_ge(xs_full[b], lay * (16 * PAIRS // 2) + body * 16 + 16)
                        for half in range(2):
                            transposed(("xsT", half), lay, xs[:, b, half * 512:half * 512 + 512], 4, pair)
                        for half in range(2):
                            read_out(pe, ("xsT", half), lay, pair)
                        for part, kind in enumerate("GU"):
                            for n in range(2):
                                before(pe, (kind, n), lay, pair)
                            for k in range(KD):
                                j = at0 + part * KD + k
                                slot_in(pe, lay, j, body)
                                w = ring[:, j % RING].rearrange("p (e f) -> p e f", e=2)
                                for n in range(2):
                                    for e in range(2):
                                        ins = mm(B((kind, n))[64 * e:64 * e + 64, :], xsT[:, k, 64 * e:64 * e + 64],
                                                 w[:, e, n * 512:(n + 1) * 512], start=(k == 0), stop=(k == KD - 1))
                                        if n == 0 and e == 0 and part + k > 0:
                                            ins.then_inc(chunk_free, 1)
                                    if k == KD - 1:
                                        ins.then_inc(fullsem((kind, n)), 1)
                        for half in range(2):
                            read_out(pe, ("U", half), lay, pair)
                            transposed(("hT", half), lay, hid[:, half * 512:half * 512 + 512], 4, pair,
                                       retire=1 if half == 0 else 0)
                        for half in range(2):
                            read_out(pe, ("hT", half), lay, pair)
                        for n in range(2):
                            before(pe, ("O", n), lay, pair)
                        for k in range(KD):
                            j = at0 + 2 * KD + k
                            slot_in(pe, lay, j, body)
                            w = ring[:, j % RING].rearrange("p (e f) -> p e f", e=2)
                            for n in range(2):
                                for e in range(2):
                                    ins = mm(B(("O", n))[64 * e:64 * e + 64, :], hidT[:, k, 64 * e:64 * e + 64],
                                             w[:, e, n * 512:(n + 1) * 512], start=(k == 0), stop=(k == KD - 1))
                                    if n == 0 and e == 0 and k > 0:
                                        ins.then_inc(chunk_free, 1)
                                if k == KD - 1:
                                    ins.then_inc(fullsem(("O", n)), 1)
                        pe.wait_ge(g_ready, lay * PAIRS + body * BODY_PAIRS + (b + 1))
                        for n in range(2):
                            read_out(pe, ("O", n), lay, pair)
                        for t in range(NT):
                            for n in range(2):
                                name = ("Y", t, n)
                                bank, nth = USES[name]
                                before(pe, name, lay, pair)
                                ins = mm(banks[bank][:, :], G[:, t * P:(t + 1) * P], o_sb[:, n * 512:(n + 1) * 512],
                                         start=True, stop=True)
                                if t == 0 and n == 0:
                                    ins.then_inc(bank_full[bank], 1)
                                elif t == 0 and n == 1:
                                    ins.then_inc(bank_full[bank], 1)
                                else:
                                    ins.then_inc(bank_full[bank], 1)
                        pe.wait_ge(bank_full[USES[("Y", 0, 0)][0]],
                                   bank_count(("Y", 0, 0), lay, 1, pair)[1])
                        pe.sem_inc(chunk_free, 1)

        @block.vector
        def _(v):
            step = Steps(v, dve_step)
            did, wait = step.did, step.wait

            def hold(s, n):
                v.wait_ge(s, n)
                v.sem_inc(passed["dve"], 1)

            nc.vector.memset(half_neg, -0.5)
            nc.vector.memset(c_rms, RMS_EPS)
            nc.vector.memset(c_ln, LN_EPS).then_inc(small_ready, 1)

            v.wait_ge(pos_in, 16)
            v.wait_ge(consts_in, 32)
            pos, ang, turns = trig[:, 0], trig[:, 1], trig[:, 2]
            sin_arg, cos_arg = trig[:, 3], trig[:, 4]
            did(nc.vector.tensor_copy(pos, trig[:, 5].bitcast(I32)))
            wait()
            did(nc.vector.tensor_scalar(ang, pos, freq, None, ALU.mult))
            wait()
            for arg, quarter in ((sin_arg, 0.0), (cos_arg, 0.25)):
                did(nc.vector.tensor_scalar(turns, ang, float(1 / (2 * np.pi)), quarter, ALU.mult, ALU.add))
                wait()
                did(nc.vector.tensor_scalar(turns, turns, ROUND, None, ALU.add))
                wait()
                did(nc.vector.tensor_scalar(turns, turns, ROUND, None, ALU.subtract))
                wait()
                src = ang
                for c in (TWO_PI_1, TWO_PI_2, TWO_PI_3):
                    did(nc.vector.scalar_tensor_tensor(out=arg, in0=turns, scalar=-c, in1=src,
                                                       op0=ALU.mult, op1=ALU.add))
                    wait()
                    src = arg
                did(nc.vector.tensor_scalar(arg, arg, 2 * np.pi * quarter, PI_BELOW, ALU.add, ALU.min))
                wait()
                nc.vector.tensor_scalar(arg, arg, -PI_BELOW, None, ALU.max).then_inc(angles_ready, 1)
                wait()
            v.wait_ge(sines_ready, 2)
            every_second = [2 * (i % 16) for i in range(32)]
            nc.vector.stream_shuffle(sin_a[:], sin_d[:], every_second).then_inc(trig_ready, 1)
            nc.vector.stream_shuffle(cos_a[:], cos_d[:], every_second).then_inc(trig_ready, 1)
            v.wait_ge(trig_ready, 2)

            def half_stats(t, n):
                did(nc.vector.bn_stats(bn[:, t, 6 * n:6 * n + 6], X[:, t, n * 512:(n + 1) * 512]))

            def variance(lay, t, second):
                wait()
                nc.vector.bn_aggr(mv[:, t, :], bn[:, t, :]).then_inc(var_ready, 1)
                v.wait_ge(var_ready, at(lay, 2 * NT, 4 * second + t + 1))

            def layer_norm(lay, t, gains, second, done):
                k = 4 * second + t
                for n in range(2):
                    cols = slice(n * 512, (n + 1) * 512)
                    did(nc.vector.scalar_tensor_tensor(out=X[:, t, cols], in0=X[:, t, cols], scalar=mv[:, t, 0:1],
                                                       in1=gains[:, cols], op0=ALU.subtract, op1=ALU.mult))
                hold(rstd_ready, at(lay, 2 * NT, k + 1))
                for n in range(2):
                    cols = slice(n * 512, (n + 1) * 512)
                    v.wait_ge(dve_step, step.n - 1 + n)
                    nc.vector.scalar_tensor_tensor(out=X[:, t, cols], in0=X[:, t, cols], scalar=rstd[:, t:t + 1],
                                                   in1=gains[:, D + n * 512:D + (n + 1) * 512],
                                                   op0=ALU.mult, op1=ALU.add).then_inc(done, 1)

            with v.Fori(0, DEPTH) as lay:
                step.restart()
                for place in (2, 0, 1, 3):
                    t = TILE_ORDER[place]
                    for half in range(2):
                        name = ("xT", t, half)
                        cols = (slice(4 * half, 4 * half + 4), slice(t * P, (t + 1) * P))
                        v.wait_ge(x_hi_ready, at(lay, 2 * NT, 2 * place + half + 1))
                        nc.vector.tensor_tensor(x_lo[:, cols[0], cols[1]],
                                                B(name)[:, :].rearrange("p (c f) -> p c f", c=4),
                                                x_hi[:, cols[0], cols[1]].bitcast(F32), ALU.subtract)\
                            .then_inc(freesem(name), 1)
                v.wait_ge(w_hi_ready, at(lay, IN_SLOTS, 1))
                nc.vector.tensor_tensor(w_lo[:, 0], ring[:, 0], w_hi[:, 0].bitcast(F32), ALU.subtract)\
                    .then_inc(w_lo0_ready, 1)
                hold(x_stored, at(lay, 16 * NT, 16 * NT))
                full(v, ("in", 0), lay)
                v.sem_inc(passed["dve"], 1)
                pad = CF_K // 2
                did(nc.vector.memset(u[:, :, 0:pad], 0.0))
                did(nc.vector.memset(u[:, :, pad + S:], 0.0))
                did(nc.vector.memset(prod[:, :, 0:1], 0.0))
                did(nc.vector.memset(prod[:, :, S + 1:], 0.0))
                for j in range(2):
                    read_out(v, ("in", CF_G + j), lay)
                    v.sem_inc(passed["dve"], 1)
                    full(v, ("in", CF_A + j), lay)
                    nc.vector.scalar_tensor_tensor(out=u[:, j, pad:pad + S], in0=mix[:, YC + j], scalar=1.0,
                                                   in1=B(("in", CF_A + j))[:, :], op0=ALU.add, op1=ALU.mult)\
                        .then_inc(freesem(("in", CF_A + j)), 1)
                hold(params_in, at(lay, 64, 64))
                for j in range(2):
                    read_out(v, ("in", CF_A + j), lay)
                wait()
                for j in range(2):
                    c = PAR["cconv"] + j * CF_K
                    did(nc.vector.tensor_scalar(mix[:, YC + j], u[:, j, 0:S], par[:, c:c + 1], None, ALU.mult))
                start = step.n
                with v.Fori(1, CF_K) as tap:
                    for j in range(2):
                        v.wait_ge(dve_step, tap * 2 + (start - 3 + j))
                        nc.vector.scalar_tensor_tensor(
                            out=mix[:, YC + j], in0=u[:, j, bass.ds(tap, S)],
                            scalar=par[:, bass.ds(tap + (PAR["cconv"] + j * CF_K), 1)],
                            in1=mix[:, YC + j], op0=ALU.mult, op1=ALU.add).then_inc(dve_step, 1)
                step.n += 2 * (CF_K - 1)
                wait()
                for j in range(2):
                    c = PAR["cconv_b"] + j
                    nc.vector.tensor_scalar(mix[:, YC + j], mix[:, YC + j], 0.5, par[:, c:c + 1], ALU.mult, ALU.add)\
                        .then_inc(cconv_ready, 1)
                did(nc.vector.tensor_scalar(halfgb, par[:, PAR["cnorm_g"]:PAR["cnorm_g"] + 4], 0.5, None, ALU.mult))
                hold(prod_ready, at(lay, 2, 2))
                for k in range(SC_K):
                    for j in range(2):
                        c = PAR["sconv"] + j * SC_K + k
                        if k == 0:
                            did(nc.vector.tensor_scalar(scc[:, j], prod[:, j, 0:S], par[:, c:c + 1], None, ALU.mult))
                        else:
                            v.wait_ge(dve_step, step.n - 1 if (j == 0 or k < SC_K - 1) else step.n)
                            ins = nc.vector.scalar_tensor_tensor(
                                out=scc[:, j], in0=prod[:, j, k:k + S], scalar=par[:, c:c + 1],
                                in1=scc[:, j], op0=ALU.mult, op1=ALU.add)
                            if k < SC_K - 1:
                                did(ins)
                            else:
                                ins.then_inc(sconv_ready, 1)
                for j in range(2):
                    full(v, ("mean",), lay)
                    v.sem_inc(passed["dve"], 1)
                    v.wait_ge(cconv_ready, at(lay, 2, 2))
                    nc.vector.scalar_tensor_tensor(
                        out=mix[:, YC + j], in0=B(("mean",))[:, :], scalar=-1.0 / CF_W, in1=mix[:, YC + j],
                        op0=ALU.mult, op1=ALU.add).then_inc(freesem(("mean",)) if j else cdev_ready, 1)
                v.wait_ge(rnorm_ready, at(lay, 3, 1))
                nc.vector.scalar_tensor_tensor(out=kvlat, in0=kvlat, scalar=par[:, PAR["kv_g"]:PAR["kv_g"] + 1],
                                               in1=r_kv, op0=ALU.mult, op1=ALU.mult).then_inc(lat_ready, 1)
                hold(yb_ready, at(lay, 2, 2))
                full(v, ("rotD", 0), lay)
                nc.vector.tensor_tensor(tmp_d[:, 0], B(("rotD", 0))[:, :], sin_d[:], ALU.mult)\
                    .then_inc(freesem(("rotD", 0)), 1)
                v.wait_ge(rnorm_ready, at(lay, 3, 2))
                for j in range(2):
                    c = PAR["q_g"] + j
                    nc.vector.scalar_tensor_tensor(out=qlat[:, j], in0=qlat[:, j], scalar=par[:, c:c + 1], in1=r_q,
                                                   op0=ALU.mult, op1=ALU.mult).then_inc(lat_ready, 1)
                for j in range(2):
                    name = ("rotD", 1 + j)
                    full(v, name, lay)
                    nc.vector.tensor_tensor(tmp_d[:, 1 + j], B(name)[:, :], sin_d[:], ALU.mult)\
                        .then_inc(freesem(name), 1)
                v.wait_ge(rnorm_ready, at(lay, 3, 3))
                for j in range(2):
                    did(nc.vector.tensor_tensor(mix[:, YC + j], mix[:, YC + j], crs, ALU.mult))
                wait()
                for j in range(2):
                    nc.vector.tensor_scalar(mix[:, YC + j], mix[:, YC + j], halfgb[:, j:j + 1], halfgb[:, 2 + j:3 + j],
                                            ALU.mult, ALU.add).then_inc(z_ready, 1)
                v.wait_ge(th_ready, at(lay, 2, 2))
                for j in range(2):
                    nc.vector.scalar_tensor_tensor(out=mix[:, YC + j], in0=csq[:, j], scalar=1.0, in1=mix[:, YC + j],
                                                   op0=ALU.add, op1=ALU.mult).then_inc(yc_ready, 1)

                def d_width(n):
                    return (0 if n > 0 else P), ((min(n + 2, NT) - max(n - 1, 0)) * P)

                def d_max(i):
                    n, h = divmod(i, GQ_H)
                    off, w = d_width(n)
                    if i >= GQ_H:
                        full(v, ("TD", i - GQ_H), lay)
                        v.sem_inc(passed["dve"], 1)
                    full(v, ("SD", i), lay)
                    v.sem_inc(passed["dve"], 1)
                    ins = nc.vector.tensor_tensor_reduce(p_d[:, h, 0:w], B(("SD", i))[:, 0:w], band[:, off:off + w],
                                                         1.0, -3.0e38, ALU.add, ALU.max, mx[:, i:i + 1])
                    ins.then_inc(freesem(("SD", i)), 1)
                    read_out(v, ("SD", i), lay)
                    c = PAR["sink"] + h
                    nc.vector.tensor_scalar(nmx[:, i:i + 1], mx[:, i:i + 1], par[:, c:c + 1], -1.0,
                                            ALU.max, ALU.mult).then_inc(dmax_ready, 1)

                def d_norm(i):
                    n, h = divmod(i, GQ_H)
                    off, w = d_width(n)
                    v.wait_ge(dexp_done, at(lay, NT * GQ_H, i + 1))
                    did(nc.vector.tensor_tensor(rs[:, i:i + 1], rs[:, i:i + 1], snk[:, i:i + 1], ALU.add))
                    wait()
                    did(nc.vector.reciprocal(rinv[:, i:i + 1], rs[:, i:i + 1]))
                    wait()
                    nc.vector.tensor_scalar(p_d[:, h, 0:w], p_d[:, h, 0:w], rinv[:, i:i + 1], None, ALU.mult)\
                        .then_inc(dp_ready, 1)

                hold(rope_d_ready, at(lay, 3, 3))
                def a_max(i):
                    full(v, ("SA", i), lay)
                    v.sem_inc(passed["dve"], 1)
                    nc.vector.tensor_reduce(nmx[:, i:i + 1], B(("SA", i))[:, :], AX_X, ALU.max, negate=True)\
                        .then_inc(amax_ready, 1)

                def a_norm(i):
                    read_out(v, ("SA", i), lay)
                    did(nc.vector.reciprocal(rinv[:, i:i + 1], rs[:, i:i + 1]))
                    wait()
                    nc.vector.tensor_scalar(p_a[:, i % 4], p_a[:, i % 4], rinv[:, i:i + 1], None, ALU.mult)\
                        .then_inc(ap_ready, 1)

                r = slice(NOPE, QK)

                def k_rope():
                    tmp = mix[r, YA]
                    hold(cos_a_done, at(lay, 3, 1))
                    full(v, ("rotK",), lay)
                    nc.vector.tensor_tensor(tmp, B(("rotK",))[r, :], sin_a[r, :], ALU.mult)\
                        .then_inc(freesem(("rotK",)), 1)
                    read_out(v, ("rotK",), lay)
                    nc.vector.tensor_tensor(Kh[r, 0, :], Kh[r, 0, :], tmp, ALU.add).then_inc(rope_k_ready, 1)

                def q_rope(h):
                    tmp = mix[r, YA + (h + 1) % 2]
                    if h % 2 == 0:
                        hold(cos_a_done, at(lay, 3, 2 + h // 2))
                    own = slice(ROPE * h, ROPE * (h + 1))
                    full(v, ("rotQ",), lay)
                    v.sem_inc(passed["dve"], 1)
                    ins = nc.vector.tensor_tensor(tmp, B(("rotQ",))[own, :], sin_a[own, :], ALU.mult)
                    if h < MLA_H - 1:
                        did(ins)
                        wait()
                    else:
                        ins.then_inc(freesem(("rotQ",)), 1)
                        read_out(v, ("rotQ",), lay)
                    nc.vector.tensor_tensor(Qh[r, h, :], Qh[r, h, :], tmp, ALU.add).then_inc(queries_ready, 1)

                d_max(0)
                d_max(1)
                for i in range(NT * GQ_H):
                    if i + 2 < NT * GQ_H:
                        d_max(i + 2)
                    else:
                        a_max(i + 2 - NT * GQ_H)
                    d_norm(i)
                    if i == 1:
                        k_rope()
                    elif i % 2 == 1 and i <= 2 * MLA_H + 1:
                        q_rope(i // 2 - 1)
                def mix_low(name, k, n):
                    v.wait_ge(mix_hi_ready, at(lay, 4, n))
                    nc.vector.tensor_tensor(mix_lo[:, k], B(name)[:, :], mix_hi[:, k].bitcast(F32), ALU.subtract)\
                        .then_inc(freesem(name), 1)

                a_norm(0)
                a_max(2)
                for j in range(2):
                    mix_low(("YD", j), YD + j, j + 1)
                for i in range(1, NT * MLA_H):
                    if i + 2 < NT * MLA_H:
                        a_max(i + 2)
                    a_norm(i)
                for j in range(2):
                    mix_low(("YA", j), YA + j, 3 + j)

                ln1_gb = ring[:, LN1_AT % RING]
                hold(x_back, at(lay, 16, 16))
                slot_in(v, lay, LN1_AT)
                v.sem_inc(passed["dve"], 1)
                for t in range(NT):
                    for n in range(2):
                        name = ("mix", t, n)
                        full(v, name, lay)
                        cols = slice(n * 512, (n + 1) * 512)
                        nc.vector.scalar_tensor_tensor(out=X[:, t, cols], in0=X[:, t, cols], scalar=ALPHA,
                                                       in1=B(name)[:, :], op0=ALU.mult, op1=ALU.add)\
                            .then_inc(freesem(name), 1)
                        read_out(v, name, lay)
                        v.sem_inc(passed["dve"], 1)
                        half_stats(t, n)
                    variance(lay, t, 0)
                    layer_norm(lay, t, ln1_gb, 0, x1_ready)

                lg = aff
                full(v, ("logits",), lay)
                v.sem_inc(passed["dve"], 1)
                lgp = B(("logits",))[:, 0:NT * N_EXP].rearrange("p (t e) -> p t e", e=N_EXP)
                br = par[:, PAR["b_router"]:PAR["b_router"] + N_EXP].unsqueeze(1).broadcast_to([P, NT, N_EXP])
                nc.vector.tensor_tensor(lg, lgp, br, ALU.add).then_inc(freesem(("logits",)), 1)
                read_out(v, ("logits",), lay)
                v.sem_inc(passed["dve"], 1)
                did(nc.vector.tensor_reduce(lmax, lg, AX_X, ALU.max))
                wait()
                nc.vector.tensor_tensor(lg, lg, lmax.unsqueeze(2).broadcast_to([P, NT, N_EXP]), ALU.subtract)\
                    .then_inc(lsub_ready, 1)
                hold(lexp_done, at(lay, 1, 1))
                did(nc.vector.tensor_reduce(lsum, lg, AX_X, ALU.add))
                wait()
                did(nc.vector.reciprocal(lsum, lsum))
                wait()
                nc.vector.tensor_tensor(lg, lg, lsum.unsqueeze(2).broadcast_to([P, NT, N_EXP]), ALU.mult)\
                    .then_inc(aff_ready, 1)
                full(v, ("affT",), lay)
                nc.vector.tensor_copy(aff2[0:N_EXP, 0], B(("affT",))[0:N_EXP, :]).then_inc(freesem(("affT",)), 1)
                read_out(v, ("affT",), lay)
                v.sem_inc(passed["dve"], 1)
                for r8 in range(CAP // 8):
                    src, nxt = aff2[0:N_EXP, r8 % 2], aff2[0:N_EXP, (r8 + 1) % 2]
                    top = vals[0:N_EXP, 0, 8 * r8:8 * r8 + 8]
                    did(nc.vector.max(top, src))
                    wait()
                    if r8 < CAP // 8 - 1:
                        did(nc.vector.match_replace(nxt, top, src, -1.0))
                    did(nc.vector.max_index(idx[0:N_EXP, 8 * r8:8 * r8 + 8], top, src))
                    v.wait_ge(dve_step, step.n - 1)
                wait()
                did(nc.vector.tensor_copy(slotf[0:N_EXP, 0, :], idx[0:N_EXP, :]))
                did(nc.vector.tensor_copy(slotf[0:N_EXP, 1, :], idx[0:N_EXP, :]))
                did(nc.vector.tensor_copy(vals[0:N_EXP, 1, :], vals[0:N_EXP, 0, :]))
                wait()
                v.sem_inc(slots_ready, 1)
                full(v, ("slotT",), lay)
                v.sem_inc(passed["dve"], 1)
                for c, dst in enumerate((slot_f, slot_gate)):
                    src = B(("slotT",))[:, c * N_EXP:(c + 1) * N_EXP].rearrange("p (q e) -> p q e", e=2)
                    for e in range(2):
                        rows = slice(64 * e, 64 * e + 64)
                        ins = nc.vector.tensor_copy(dst[rows, :], src[rows, :, e])
                        if (c, e) != (1, 1):
                            did(ins)
                        else:
                            ins.then_inc(freesem(("slotT",)), 1)
                wait()
                nc.vector.tensor_copy(slot_i[:], slot_f).then_inc(route_ready, 1)

                hold(y_init, at(lay, NT, NT))

                def expert_pair(pair, last=False):
                    for n in range(2):
                        cols = slice(n * 512, (n + 1) * 512)
                        read_out(v, ("G", n), lay, pair)
                        v.sem_inc(passed["dve"], 1)
                        full(v, ("U", n), lay, pair)
                        nc.vector.tensor_tensor(hid[:, cols], hid[:, cols], B(("U", n))[:, :], ALU.mult)\
                            .then_inc(freesem(("U", n)), 1)
                    nc.vector.tensor_scalar(G, slot_iota[:], slot_f[:, bass.ds(pair, 1)],
                                            slot_gate[:, bass.ds(pair, 1)], ALU.is_equal, ALU.mult)\
                        .then_inc(g_ready, 1)
                    full(v, ("O", 1), lay, pair)
                    nc.vector.tensor_copy(o_sb[:, 512:1024], B(("O", 1))[:, :]).then_inc(freesem(("O", 1)), 1)
                    for t in range(NT):
                        for n in range(2):
                            name = ("Y", t, n)
                            cols = slice(n * 512, (n + 1) * 512)
                            full(v, name, lay, pair)
                            nc.vector.tensor_tensor(X[:, t, cols], X[:, t, cols], B(name)[:, :], ALU.add)\
                                .then_inc(freesem(name), 1)
                            if last:
                                if n == 1:
                                    for half in range(2):
                                        read_out(v, ("Y", t, half), lay, pair)
                                        v.sem_inc(passed["dve"], 1)
                                        half_stats(t, half)
                                if (t, n) == (3, 0):
                                    v.wait_ge(ln2_in, at(lay, 16, 16))
                                    v.sem_inc(passed["dve"], 1)
                                    layer_norm(lay, 2, ln2_gb, 1, x_ready)
                        if last:
                            variance(lay, t, 1)
                    if last:
                        hold(gained, at(lay, 2, 2))
                        nc.vector.tensor_tensor(X[:, 1], X[:, 1], ln2_gb[:, D:2 * D], ALU.add).then_inc(x_ready, 2)
                        layer_norm(lay, NT - 1, ln2_gb, 1, x_ready)

                with v.Fori(0, PAIRS // BODY_PAIRS - 1) as body:
                    for b in range(BODY_PAIRS):
                        expert_pair(body * BODY_PAIRS + b)
                expert_pair(PAIRS - 2)
                expert_pair(PAIRS - 1, last=True)

        @block.scalar
        def _(ac):
            step = Steps(ac, act_step)
            did, wait = step.did, step.wait
            act = nc.scalar.activation

            ac.dma_start(trig[:, 5].bitcast(I32), positions.partition_broadcast(P)).then_inc(pos_in, 16)
            for t in range(NT):
                ac.dma_start(X[:, t], x_in[t * P:(t + 1) * P]).then_inc(x_in_sem, 16)
            nc.scalar.preload_act_table(ACT.Sin)
            ac.wait_ge(angles_ready, 1)
            act(sin_d[:], trig[:, 3], ACT.Sin).then_inc(sines_ready, 1)
            ac.wait_ge(angles_ready, 2)
            act(cos_d[:], trig[:, 4], ACT.Sin).then_inc(sines_ready, 1)
            ac.wait_ge(sines_ready, 2)
            ac.wait_ge(small_ready, 1)

            with ac.Fori(0, DEPTH) as lay:
                step.restart()
                def arrived(i):
                    if i % 2 == 1 and 3 <= i < 2 * IN_SLOTS - 3:
                        w_high((i + 3) // 2)

                def w_high(n):
                    if n >= 2:
                        full(ac, ("in", 2 * n - 3), lay)
                    slot_in(ac, lay, n)
                    act(w_hi[:, n % 2], ring[:, n], ACT.Copy).then_inc(w_hi_ready, 1)

                for place, t in enumerate(TILE_ORDER):
                    if place == 2:
                        w_high(0)
                    for half in range(2):
                        name = ("xT", t, half)
                        full(ac, name, lay)
                        act(x_hi[:, 4 * half:4 * half + 4, t * P:(t + 1) * P],
                            B(name)[:, :].rearrange("p (c f) -> p c f", c=4), ACT.Copy).then_inc(x_hi_ready, 1)
                w_high(1)
                nc.scalar.preload_act_table_set("exp_and_others")
                ac.wait_ge(x_stored, at(lay, 16 * NT, 16 * NT))
                ac.dma_start(par[:], params[lay]).then_inc(params_in, 16)
                ac.dma_start(wq[:], w_uq[lay].rearrange("(c p) f -> p c f", p=P)).then_inc(params_in, 16)
                ac.dma_start(wkv[:], w_ukv[lay]).then_inc(params_in, 16)
                ac.dma_start(wr[:], w_router[lay].rearrange("(c p) f -> p c f", p=P)).then_inc(params_in, 16)

                def copy_out(name, dst, src=None, scale=1.0, frees=True):
                    if name[0] == "in":
                        arrived(name[1])
                    full(ac, name, lay)
                    ins = act(dst, B(name)[:, :] if src is None else src, ACT.Copy, scale=scale)
                    if frees:
                        ins.then_inc(freesem(name), 1)
                    return ins

                for j in range(2):
                    name = ("in", CF_G + j)
                    if j == 1:
                        w_high(2)
                    full(ac, name, lay)
                    act(mix[:, YC + j], B(name)[:, :], ACT.Tanh, scale=0.5).then_inc(freesem(name), 1)
                nc.scalar.preload_act_table_set("natural_log_exp_and_others")
                arrived(CF_A + 1)
                for j in range(2):
                    copy_out(("in", SC_C + j), scc[:, j])
                for j in range(2):
                    copy_out(("in", SC_H + j), prod[:, j, 1:1 + S])
                for j in range(2):
                    copy_out(("in", SC_B + j), mix[:, YB + j])
                copy_out(("in", KV), kvlat, frees=False)
                act(sq_kv, B(("in", KV))[:, :], ACT.Square).then_inc(freesem(("in", KV)), 1)
                copy_out(("in", GQK), gk)
                for j in range(2):
                    name = ("in", QLAT + j)
                    copy_out(name, qlat[:, j], frees=False)
                    act(sq_q[j], B(name)[:, :], ACT.Square).then_inc(freesem(name), 1)

                def inverse_root(name, dst, n, eps):
                    full(ac, name, lay)
                    act(dst, B(name)[:, :], ACT.Ln, scale=1.0 / n, bias=eps).then_inc(freesem(name), 1)
                    read_out(ac, name, lay)
                    act(dst, dst, ACT.Exp, scale=-0.5).then_inc(rnorm_ready, 1)

                inverse_root(("ssq", 0), r_kv, KV_RANK, c_rms)
                for j in range(2):
                    copy_out(("in", GQQ + j), gq[:, j], scale=GQ_SCALE)
                for j in range(2):
                    read_out(ac, ("mean",), lay)
                    act(csq[:, j], mix[:, YC + j], ACT.Square).then_inc(csq_ready, 1)
                inverse_root(("ssq", 1), r_q, Q_RANK, c_rms)
                copy_out(("in", GQV), gv_turned)
                copy_out(("in", KROPE), Kh[NOPE:QK, 0, :], B(("in", KROPE))[NOPE:QK, :])
                inverse_root(("var",), crs, CF_W, c_ln)
                nc.scalar.preload_act_table_set("exp_and_others")
                copy_out(("gvT",), gv[:].rearrange("p t f -> p (t f)"))
                for h in range(MLA_H):
                    copy_out(("qup", h), Qh[0:QK, h, :], B(("qup", h))[0:QK, :], scale=MLA_SCALE)
                for j in range(2):
                    ac.wait_ge(z_ready, at(lay, 2, 2))
                    act(csq[:, j], mix[:, YC + j], ACT.Tanh).then_inc(th_ready, 1)
                for j in range(2):
                    for e in range(2):
                        copy_out(("kup", j), Kh[0:NOPE, 2 * j + e, :], B(("kup", j))[64 * e:64 * e + 64, :],
                                 frees=(e == 1))
                for j in range(2):
                    copy_out(("vup", j), V[:, 2 * j:2 * j + 2, :].rearrange("p t f -> p (t f)"))

                def d_exp(i):
                    n, h = divmod(i, GQ_H)
                    w = (min(n + 2, NT) - max(n - 1, 0)) * P
                    ac.wait_ge(dmax_ready, at(lay, NT * GQ_H, i + 1))
                    did(act(p_d[:, h, 0:w], p_d[:, h, 0:w], ACT.Exp, bias=nmx[:, i:i + 1], accum_out=rs[:, i:i + 1]))
                    c = PAR["sink"] + h
                    wait()
                    act(snk[:, i:i + 1], par[:, c:c + 1], ACT.Exp, bias=nmx[:, i:i + 1]).then_inc(dexp_done, 1)

                def d_turned(i):
                    n, h = divmod(i, GQ_H)
                    w = (min(n + 2, NT) - max(n - 1, 0)) * P
                    if i == 0:
                        ac.wait_ge(yc_ready, at(lay, 2, 2))
                        ac.wait_ge(yb_ready, at(lay, 2, 2))
                    if n > 0:
                        ac.wait_ge(pvd_done, at(lay, 2 * (NT - 1), 2 * (n - 1) + h // 2 + 1))
                    full(ac, ("TD", i), lay)
                    act(pt_d[:, h, 0:w], B(("TD", i))[:, 0:w], ACT.Copy).then_inc(freesem(("TD", i)), 1)

                def a_exp(i):
                    if i < 3:
                        full(ac, ("TD", NT * GQ_H - 3 + i), lay)
                    elif i > 3:
                        full(ac, ("TA", i - 4), lay)
                    ac.wait_ge(amax_ready, at(lay, NT * MLA_H, i + 1))
                    act(p_a[:, i % 4], B(("SA", i))[:, :], ACT.Exp, bias=nmx[:, i:i + 1],
                        accum_out=rs[:, i:i + 1]).then_inc(freesem(("SA", i)), 1)

                def a_turned(i):
                    if i == 0:
                        full(ac, ("YD", 0), lay)
                        full(ac, ("YD", 1), lay)
                    if i >= 4:
                        j, t = (i - 4) // 8, (i - 4) // 2 % NT
                        if t < NT - 1:
                            ac.wait_ge(pva_done, at(lay, 2 * (NT - 1), (NT - 1) * j + t + 1))
                        else:
                            full(ac, ("YA", j), lay)
                    full(ac, ("TA", i), lay)
                    act(pt_a[:, i % 4], B(("TA", i))[:, :], ACT.Copy).then_inc(freesem(("TA", i)), 1)

                def wout_high(n):
                    j = MIX_ORDER[2 * n] // 2
                    slot_in(ac, lay, WOUT_AT + j)
                    act(wout_hi[j], ring[:, (WOUT_AT + j) % RING], ACT.Copy).then_inc(wout_hi_ready, 1)

                def mix_high(name, k):
                    full(ac, name, lay)
                    act(mix_hi[:, k], B(name)[:, :], ACT.Copy).then_inc(mix_hi_ready, 1)

                d_exp(0)
                d_exp(1)
                for i in range(NT * GQ_H):
                    if i + 2 < NT * GQ_H:
                        d_exp(i + 2)
                    else:
                        a_exp(i + 2 - NT * GQ_H)
                    d_turned(i)
                    if i % 3 == 2 and i < 12:
                        wout_high(i // 3)
                for j in range(2):
                    mix_high(("YD", j), YD + j)
                a_turned(0)
                a_exp(2)
                for i in range(1, NT * MLA_H):
                    if i + 2 < NT * MLA_H:
                        a_exp(i + 2)
                    a_turned(i)
                    if i == 11:
                        mix_high(("YA", 0), YA)
                mix_high(("YA", 1), YA + 1)
                ac.dma_start(X[:], out.rearrange("(t p) f -> p t f", p=P)).then_inc(x_back, 16)

                def x1_turned(t):
                    ac.wait_ge(x1_ready, at(lay, 2 * NT, 2 * t + 2))
                    ac.dma_start(x1_rows[t * P:(t + 1) * P], X[:, t]).then_inc(x1_stored, 16)
                    for half in range(2):
                        name = ("x1T", t, half)
                        full(ac, name, lay)
                        act(x1T[:, 4 * half:4 * half + 4, t * P:(t + 1) * P],
                            B(name)[:, :].rearrange("p (c f) -> p c f", c=4), ACT.Copy).then_inc(freesem(name), 1)

                for t in range(NT):
                    x1_turned(t)
                ac.wait_ge(lsub_ready, at(lay, 1, 1))
                act(aff, aff, ACT.Exp).then_inc(lexp_done, 1)
                nc.scalar.preload_act_table(ACT.Silu)
                ac.wait_ge(x1_stored, at(lay, 16 * NT, 16 * NT))
                for t in range(NT):
                    act(X[:, t], X[:, t], ACT.Copy, scale=ALPHA).then_inc(y_init, 1)
                ac.wait_ge(xs_full[0], at(lay, 16 * PAIRS // 2, 16))
                ac.dma_start(ln2_gb, ln2[lay].partition_broadcast(P)).then_inc(ln2_in, 16)

                with ac.Fori(0, PAIRS // BODY_PAIRS) as body:
                    for b in range(BODY_PAIRS):
                        pair = body * BODY_PAIRS + b

                        def quarter_copies(kind, dst):
                            for half in range(2):
                                full(ac, (kind, half), lay, pair)
                                act(dst[:, 4 * half:4 * half + 4, :].rearrange("p c f -> p (c f)"),
                                    B((kind, half))[:, :], ACT.Copy).then_inc(freesem((kind, half)), 1)

                        quarter_copies("xsT", xsT)
                        for n in range(2):
                            full(ac, ("G", n), lay, pair)
                            act(hid[:, n * 512:(n + 1) * 512], B(("G", n))[:, :], ACT.Silu)\
                                .then_inc(freesem(("G", n)), 1)
                        quarter_copies("hT", hidT)
                        full(ac, ("O", 0), lay, pair)
                        act(o_sb[:, 0:512], B(("O", 0))[:, :], ACT.Copy).then_inc(freesem(("O", 0)), 1)

                for t in range(2):
                    ac.wait_ge(nmr_ready, at(lay, 2, t + 1))
                    act(X[:, t], X[:, t], ACT.Identity, scale=rstd[:, t:t + 1], bias=nmr[:, t:t + 1])\
                        .then_inc(centred, 1)
            ac.wait_ge(x_stored, 16 * NT * (DEPTH + 1))
            ac.wait_ge(x1_stored, 16 * NT * DEPTH)

        @block.gpsimd
        def _(g):
            step = Steps(g, pool_step)
            did, wait = step.did, step.wait
            tt = nc.gpsimd.tensor_tensor

            def hold(s, n):
                g.wait_ge(s, n)
                g.sem_inc(passed["pool"], 1)

            hold(x_in_sem, 16 * NT)
            for t in range(NT):
                g.dma_start(out[t * P:(t + 1) * P], X[:, t]).then_inc(x_stored, 16)
            g.wait_ge(small_ready, 1)
            g.wait_ge(trig_ready, 2)

            def mean_part(lay, t):
                hold(rstd_ready, at(lay, 2 * NT, NT + t + 1))
                nc.gpsimd.tensor_scalar(nmr[:, t:t + 1], mv[:, t, 0:1], rstd[:, t:t + 1], -1.0, ALU.mult, ALU.mult)\
                    .then_inc(nmr_ready, 1)

            def inverse_deviation(lay, t, second):
                hold(var_ready, at(lay, 2 * NT, 4 * second + t + 1))
                did(nc.gpsimd.tensor_scalar(rstd[:, t:t + 1], mv[:, t, 1:2], LN_EPS, None, ALU.add))
                wait()
                tt(rstd[:, t:t + 1], rstd[:, t:t + 1], half_neg, ALU.pow).then_inc(rstd_ready, 1)

            with g.Fori(0, DEPTH) as lay:
                step.restart()
                def w_low(n):
                    hold(w_hi_ready, at(lay, IN_SLOTS, n + 1))
                    tt(w_lo[:, n], ring[:, n], w_hi[:, n % 2].bitcast(F32), ALU.subtract)\
                        .then_inc(w_lo_ready, 1)

                for n in range(1, 6):
                    w_low(n)
                for j in range(2):
                    hold(freesem(("in", SC_C + j)), bank_count(("in", SC_C + j), lay, 2, 0)[1])
                    hold(freesem(("in", SC_H + j)), bank_count(("in", SC_H + j), lay, 2, 0)[1])
                    tt(prod[:, j, 1:1 + S], prod[:, j, 1:1 + S], scc[:, j], ALU.mult).then_inc(prod_ready, 1)
                for n in range(6, IN_SLOTS):
                    w_low(n)
                hold(sconv_ready, at(lay, 2, 2))
                for j in range(2):
                    hold(freesem(("in", SC_B + j)), bank_count(("in", SC_B + j), lay, 2, 0)[1])
                    tt(mix[:, YB + j], mix[:, YB + j], scc[:, j], ALU.mult).then_inc(yb_ready, 1)
                for j, buf in enumerate((gk, gq[:, 0], gq[:, 1])):
                    hold(freesem(("rotD", j)), bank_count(("rotD", j), lay, 2, 0)[1])
                    did(tt(buf, buf, cos_d[:], ALU.mult))
                    wait()
                    tt(buf, buf, tmp_d[:, j], ALU.add).then_inc(rope_d_ready, 1)
                r = slice(NOPE, QK)
                hold(rope_d_ready, at(lay, 3, 3))
                hold(fullsem(("rotK",)), bank_count(("rotK",), lay, 1, 0)[1])
                tt(Kh[r, 0, :], Kh[r, 0, :], cos_a[r, :], ALU.mult).then_inc(cos_a_done, 1)
                hold(fullsem(("rotQ",)), bank_count(("rotQ",), lay, 1, 0)[1])
                for h in range(0, MLA_H, 2):
                    tt(Qh[r, h:h + 2, :], Qh[r, h:h + 2, :], cos_a[r, :].unsqueeze(1).broadcast_to([ROPE, 2, S]),
                       ALU.mult).then_inc(cos_a_done, 1)
                hold(rope_k_ready, at(lay, 1, 1))
                for h in range(1, MLA_H):
                    ins = nc.gpsimd.tensor_copy(Kh[r, h, :], Kh[r, 0, :])
                ins.then_inc(keys_ready, 1)

                hold(keys_ready, at(lay, 1, 1))
                hold(yc_ready, at(lay, 2, 2))
                for k in MIX_ORDER[0:4]:
                    nc.gpsimd.tensor_copy(mix_hi[:, k], mix[:, k]).then_inc(split_hi, 1)
                for n in range(4):
                    j = MIX_ORDER[2 * n] // 2
                    hold(wout_hi_ready, at(lay, 4, n + 1))
                    tt(wout_low[j], ring[:, (WOUT_AT + j) % RING], wout_hi[j].bitcast(F32), ALU.subtract)\
                        .then_inc(wout_lo_ready, 1)
                    if n < 2:
                        hold(split_hi, at(lay, 4, 4))
                        for k in MIX_ORDER[2 * n:2 * n + 2]:
                            tt(mix_lo[:, k], mix[:, k], mix_hi[:, k].bitcast(F32), ALU.subtract)\
                                .then_inc(split_ready, 1)
                for t in range(NT):
                    inverse_deviation(lay, t, 0)

                hold(route_ready, at(lay, 1, 1))
                hold(x1_stored, at(lay, 16 * NT, 16 * NT))

                def gather(b, pair, count):
                    nc.gpsimd.tensor_copy(cur[:, b:b + 1], slot_i[:, bass.ds(pair, 1)]).then_inc(cur_ready, 1)
                    hold(cur_ready, count)
                    nc.gpsimd.indirect_dma_start(xs[:, b, :], None, x1_rows,
                                                 bass.IndirectOffsetOnAxis(ap=cur[:, b:b + 1], axis=0))\
                        .then_inc(xs_full[b], 16)

                for b in range(BODY_PAIRS):
                    gather(b, b, at(lay, PAIRS, b + 1))
                with g.Fori(1, PAIRS // BODY_PAIRS) as body:
                    for b in range(BODY_PAIRS):
                        bank, nth = USES[("xsT", 1)]
                        hold(bank_full[bank], lay * PER_LAYER[bank] + body * (BODY_PAIRS * PER_PAIR[bank])
                             + ((b - BODY_PAIRS) * PER_PAIR[bank] + nth + 1))
                        gather(b, body * BODY_PAIRS + b, lay * PAIRS + body * BODY_PAIRS + (b + 1))

                g.wait_ge(ln2_in, at(lay, 16, 16))
                g.sem_inc(passed["pool"], 1)
                inverse_deviation(lay, 0, 1)
                mean_part(lay, 0)
                hold(centred, at(lay, 2, 1))
                tt(X[:, 0], X[:, 0], ln2_gb[:, 0:D], ALU.mult).then_inc(gained, 1)
                inverse_deviation(lay, 1, 1)
                mean_part(lay, 1)
                inverse_deviation(lay, 2, 1)
                hold(gained, at(lay, 2, 1))
                tt(X[:, 0], X[:, 0], ln2_gb[:, D:2 * D], ALU.add).then_inc(biased, 1)
                hold(centred, at(lay, 2, 2))
                tt(X[:, 1], X[:, 1], ln2_gb[:, 0:D], ALU.mult).then_inc(gained, 1)
                inverse_deviation(lay, 3, 1)
                hold(biased, at(lay, 1, 2))
                for place, t in enumerate(TILE_ORDER):
                    if place > 0:
                        hold(x_ready, at(lay, 6, 6 + 2 * place))
                    g.dma_start(out[t * P:(t + 1) * P], X[:, t]).then_inc(x_stored, 16)


def constants():
    c = np.zeros((P, N_CONST), np.float32)
    c[:, IDENT:IDENT + P] = np.eye(P, dtype=np.float32)
    c[:, ONES:ONES + P] = 1.0
    for at, block in ((ROT_A, ROPE), (ROT_D, GQ_D)):
        half = block // 2
        for m in range(P):
            first = m % block < half
            c[m + half if first else m - half, at + m] = -1.0 if first else 1.0
    i, j = np.arange(P)[:, None], np.arange(3 * P)[None, :]
    c[:, BAND:BAND + 3 * P] = np.where(np.abs(i - (j - P)) <= 128, 0.0, -1.0e30)
    inv = 1.0 / (np.float32(10000.0) ** (np.arange(0, GQ_D, 2, dtype=np.float32) / np.float32(GQ_D)))
    c[:, FREQ] = inv.astype(np.float32)[np.arange(P) % (GQ_D // 2)]
    iota = np.ascontiguousarray(np.broadcast_to(np.arange(S, dtype=np.int16), (P, S)))
    return c, iota


def lay_out(a):
    sizes = (256, 128, 32, 256, 256, 256, 256, 256, 256, 128, 128)
    ends = np.cumsum(sizes)
    q_lat, kv, k_rope, sc_b, sc_c, sc_h, cf_a, cf_g, gq_q, gq_k, gq_v = (
        np.arange(e - n, e) for e, n in zip(ends, sizes))
    gq_q = gq_q.reshape(GQ_H, GQ_D)[[0, 2, 1, 3]].ravel()
    order = np.concatenate([cf_g, cf_a, sc_c, sc_h, sc_b, kv, gq_k, q_lat, gq_q, gq_v])
    w_in = np.zeros((DEPTH, D, IN_SLOTS * 256), np.float32)
    w_in[:, :, :len(order)] = a["w_in"][:, :, order]
    w_in[:, :, len(order) + NOPE:len(order) + QK] = a["w_in"][:, :, k_rope]
    w_in = w_in.reshape(DEPTH, KD, P, IN_SLOTS, 256).transpose(0, 3, 2, 1, 4).reshape(DEPTH, IN_SLOTS, P, SLOT)
    ukv = a["w_ukv"].reshape(DEPTH, KV_RANK, MLA_H, 2, 64).transpose(0, 1, 3, 2, 4).reshape(DEPTH, KV_RANK, -1)

    def on_partitions(v):
        n = v.shape[-1] // P
        return v.reshape(DEPTH, -1, n, P).transpose(0, 3, 2, 1).reshape(DEPTH, P, -1)

    def every(v):
        return np.broadcast_to(v[:, None, :], (DEPTH, P, v.shape[-1]))

    par = np.concatenate([on_partitions(a[k]) for k in (
        "sconv_w", "cconv_w", "cconv_b", "cnorm_g", "cnorm_b", "q_norm_g", "kv_norm_g")]
        + [every(a["sink"]), every(a["b_router"])], axis=2)
    c, iota = constants()
    return {
        "x_in": a["x"].reshape(S, D), "positions": a["positions"].reshape(S), "w_in": w_in, "w_uq": a["w_uq"],
        "w_ukv": ukv, "w_router": a["w_router"], "params": par, "w_out": a["w_out"],
        "ln1": np.concatenate([a["ln1_g"], a["ln1_b"]], axis=1), "ln2": np.concatenate([a["ln2_g"], a["ln2_b"]], axis=1),
        "w_gate": a["w_gate"], "w_up": a["w_up"], "w_down": a["w_down"], "consts": c, "iota": iota,
    }


def kernel(**inputs):
    import concourse.bacc as bacc
    from concourse.bass_utils import run_bass_kernel_spmd

    nc = bacc.Bacc("TRN2", target_bir_lowering=False, num_devices=1)
    arrays = {k: np.ascontiguousarray(v) for k, v in lay_out({k: np.asarray(v) for k, v in inputs.items()}).items()}
    aps = {k: nc.dram_tensor(k, v.shape, mybir.dt.from_np(v.dtype), kind="ExternalInput").ap()
           for k, v in arrays.items()}
    out = nc.dram_tensor("out", (S, D), F32, kind="ExternalOutput").ap()
    trunk(nc, **aps, out=out)
    r = run_bass_kernel_spmd(nc, [arrays], core_ids=[0])
    return r.results[0]["out"].reshape(1, S, D)
```
